# Optimizing a Trainium2 kernel written in Bass

```python
import math
import jax, jax.numpy as jnp
from jax import lax
import numpy as np

D_MODEL = 1024
BATCH = 1
SEQ = 1024
DEPTH = 2
DEC_BATCH = 1
DEC_SEQ = 256
PAST_LEN = 128

N_EVEN = (DEPTH + 1) // 2
N_ODD = DEPTH // 2
D_FF = 4 * D_MODEL
EPS = 1e-6

GDN_HEADS = 4
GDN_DK = 128
GDN_DV = 128
GDN_CONV = 5
GDN_CHUNK = 64
GDN_W = GDN_HEADS * GDN_DV
GDN_COLS = 4 * GDN_W + 4 * GDN_HEADS

RWKV_HEADS = 8
RWKV_N = 64
RWKV_W = RWKV_HEADS * RWKV_N
RWKV_DECAY_LORA = 64
RWKV_AAA_LORA = 64
RWKV_GATE_LORA = 128
RWKV_LN_EPS = 64e-5
RWKV_COLS = 3 * RWKV_W + 2 * RWKV_DECAY_LORA + 2 * RWKV_AAA_LORA + RWKV_GATE_LORA

P_EVEN = GDN_COLS + RWKV_COLS

MLA_HEADS = 8
MLA_Q_LORA = 256
MLA_KV_LORA = 128
MLA_NOPE = 128
MLA_ROPE = 64
MLA_V = 128
ROPE_BASE = 10000.0
Q_BLOCK = 128
P_ODD = MLA_Q_LORA + MLA_KV_LORA + MLA_ROPE

kernel_name = 'hybrid_gdn_rwkv7_mla_encoder'

def rms_norm(x, g, eps=EPS):
    xf = x.astype(jnp.float32)
    y = xf * lax.rsqrt(jnp.mean(xf * xf, -1, keepdims=True) + eps)
    return (y * g.astype(jnp.float32)).astype(x.dtype)

def l2_normalize(x, eps=1e-6):
    xf = x.astype(jnp.float32)
    return xf * lax.rsqrt(jnp.sum(xf * xf, -1, keepdims=True) + eps)

def centred_dwconv(x, w):
    pad = w.shape[0] // 2
    return lax.conv_general_dilated(x, w[:, None, :].astype(x.dtype), window_strides=(1,),
                                    padding=[(pad, pad)], dimension_numbers=('NWC', 'WIO', 'NWC'),
                                    feature_group_count=x.shape[-1])

def centred_token_shift(x, mu):
    x_prev = jnp.pad(x, ((0, 0), (1, 0), (0, 0)))[:, :-1]
    x_next = jnp.pad(x, ((0, 0), (0, 1), (0, 0)))[:, 1:]
    return x + mu[0] * (x_prev - x) + mu[1] * (x_next - x)

def gated_delta_chunked(q, k, v, g, beta):
    B, T, H, DK = k.shape
    DV = v.shape[-1]
    C = GDN_CHUNK
    NC = T // C

    def chunks(a):
        a = jnp.moveaxis(a, 2, 1)
        return a.reshape(a.shape[:2] + (NC, C) + a.shape[3:])

    q = chunks(q) * (DK ** -0.5)
    k, v, g, beta = chunks(k), chunks(v), chunks(g), chunks(beta)
    g = jnp.cumsum(g, axis=-1)
    lower = jnp.tril(jnp.ones((C, C), bool))
    strict = jnp.tril(jnp.ones((C, C), bool), -1)
    decay = jnp.exp(jnp.where(lower, g[..., :, None] - g[..., None, :], -jnp.inf))
    k_beta = k * beta[..., None]
    v_beta = v * beta[..., None]
    L = jnp.where(strict, jnp.einsum('bhnik,bhnjk->bhnij', k_beta, k) * decay, 0.0)
    eye = jnp.eye(C, dtype=jnp.float32)
    rhs = jnp.concatenate([v_beta, k_beta * jnp.exp(g)[..., None]], -1)
    sol = lax.linalg.triangular_solve(eye + L, rhs, left_side=True, lower=True)
    u, w = sol[..., :DV], sol[..., DV:]
    qk = jnp.einsum('bhnik,bhnjk->bhnij', q, k) * decay
    q_dec = q * jnp.exp(g)[..., None]
    g_last = g[..., -1]
    k_dec = k * jnp.exp(g_last[..., None] - g)[..., None]
    xs = tuple(jnp.moveaxis(a, 2, 0) for a in (qk, q_dec, k_dec, u, w, g_last))

    def step(S, inp):
        qk_c, qd_c, kd_c, u_c, w_c, gl_c = inp
        v_new = u_c - jnp.einsum('bhck,bhkv->bhcv', w_c, S)
        o = jnp.einsum('bhck,bhkv->bhcv', qd_c, S) + jnp.einsum('bhij,bhjv->bhiv', qk_c, v_new)
        S = S * jnp.exp(gl_c)[..., None, None] + jnp.einsum('bhck,bhcv->bhkv', kd_c, v_new)
        return S, o

    _, o = lax.scan(step, jnp.zeros((B, H, DK, DV), jnp.float32), xs)
    o = jnp.moveaxis(o, 0, 2).reshape(B, H, T, DV)
    return jnp.moveaxis(o, 1, 2)

def gdn_mixer(cols, conv_w, A_log, dt_bias, o_norm):
    B, T, _ = cols.shape
    H, W = GDN_HEADS, GDN_W
    f32 = jnp.float32
    qkv = jax.nn.silu(centred_dwconv(cols[..., :3 * W], conv_w))
    z = cols[..., 3 * W:4 * W].astype(f32).reshape(B, T, H, GDN_DV)
    a_in = cols[..., 4 * W:4 * W + 2 * H].astype(f32).reshape(B, T, 2, H)
    b_in = cols[..., 4 * W + 2 * H:].astype(f32).reshape(B, T, 2, H)
    q = l2_normalize(qkv[..., :W].reshape(B, T, H, GDN_DK))
    k = l2_normalize(qkv[..., W:2 * W].reshape(B, T, H, GDN_DK))
    v = qkv[..., 2 * W:].astype(f32).reshape(B, T, H, GDN_DV)
    g = -jnp.exp(A_log.astype(f32)) * jax.nn.softplus(a_in + dt_bias.astype(f32))
    beta = jax.nn.sigmoid(b_in)
    rev = lambda a: jnp.flip(a, 1)
    o_fwd = gated_delta_chunked(q, k, v, g[:, :, 0], beta[:, :, 0])
    o_bwd = rev(gated_delta_chunked(rev(q), rev(k), rev(v), rev(g[:, :, 1]), rev(beta[:, :, 1])))
    o = rms_norm(o_fwd + o_bwd, o_norm) * jax.nn.silu(z)
    return o.reshape(B, T, W).astype(cols.dtype)

def rwkv7_scan(r, w, k, v, a_vec, b_vec, reverse):
    B, T, H, N = r.shape
    xs = tuple(jnp.moveaxis(t, 1, 0) for t in (r, w, k, v, a_vec, b_vec))

    def step(S, inp):
        r_t, w_t, k_t, v_t, a_t, b_t = inp
        Sa = jnp.einsum('bhvk,bhk->bhv', S, a_t)
        S = S * w_t[:, :, None, :] + Sa[..., None] * b_t[:, :, None, :] + v_t[..., None] * k_t[:, :, None, :]
        return S, jnp.einsum('bhvk,bhk->bhv', S, r_t)

    _, o = lax.scan(step, jnp.zeros((B, H, N, N), jnp.float32), xs, reverse=reverse)
    return jnp.moveaxis(o, 0, 1)

def rwkv7_mixer(cols, mu, w0, w2, a0, a2, g2, k_k, k_a, r_k, ln_g, ln_b):
    B, T, _ = cols.shape
    H, N, W = RWKV_HEADS, RWKV_N, RWKV_W
    DL, AL = RWKV_DECAY_LORA, RWKV_AAA_LORA
    f32 = jnp.float32
    xs = centred_token_shift(cols.astype(f32), mu.astype(f32))
    r, k, v = xs[..., :W], xs[..., W:2 * W], xs[..., 2 * W:3 * W]
    o = 3 * W
    w_lo = xs[..., o:o + 2 * DL].reshape(B, T, 2, DL)
    o += 2 * DL
    a_lo = xs[..., o:o + 2 * AL].reshape(B, T, 2, AL)
    o += 2 * AL
    g_lo = xs[..., o:]
    log_w = -jax.nn.softplus(-(w0.astype(f32) + jnp.einsum('btdl,dlc->btdc', jnp.tanh(w_lo), w2.astype(f32)))) - 0.5
    decay = jnp.exp(-jnp.exp(log_w))
    a = jax.nn.sigmoid(a0.astype(f32) + jnp.einsum('btdl,dlc->btdc', a_lo, a2.astype(f32)))
    gate = jnp.einsum('btl,lc->btc', jax.nn.sigmoid(g_lo), g2.astype(f32))
    heads = lambda t: t.reshape(B, T, H, N)
    kk = l2_normalize(heads(k * k_k.astype(f32))).reshape(B, T, W)
    k_dir = k[:, :, None] * (1.0 + (a - 1.0) * k_a.astype(f32))
    o_fwd = rwkv7_scan(heads(r), heads(decay[:, :, 0]), heads(k_dir[:, :, 0]), heads(v),
                       heads(-kk), heads(kk * a[:, :, 0]), False)
    o_bwd = rwkv7_scan(heads(r), heads(decay[:, :, 1]), heads(k_dir[:, :, 1]), heads(v),
                       heads(-kk), heads(kk * a[:, :, 1]), True)
    y = o_fwd + o_bwd
    mean = jnp.mean(y, -1, keepdims=True)
    var = jnp.mean(jnp.square(y - mean), -1, keepdims=True)
    y = ((y - mean) * lax.rsqrt(var + RWKV_LN_EPS)).reshape(B, T, W) * ln_g.astype(f32) + ln_b.astype(f32)
    bonus = jnp.sum(heads(r) * heads(k_dir.sum(2)) * r_k.astype(f32), -1, keepdims=True) * heads(v)
    y = y + bonus.reshape(B, T, W)
    return (y * gate).astype(cols.dtype)

def rope_tables(T):
    inv = 1.0 / (ROPE_BASE ** (jnp.arange(0, MLA_ROPE, 2, dtype=jnp.float32) / MLA_ROPE))
    ang = jnp.arange(T, dtype=jnp.float32)[:, None] * inv[None, :]
    return jnp.cos(ang), jnp.sin(ang)

def apply_rope(x, cos, sin):
    half = x.shape[-1] // 2
    x1, x2 = x[..., :half].astype(jnp.float32), x[..., half:].astype(jnp.float32)
    return jnp.concatenate([x1 * cos - x2 * sin, x2 * cos + x1 * sin], -1).astype(x.dtype)

def mla_mixer(cols, q_norm, w_q_b, kv_norm, w_kv_b):
    B, T, _ = cols.shape
    H = MLA_HEADS
    q_lat = rms_norm(cols[..., :MLA_Q_LORA], q_norm)
    kv_lat = rms_norm(cols[..., MLA_Q_LORA:MLA_Q_LORA + MLA_KV_LORA], kv_norm)
    k_rope = cols[..., MLA_Q_LORA + MLA_KV_LORA:]
    q = (q_lat @ w_q_b).reshape(B, T, H, MLA_NOPE + MLA_ROPE)
    kv = (kv_lat @ w_kv_b).reshape(B, T, H, MLA_NOPE + MLA_V)
    q_nope, q_rope = q[..., :MLA_NOPE], q[..., MLA_NOPE:]
    k_nope, v = kv[..., :MLA_NOPE], kv[..., MLA_NOPE:]
    cos, sin = rope_tables(T)
    q_rope = apply_rope(q_rope, cos[:, None, :], sin[:, None, :])
    k_rope = apply_rope(k_rope, cos, sin)
    scale = (MLA_NOPE + MLA_ROPE) ** -0.5
    nqb = T // Q_BLOCK
    qn_blocks = q_nope.reshape(B, nqb, Q_BLOCK, H, MLA_NOPE).transpose(1, 0, 2, 3, 4)
    qr_blocks = q_rope.reshape(B, nqb, Q_BLOCK, H, MLA_ROPE).transpose(1, 0, 2, 3, 4)

    def attend(blk):
        qn, qr = blk
        s = (jnp.einsum('bqhd,bkhd->bhqk', qn, k_nope) + jnp.einsum('bqhr,bkr->bhqk', qr, k_rope))
        p = jax.nn.softmax(s.astype(jnp.float32) * scale, axis=-1).astype(v.dtype)
        return jnp.einsum('bhqk,bkhd->bqhd', p, v)

    o = lax.map(attend, (qn_blocks, qr_blocks))
    return o.transpose(1, 0, 2, 3, 4).reshape(B, T, H * MLA_V)

def encoder_trunk(x, p):
    for layer in range(DEPTH):
        i = layer // 2
        h = rms_norm(x, p['norm_mix_pre'][layer])
        if layer % 2 == 0:
            cols = h @ p['w_in_even'][i]
            a_out = gdn_mixer(cols[..., :GDN_COLS], p['gdn_conv'][i], p['gdn_A_log'][i],
                              p['gdn_dt_bias'][i], p['gdn_o_norm'][i])
            b_out = rwkv7_mixer(cols[..., GDN_COLS:], p['rwkv_mu'][i], p['rwkv_w0'][i], p['rwkv_w2'][i],
                                p['rwkv_a0'][i], p['rwkv_a2'][i], p['rwkv_g2'][i], p['rwkv_k_k'][i],
                                p['rwkv_k_a'][i], p['rwkv_r_k'][i], p['rwkv_ln_g'][i], p['rwkv_ln_b'][i])
            mix = jnp.concatenate([a_out, b_out], -1) @ p['w_out_even'][i]
        else:
            cols = h @ p['w_in_odd'][i]
            mix = mla_mixer(cols, p['mla_q_norm'][i], p['mla_w_q_b'][i], p['mla_kv_norm'][i],
                            p['mla_w_kv_b'][i]) @ p['w_out_odd'][i]
        x = x + rms_norm(mix, p['norm_mix_post'][layer])
        h = rms_norm(x, p['norm_ffn_pre'][layer])
        f = jnp.square(jax.nn.relu(h @ p['w_ff1'][layer])) @ p['w_ff2'][layer]
        x = x + rms_norm(f, p['norm_ffn_post'][layer])
    return x

def setup_inputs(seed: int = 0) -> dict:
    key = jax.random.key(seed)
    ks = iter(jax.random.split(key, 40))
    nrm = lambda shape, scale: jax.random.normal(next(ks), shape, jnp.float32) * scale
    gain = lambda shape: 1.0 + nrm(shape, 0.1)
    NE, NO = N_EVEN, N_ODD
    dt = jnp.exp(jax.random.uniform(next(ks), (NE, 2, GDN_HEADS), jnp.float32, math.log(1e-3), math.log(1e-1)))
    return {
        'x_prompt': nrm((BATCH, SEQ, D_MODEL), 1.0),
        'x_sample': nrm((DEC_BATCH, DEC_SEQ, D_MODEL), 1.0),
        'norm_mix_pre': gain((DEPTH, D_MODEL)),
        'norm_mix_post': gain((DEPTH, D_MODEL)),
        'norm_ffn_pre': gain((DEPTH, D_MODEL)),
        'norm_ffn_post': gain((DEPTH, D_MODEL)),
        'w_ff1': nrm((DEPTH, D_MODEL, D_FF), D_MODEL ** -0.5),
        'w_ff2': nrm((DEPTH, D_FF, D_MODEL), D_FF ** -0.5),
        'w_in_even': nrm((NE, D_MODEL, P_EVEN), D_MODEL ** -0.5),
        'w_out_even': nrm((NE, GDN_W + RWKV_W, D_MODEL), (GDN_W + RWKV_W) ** -0.5),
        'gdn_conv': nrm((NE, GDN_CONV, 3 * GDN_W), GDN_CONV ** -0.5),
        'gdn_A_log': jnp.log(jax.random.uniform(next(ks), (NE, 2, GDN_HEADS), jnp.float32, 1.0, 16.0)),
        'gdn_dt_bias': dt + jnp.log(-jnp.expm1(-dt)),
        'gdn_o_norm': gain((NE, GDN_DV)),
        'rwkv_mu': jax.random.uniform(next(ks), (NE, 2, RWKV_COLS), jnp.float32, 0.0, 0.5),
        'rwkv_w0': nrm((NE, 2, RWKV_W), 0.5),
        'rwkv_w2': nrm((NE, 2, RWKV_DECAY_LORA, RWKV_W), RWKV_DECAY_LORA ** -0.5),
        'rwkv_a0': nrm((NE, 2, RWKV_W), 0.5),
        'rwkv_a2': nrm((NE, 2, RWKV_AAA_LORA, RWKV_W), RWKV_AAA_LORA ** -0.5),
        'rwkv_g2': nrm((NE, RWKV_GATE_LORA, RWKV_W), RWKV_GATE_LORA ** -0.5),
        'rwkv_k_k': 0.85 + nrm((NE, RWKV_W), 0.1),
        'rwkv_k_a': 1.0 + nrm((NE, RWKV_W), 0.1),
        'rwkv_r_k': nrm((NE, RWKV_HEADS, RWKV_N), 0.1),
        'rwkv_ln_g': gain((NE, RWKV_W)),
        'rwkv_ln_b': nrm((NE, RWKV_W), 0.1),
        'w_in_odd': nrm((NO, D_MODEL, P_ODD), D_MODEL ** -0.5),
        'mla_q_norm': gain((NO, MLA_Q_LORA)),
        'mla_w_q_b': nrm((NO, MLA_Q_LORA, MLA_HEADS * (MLA_NOPE + MLA_ROPE)), MLA_Q_LORA ** -0.5),
        'mla_kv_norm': gain((NO, MLA_KV_LORA)),
        'mla_w_kv_b': nrm((NO, MLA_KV_LORA, MLA_HEADS * (MLA_NOPE + MLA_V)), MLA_KV_LORA ** -0.5),
        'w_out_odd': nrm((NO, MLA_HEADS * MLA_V, D_MODEL), (MLA_HEADS * MLA_V) ** -0.5),
    }

def reference(x_prompt, x_sample, norm_mix_pre, norm_mix_post, norm_ffn_pre, norm_ffn_post,
              w_ff1, w_ff2, w_in_even, w_out_even, gdn_conv, gdn_A_log, gdn_dt_bias, gdn_o_norm,
              rwkv_mu, rwkv_w0, rwkv_w2, rwkv_a0, rwkv_a2, rwkv_g2, rwkv_k_k, rwkv_k_a, rwkv_r_k,
              rwkv_ln_g, rwkv_ln_b, w_in_odd, mla_q_norm, mla_w_q_b, mla_kv_norm, mla_w_kv_b, w_out_odd):
    params = dict(norm_mix_pre=norm_mix_pre, norm_mix_post=norm_mix_post, norm_ffn_pre=norm_ffn_pre,
                  norm_ffn_post=norm_ffn_post, w_ff1=w_ff1, w_ff2=w_ff2, w_in_even=w_in_even,
                  w_out_even=w_out_even, gdn_conv=gdn_conv, gdn_A_log=gdn_A_log, gdn_dt_bias=gdn_dt_bias,
                  gdn_o_norm=gdn_o_norm, rwkv_mu=rwkv_mu, rwkv_w0=rwkv_w0, rwkv_w2=rwkv_w2, rwkv_a0=rwkv_a0,
                  rwkv_a2=rwkv_a2, rwkv_g2=rwkv_g2, rwkv_k_k=rwkv_k_k, rwkv_k_a=rwkv_k_a, rwkv_r_k=rwkv_r_k,
                  rwkv_ln_g=rwkv_ln_g, rwkv_ln_b=rwkv_ln_b, w_in_odd=w_in_odd, mla_q_norm=mla_q_norm,
                  mla_w_q_b=mla_w_q_b, mla_kv_norm=mla_kv_norm, mla_w_kv_b=mla_w_kv_b, w_out_odd=w_out_odd)
    y_prompt = encoder_trunk(x_prompt, params)
    y_sample = encoder_trunk(x_sample, params)
    return (y_prompt, y_sample)


_drawn_inputs = setup_inputs


def setup_inputs(seed=0):
    import zlib

    import numpy as np

    out = dict(_drawn_inputs(seed))
    spreads = {}
    factors = {'rwkv_k_k': 3.157, 'mla_q_norm': 3.308}
    for name, (base, spread) in spreads.items():
        noise = np.random.default_rng([zlib.crc32(name.encode()), seed]).standard_normal(out[name].shape)
        drawn = base * np.exp(spread * noise) if base else spread * noise
        out[name] = __import__('jax').numpy.asarray(drawn.astype(out[name].dtype))
    for name, factor in factors.items():
        out[name] = (out[name] * factor).astype(out[name].dtype)
    return out
```

```python
import math
from contextlib import ExitStack

import numpy as np
import concourse.bass as bass
from concourse import mybir

F32 = mybir.dt.float32
ACT = mybir.ActivationFunctionType
ALU = mybir.AluOpType
AX = mybir.AxisListType

P = 128
D = 1024
KB = D // P
T_PROMPT, T_SAMPLE = 1024, 256
NT = T_PROMPT + T_SAMPLE
TILES = NT // P
TILES_P = T_PROMPT // P
D_FF = 4 * D
EPS = 1e-6
GH, GD = 4, 128
GW = GH * GD
RH, RN = 8, 64
RW = RH * RN
RB = RW // P
LN_EPS = 64e-5
GDN_COLS = 4 * GW + 4 * GH
CONV_BLOCKS = 3 * GW // P
RWKV_BLOCKS = 15
TAPS = 5
PAD = 2
PADDED = PAD + T_PROMPT + PAD + T_SAMPLE + PAD
SPAN = T_PROMPT + PAD + T_SAMPLE
PIECES = ((0, 512), (512, 512), (1024, 256))
LEVELS = 7
MH, NOPE, ROPE, MV = 8, 128, 64, 128
Q_LORA, KV_LORA = 256, 128


def bc(ap, n):
    return ap.unsqueeze(2).broadcast_to([ap.shape[0], ap.shape[1], n])


def bcm(ap, m):
    return ap.unsqueeze(1).broadcast_to([ap.shape[0], m, ap.shape[1]])


class Chain:

    def __init__(self, eng, sem, i=None, per=0):
        self.eng, self.sem, self.i, self.per, self.n = eng, sem, i, per, 0

    def __call__(self, ins):
        self.n += 1
        ins.then_inc(self.sem, 1)
        self.eng.wait_ge(self.sem, self.n if self.i is None else self.i * self.per + self.n)

    def done(self):
        assert self.i is None or self.n == self.per, (self.sem, self.n, self.per)


class Env:

    def __init__(self, nc, stack, tag):
        self.nc, self.stack, self.tag, self.made = nc, stack, tag, []

    def sb(self, name, shape):
        return self.stack.enter_context(self.nc.sbuf_tensor(f"{self.tag}_{name}", shape, F32))

    def banks(self, n):
        return [self.stack.enter_context(self.nc.psum_tensor(f"{self.tag}_bank{i}", [P, 512], F32)) for i in range(n)]

    def sem(self, name):
        sem = self.sems.enter_context(self.nc.semaphore(f"{self.tag}_{name}"))
        self.made.append(sem)
        return sem


def token_tile(x_prompt, x_sample):
    return (x_prompt[0].rearrange("(t p) d -> p t d", p=P), x_sample[0].rearrange("(t p) d -> p t d", p=P))


def load_x(nc, E, X, x_prompt, x_sample):
    loaded = E.sem("x_loaded")
    xp, xs = token_tile(x_prompt, x_sample)
    with nc.Block() as block:
        @block.sync
        def _(sp):
            sp.dma_start(X[:, 0:TILES_P, :], xp).then_inc(loaded, 16)
            sp.dma_start(X[:, TILES_P:TILES, :], xs).then_inc(loaded, 16)
            sp.wait_ge(loaded, 32)


def residual_norm(nc, E, X, hT, ident, mix, g_post, g_pre, outs=None):
    gpost = E.sb("gpost", [P, D])
    gpre = E.sb("gpre", [P, KB])
    eps = E.sb("eps", [P, 1])
    junk = [E.sb(f"junk{j}", [P, D]) for j in range(2)]
    h = [E.sb(f"h{j}", [P, D]) for j in range(2)]
    sq1, rt1, rc1, sq2, rt2, rc2 = (E.sb(n, [P, 2]) for n in ("sq1", "rt1", "rc1", "sq2", "rt2", "rc2"))
    ps = [E.stack.enter_context(nc.psum_tensor(f"{E.tag}_ps{j}", [P, KB, P], F32)) for j in range(2)]
    gains, eps_set, mix_root, x_updated, x_root, h_ready, turned, ht_done, act_chain, dve_chain, stored = (
        E.sem(n) for n in ("gains", "eps_set", "mix_root", "x_updated", "x_root", "h_ready", "turned", "ht_done",
                           "act_chain", "dve_chain", "stored"))
    n_gains = 16 * ((mix is not None) + (g_pre is not None))
    with nc.Block() as block:
        @block.sync
        def _(sp):
            if mix is not None:
                sp.dma_start(gpost[:, :], g_post.partition_broadcast(P)).then_inc(gains, 16)
            if g_pre is not None:
                sp.dma_start(gpre[:, :], g_pre.rearrange("(k p) -> p k", p=P),
                             allow_slow_non_contiguous=True).then_inc(gains, 16)
            if outs is not None:
                yp, ys = token_tile(*outs)
                with sp.Fori(0, TILES_P) as t:
                    sp.wait_ge(x_updated, t + 1)
                    sp.dma_start(yp[:, bass.ds(t, 1), :], X[:, bass.ds(t, 1), :]).then_inc(stored, 16)
                with sp.Fori(0, TILES - TILES_P) as t:
                    sp.wait_ge(x_updated, t + TILES_P + 1)
                    sp.dma_start(ys[:, bass.ds(t, 1), :], X[:, bass.ds(t + TILES_P, 1), :]).then_inc(stored, 16)
                sp.wait_ge(stored, 16 * TILES)

        @block.scalar
        def _(act):
            act.wait_ge(eps_set, 1)
            with act.Fori(0, TILES // 2) as i:
                link = Chain(act, act_chain, i, 2 * (mix is not None) + 2 * (g_pre is not None))
                if mix is not None:
                    for j in range(2):
                        link(act.activation(junk[j][:, :].unsqueeze(1), mix[:, bass.ds(2 * i + j, 1), :], ACT.Square,
                                            accum_out=sq1[:, j:j + 1]))
                    for j in range(2):
                        act.activation(rt1[:, j:j + 1], sq1[:, j:j + 1], ACT.Sqrt, bias=eps[:, :],
                                       scale=1.0 / D).then_inc(mix_root, 1)
                if g_pre is not None:
                    for j in range(2):
                        if mix is not None:
                            act.wait_ge(x_updated, 2 * i + j + 1)
                        link(act.activation(junk[j][:, :].unsqueeze(1), X[:, bass.ds(2 * i + j, 1), :], ACT.Square,
                                            accum_out=sq2[:, j:j + 1]))
                    for j in range(2):
                        act.activation(rt2[:, j:j + 1], sq2[:, j:j + 1], ACT.Sqrt, bias=eps[:, :],
                                       scale=1.0 / D).then_inc(x_root, 1)
                if mix is None:
                    act.wait_ge(h_ready, 2 * i + 2)
                if g_pre is None:
                    act.wait_ge(x_updated, 2 * i + 2)
                link.done()

        @block.vector
        def _(dve):
            dve.memset(eps[:, :], EPS).then_inc(eps_set, 1)
            dve.wait_ge(gains, n_gains)
            with dve.Fori(0, TILES // 2) as i:
                link = Chain(dve, dve_chain, i, 4 * (mix is not None) + 2 * (g_pre is not None))
                if mix is not None:
                    for j in range(2):
                        dve.wait_ge(mix_root, 2 * i + j + 1)
                        link(dve.reciprocal(rc1[:, j:j + 1], rt1[:, j:j + 1]))
                        m = mix[:, bass.ds(2 * i + j, 1), :]
                        x = X[:, bass.ds(2 * i + j, 1), :]
                        link(dve.scalar_tensor_tensor(m, m, rc1[:, j:j + 1], gpost[:, :].unsqueeze(1),
                                                      ALU.mult, ALU.mult))
                        dve.tensor_tensor(x, x, m, ALU.add).then_inc(x_updated, 1)
                if g_pre is not None:
                    for j in range(2):
                        dve.wait_ge(x_root, 2 * i + j + 1)
                        link(dve.reciprocal(rc2[:, j:j + 1], rt2[:, j:j + 1]))
                        dve.tensor_scalar(h[j][:, :].unsqueeze(1), X[:, bass.ds(2 * i + j, 1), :], rc2[:, j:j + 1],
                                          None, ALU.mult).then_inc(h_ready, 1)
                    for j in range(2):
                        dve.wait_ge(turned, 2 * i + j + 1)
                        dve.tensor_tensor(hT[:, :, bass.ds((2 * i + j) * P, P)], ps[j][:, :, :], bc(gpre[:, :], P),
                                          ALU.mult).then_inc(ht_done, 1)
                    dve.wait_ge(ht_done, 2 * i + 2)
                link.done()

        @block.tensor
        def _(pe):
            if g_pre is not None:
                with pe.Fori(0, TILES // 2) as i:
                    for j in range(2):
                        pe.wait_ge(h_ready, 2 * i + j + 1)
                        for k in range(KB):
                            last = pe.transpose(ps[j][:, k, :], h[j][:, k * P:(k + 1) * P], ident[:, :])
                        last.then_inc(turned, 1)


def in_proj_fm(nc, E, hT, w_in, first_col, turns, dst, weights, conv):
    n_taps = TAPS if conv else 3
    reach = n_taps // 2
    n_in = TAPS if conv else 2
    w = [E.sb(f"w{j}", [P, KB, P]) for j in range(3)]
    padded = [E.sb(f"padded{j}", [P, PADDED]) for j in range(3)]
    mixed = [E.sb(f"mixed{j}", [P, SPAN]) for j in range(3)]
    bank = E.banks(8)
    BANK = (0, 1, 2, 3, 4, 5, 6, 7, 2)
    w_loaded = [E.sem(f"w_loaded{j}") for j in range(3)]
    stored = [E.sem(f"stored{j}") for j in range(3)]
    product, copied, taps_done, silu_done, dve_chain, zeroed, taps_loaded, setup_chain = (
        E.sem(n) for n in ("product", "copied", "taps_done", "silu_done", "dve_chain", "zeroed", "taps_loaded",
                           "setup_chain"))
    tap = E.sb("tap", [P, 3 * turns, n_taps])
    raw_tap = E.sb("raw_tap", [P, 3 * turns, 2])
    wv = w_in.rearrange("(k p) n -> p k n", p=P)
    CREDIT = 3

    with nc.Block() as block:
        @block.sync
        def _(sp):
            for u in range(n_in):
                sp.dma_start((tap if conv else raw_tap)[:, :, u], weights[u].rearrange("(b p) -> p b", p=P),
                             allow_slow_non_contiguous=True).then_inc(taps_loaded, 16)
            for j in range(3):
                sp.dma_start(w[j][:, :, :], wv[:, :, first_col + j * P:first_col + (j + 1) * P]).then_inc(w_loaded[j], 16)

            def store(i, j):
                sp.wait_ge(silu_done if conv else taps_done, 3 * i + j + 1 + (0 if conv else CREDIT))
                blk = dst[bass.ds(i * 3 + j, 1)].rearrange("b p n -> p b n")
                sp.dma_start(blk[:, :, 0:T_PROMPT], mixed[j][:, 0:T_PROMPT].unsqueeze(1)).then_inc(stored[j], 16)
                sp.dma_start(blk[:, :, T_PROMPT:NT], mixed[j][:, T_PROMPT + PAD:SPAN].unsqueeze(1)).then_inc(stored[j], 16)

            with sp.Fori(0, turns - 1) as i:
                for j in range(3):
                    sp.wait_ge(product, 9 * i + 3 * j + 3)
                    sp.dma_start(w[j][:, :, :], wv[:, :, bass.ds(i * (3 * P) + (first_col + (3 + j) * P), P)]
                                 ).then_inc(w_loaded[j], 16)
                for j in range(3):
                    store(i, j)
            for j in range(3):
                store(turns - 1, j)
            for j in range(3):
                sp.wait_ge(stored[j], 32 * (turns + 1))

        @block.tensor
        def _(pe):
            with pe.Fori(0, turns) as i:
                for j in range(3):
                    pe.wait_ge(w_loaded[j], 16 * i + 16)
                    for q, (t0, n) in enumerate(PIECES):
                        pe.wait_ge(copied, 9 * i + 3 * j + q + 1)
                        for k in range(KB):
                            last = pe.matmul(bank[BANK[3 * j + q]][:, 0:n], w[j][:, k, :], hT[:, k, t0:t0 + n],
                                             start=(k == 0), stop=(k == KB - 1))
                        last.then_inc(product, 1)

        def silu(act, i, j):
            act.wait_ge(taps_done, 3 * i + j + 1 + CREDIT)
            act.activation(mixed[j][:, :], mixed[j][:, :], ACT.Silu).then_inc(silu_done, 1)

        @block.scalar
        def _(act):
            act.wait_ge(zeroed, 3)
            act.sem_inc(copied, CREDIT)
            with act.Fori(0, turns) as i:
                for j in range(3):
                    act.wait_ge(taps_done, 3 * i + j + 1)
                    for q, (t0, n) in enumerate(PIECES):
                        act.wait_ge(product, 9 * i + 3 * j + q + 1)
                        at = PAD + t0 if q < 2 else PAD + t0 + PAD
                        act.activation(padded[j][:, at:at + n], bank[BANK[3 * j + q]][:, 0:n], ACT.Copy).then_inc(copied, 1)
                    if conv and j > 0:
                        silu(act, i, j - 1)
                if conv:
                    silu(act, i, 2)

        @block.vector
        def _(dve):
            dve.sem_inc(taps_done, CREDIT)
            for j in range(3):
                dve.memset(padded[j][:, :], 0.0).then_inc(zeroed, 1)
                dve.sem_inc(stored[j], 32)
            dve.wait_ge(zeroed, 3)
            dve.wait_ge(taps_loaded, 16 * n_in)
            if not conv:
                link = Chain(dve, setup_chain)
                link(dve.tensor_tensor(tap[:, :, 1], raw_tap[:, :, 0], raw_tap[:, :, 1], ALU.add))
                link(dve.tensor_scalar(tap[:, :, 1], tap[:, :, 1], -1.0, 1.0, ALU.mult, ALU.add))
                link(dve.tensor_copy(tap[:, :, 0], raw_tap[:, :, 0]))
                link(dve.tensor_copy(tap[:, :, 2], raw_tap[:, :, 1]))
            with dve.Fori(0, turns) as i:
                link = Chain(dve, dve_chain, i, 3 * (n_taps - 1))
                for j in range(3):
                    dve.wait_ge(copied, 9 * i + 3 * j + 3 + CREDIT)
                    dve.wait_ge(stored[j], 32 * i + 32)
                    b = i * 3 + j
                    out = mixed[j][:, :].unsqueeze(1)
                    for u in range(n_taps):
                        src = padded[j][:, PAD - reach + u:PAD - reach + u + SPAN].unsqueeze(1)
                        c = tap[:, bass.ds(b, 1), u]
                        if u == 0:
                            link(dve.tensor_scalar(out, src, c, None, ALU.mult))
                        elif u < n_taps - 1:
                            link(dve.scalar_tensor_tensor(out, src, c, out, ALU.mult, ALU.add))
                        else:
                            dve.scalar_tensor_tensor(out, src, c, out, ALU.mult, ALU.add).then_inc(taps_done, 1)
                link.done()


def in_proj_tm(nc, E, hT, w_in, gates, z_dst):
    n_ab = 4 * GH
    w = E.sb("w", [P, KB, GW + n_ab])
    z = [E.sb(f"z{j}", [P, GW]) for j in range(2)]
    bank = E.banks(8)
    w_loaded, product, silu_done, ab_done = (E.sem(n) for n in ("w_loaded", "product", "silu_done", "ab_done"))
    stored = [E.sem(f"stored{j}") for j in range(2)]
    with nc.Block() as block:
        @block.sync
        def _(sp):
            sp.dma_start(w[:, :, :], w_in.rearrange("(k p) n -> p k n", p=P)[:, :, 3 * GW:GDN_COLS]).then_inc(w_loaded, 16)
            for t in range(TILES):
                sp.wait_ge(silu_done, t + 1)
                sp.dma_start(z_dst[t], z[t % 2][:, :]).then_inc(stored[t % 2], 16)
            for j in range(2):
                sp.wait_ge(stored[j], 16 * (TILES // 2))

        @block.tensor
        def _(pe):
            pe.wait_ge(w_loaded, 16)
            for t in range(TILES):
                if t >= 4:
                    pe.wait_ge(silu_done, t - 3)
                    pe.wait_ge(ab_done, t - 3)
                for half, (c0, n) in enumerate(((0, GW), (GW, n_ab))):
                    for k in range(KB):
                        last = pe.matmul(bank[2 * (t % 4) + half][:, 0:n], hT[:, k, t * P:(t + 1) * P],
                                         w[:, k, c0:c0 + n], start=(k == 0), stop=(k == KB - 1))
                last.then_inc(product, 1)

        @block.scalar
        def _(act):
            for t in range(TILES):
                act.wait_ge(product, t + 1)
                if t >= 2:
                    act.wait_ge(stored[t % 2], 16 * (t // 2))
                act.activation(z[t % 2][:, :], bank[2 * (t % 4)][:, :], ACT.Silu).then_inc(silu_done, 1)

        @block.vector
        def _(dve):
            for t in range(TILES):
                dve.wait_ge(product, t + 1)
                dve.tensor_copy(gates[:, t, :], bank[2 * (t % 4) + 1][:, 0:n_ab]).then_inc(ab_done, 1)
            dve.wait_ge(ab_done, TILES)


def feed_forward(nc, E, hT, acc, w1, w2):
    GB = 4
    GROUPS = D_FF // (GB * P)
    w1_sb = E.sb("w1", [P, KB, GB * P])
    w2_sb = E.sb("w2", [P, GB, D])
    f = E.sb("f", [P, GB, NT])
    bank = E.banks(8)
    w1_loaded, w2_loaded, up_product, relu_done, squared, down_product, added, zeroed = (
        E.sem(n) for n in ("w1_loaded", "w2_loaded", "up_product", "relu_done", "squared", "down_product", "added",
                           "zeroed"))
    w1v = w1.rearrange("(k p) n -> p k n", p=P)
    w2v = w2.rearrange("(b p) n -> p b n", p=P)
    UP = GB * len(PIECES)
    DOWN = TILES * 2
    with nc.Block() as block:
        @block.sync
        def _(sp):
            sp.dma_start(w1_sb[:, :, :], w1v[:, :, 0:GB * P]).then_inc(w1_loaded, 16)
            sp.dma_start(w2_sb[:, :, :], w2v[:, 0:GB, :]).then_inc(w2_loaded, 16)
            with sp.Fori(0, GROUPS - 1) as i:
                sp.wait_ge(up_product, UP * i + UP)
                sp.dma_start(w1_sb[:, :, :], w1v[:, :, bass.ds((i + 1) * (GB * P), GB * P)]).then_inc(w1_loaded, 16)
                sp.wait_ge(down_product, DOWN * i + DOWN)
                sp.dma_start(w2_sb[:, :, :], w2v[:, bass.ds((i + 1) * GB, GB), :]).then_inc(w2_loaded, 16)

        @block.tensor
        def _(pe):
            with pe.Fori(0, GROUPS) as i:
                pe.wait_ge(w1_loaded, 16 * i + 16)
                for b in range(GB):
                    for q, (t0, n) in enumerate(PIECES):
                        u = len(PIECES) * b + q
                        pe.wait_ge(relu_done, UP * i + u + 1)
                        for k in range(KB):
                            last = pe.matmul(bank[u % 4][:, 0:n], w1_sb[:, k, b * P:(b + 1) * P], hT[:, k, t0:t0 + n],
                                             start=(k == 0), stop=(k == KB - 1))
                        last.then_inc(up_product, 1)
                pe.wait_ge(w2_loaded, 16 * i + 16)
                for t in range(TILES):
                    for half in range(2):
                        u = 2 * t + half
                        if u == 0:
                            pe.wait_ge(squared, UP * i + UP)
                        pe.wait_ge(added, DOWN * i + u + 1)
                        for b in range(GB):
                            last = pe.matmul(bank[4 + u % 4][:, :], f[:, b, t * P:(t + 1) * P],
                                             w2_sb[:, b, half * 512:(half + 1) * 512], start=(b == 0), stop=(b == GB - 1))
                        last.then_inc(down_product, 1)

        @block.scalar
        def _(act):
            act.sem_inc(relu_done, 4)
            with act.Fori(0, GROUPS) as i:
                for b in range(GB):
                    for q, (t0, n) in enumerate(PIECES):
                        u = len(PIECES) * b + q
                        act.wait_ge(up_product, UP * i + u + 1)
                        act.activation(f[:, b, t0:t0 + n], bank[u % 4][:, 0:n], ACT.Relu).then_inc(relu_done, 1)

        @block.vector
        def _(dve):
            dve.memset(acc[:, :, :], 0.0).then_inc(zeroed, 1)
            dve.wait_ge(zeroed, 1)
            dve.sem_inc(added, 4)
            with dve.Fori(0, GROUPS) as i:
                for b in range(GB):
                    for q, (t0, n) in enumerate(PIECES):
                        u = len(PIECES) * b + q
                        dve.wait_ge(relu_done, UP * i + u + 1 + 4)
                        dve.tensor_tensor(f[:, b, t0:t0 + n], f[:, b, t0:t0 + n], f[:, b, t0:t0 + n],
                                          ALU.mult).then_inc(squared, 1)
                for u in range(DOWN):
                    dve.wait_ge(down_product, DOWN * i + u + 1)
                    a = acc[:, u // 2, (u % 2) * 512:(u % 2 + 1) * 512]
                    dve.tensor_tensor(a, a, bank[4 + u % 4][:, :], ALU.add).then_inc(added, 1)
                dve.wait_ge(added, DOWN * i + DOWN + 4)


def gdn_rates(nc, E, ins, gates, rates, eps):
    incl = [E.sb(f"incl{d}", [P, P]) for d in range(2)]
    excl = [E.sb(f"excl{d}", [P, P]) for d in range(2)]
    ones = E.sb("ones", [P, P])
    a_log, dt = E.sb("a_log", [P, 2 * GH]), E.sb("dt", [P, 2 * GH])
    a, b, c = (E.sb(n, [P, TILES, 2 * GH]) for n in ("a", "b", "c"))
    bank = E.banks(8)
    loaded, dve_chain, act_chain, to_act, to_dve, summed = (
        E.sem(n) for n in ("loaded", "dve_chain", "act_chain", "to_act", "to_dve", "summed"))
    n_th = TILES * GH
    with nc.Block() as block:
        @block.sync
        def _(sp):
            for d in range(2):
                sp.dma_start(incl[d][:, :], ins["c_incl"][d]).then_inc(loaded, 16)
                sp.dma_start(excl[d][:, :], ins["c_excl"][d]).then_inc(loaded, 16)
            sp.dma_start(ones[:, :], ins["c_ones"]).then_inc(loaded, 16)
            sp.dma_start(a_log[:, :], ins["gdn_A_log"].rearrange("n d h -> (n d h)").partition_broadcast(P)).then_inc(loaded, 16)
            sp.dma_start(dt[:, :], ins["gdn_dt_bias"].rearrange("n d h -> (n d h)").partition_broadcast(P)).then_inc(loaded, 16)

        @block.vector
        def _(dve):
            link = Chain(dve, dve_chain)
            dve.wait_ge(loaded, 16 * 7)
            link(dve.tensor_tensor(c[:, :, :], gates[:, :, 0:2 * GH], bcm(dt[:, :], TILES), ALU.add))
            link(dve.tensor_scalar(a[:, :, :], c[:, :, :], 0.0, None, ALU.max))
            link(dve.tensor_scalar(b[:, :, :], c[:, :, :], 0.0, None, ALU.min))
            dve.tensor_tensor(b[:, :, :], b[:, :, :], a[:, :, :], ALU.subtract).then_inc(to_act, 1)
            dve.wait_ge(to_dve, 1)
            link(dve.tensor_tensor(a[:, :, :], a[:, :, :], b[:, :, :], ALU.add))
            link(dve.scalar_tensor_tensor(a[:, :, :], a[:, :, :], -1.0, bcm(a_log[:, :], TILES), ALU.mult, ALU.mult))
            for d in range(2):
                dve.tensor_copy(rates["g"][d][:, :, :], a[:, :, d * GH:(d + 1) * GH]).then_inc(to_act, 1)
            dve.wait_ge(to_dve, 2)
            link(dve.reciprocal(c[:, :, :], c[:, :, :]))
            for d in range(2):
                link(dve.tensor_copy(rates["beta"][d][:, :, :], c[:, :, d * GH:(d + 1) * GH]))
                link(dve.tensor_scalar(rates["neg_beta"][d][:, :, :], c[:, :, d * GH:(d + 1) * GH], -1.0, None, ALU.mult))
            for d in range(2):
                dve.wait_ge(summed, 3 * d + 3)
                link(dve.tensor_copy(rates["G"][d][:, :, :], bank[3 * d][:, 0:n_th].rearrange("p (t h) -> p t h", h=GH)))

        @block.scalar
        def _(act):
            link = Chain(act, act_chain)
            act.wait_ge(loaded, 16 * 7)
            link(act.activation(a_log[:, :], a_log[:, :], ACT.Exp))
            act.wait_ge(to_act, 1)
            link(act.activation(b[:, :, :], b[:, :, :], ACT.Exp))
            act.activation(b[:, :, :], b[:, :, :], ACT.Ln, bias=ones[:, 0:1]).then_inc(to_dve, 1)
            act.wait_ge(to_act, 3)
            link(act.activation(c[:, :, :], gates[:, :, 2 * GH:4 * GH], ACT.Exp, scale=-1.0))
            act.activation(c[:, :, :], c[:, :, :], ACT.Identity, bias=ones[:, 0:1]).then_inc(to_dve, 1)
            for d in range(2):
                act.wait_ge(summed, 3 * d + 3)
                act.wait_ge(dve_chain, 11 + d)
                for u, name in enumerate(("exp_G", "exp_rest", "exp_last")):
                    link(act.activation(rates[name][d][:, :, :],
                                        bank[3 * d + u][:, 0:n_th].rearrange("p (t h) -> p t h", h=GH), ACT.Exp))

        @block.tensor
        def _(pe):
            for d in range(2):
                pe.wait_ge(to_act, 2 + d)
                g = rates["g"][d][:, :, :].rearrange("p t h -> p (t h)")
                for u, sums in enumerate((incl[d], excl[1 - d], ones)):
                    pe.matmul(bank[3 * d + u][:, 0:n_th], sums[:, :], g, start=True, stop=True).then_inc(summed, 1)


def prepare_tokens(nc, E, ins, ident, eps, conv_fm, shift_fm, fm_both, fm_dir, tm_both, tm_dir):
    qkv = E.sb("qkv", [P, CONV_BLOCKS, P])
    rk = E.sb("rk", [P, RWKV_BLOCKS, P])
    squares = E.sb("squares", [P, 3 * GH, P])
    root = E.sb("root", [P, 3, GW])
    fb = E.sb("fb", [P, 3, GH, P])
    fd = [E.sb(f"fd{d}", [P, 2, RB, P]) for d in range(2)]
    tb = E.sb("tb", [P, 5, GW])
    td = [E.sb(f"td{d}", [P, RW]) for d in range(2)]
    a = [E.sb(f"a{d}", [P, RB, P]) for d in range(2)]
    mixk = [E.sb(f"mixk{d}", [P, RB, P]) for d in range(2)]
    kkr = E.sb("kkr", [P, RB, P])
    rksum = E.sb("rksum", [P, RB, P])
    th, sg = E.sb("th", [P, P]), E.sb("sg", [P, P])
    bsum = E.sb("bsum", [P, RH])
    ones, head_ones, head_cols = E.sb("ones", [P, P]), E.sb("head_ones", [P, P]), E.sb("head_cols", [P, 2])
    w2, a2, g2 = (E.sb(n, [P, RW]) for n in ("w2", "a2", "g2"))
    w0 = E.sb("w0", [1, 2 * RW])
    a0 = [E.sb(f"a0_{d}", [P, RB]) for d in range(2)]
    k_k, k_a, r_k, one_ka = (E.sb(n, [P, RB]) for n in ("k_k", "k_a", "r_k", "one_ka"))
    bank = E.banks(8)
    names = ("params", "loaded", "turned", "kk_raw", "squared", "sums", "rooted", "low_in", "a_product", "a_biased",
             "a_done", "k_normal", "bonus_in", "gate_product", "w_product", "w_done", "bonus_product", "k_turned",
             "dve_chain", "act_chain", "pool_chain", "setup_chain", "dve_out", "stored", "all_done", "act_out")
    s = {n: E.sem(n) for n in names}
    fb_names = []
    PARAMS = 14

    def fm_vec(v):
        return v.rearrange("(b p) -> p b", p=P)

    with nc.Block() as block:
        @block.sync
        def _(sp):
            for dst, src in ((ones, ins["c_ones"]), (head_ones, ins["c_head_ones"]), (head_cols, ins["c_head_cols"]),
                             (w2, ins["rwkv_w2"][0].rearrange("d l c -> (d l) c")),
                             (a2, ins["rwkv_a2"][0].rearrange("d l c -> (d l) c")), (g2, ins["rwkv_g2"][0]),
                             (w0, ins["rwkv_w0"].rearrange("n d c -> n (d c)"))):
                sp.dma_start(dst[:, :], src).then_inc(s["params"], 16)
            for dst, src in ((a0[0], ins["rwkv_a0"][0][0]), (a0[1], ins["rwkv_a0"][0][1]), (k_k, ins["rwkv_k_k"][0]),
                             (k_a, ins["rwkv_k_a"][0]), (r_k, ins["rwkv_r_k"][0].rearrange("h n -> (h n)"))):
                sp.dma_start(dst[:, :], fm_vec(src), allow_slow_non_contiguous=True).then_inc(s["params"], 16)

            def load(t):
                sp.dma_start(qkv[:, :, :], conv_fm.rearrange("b p n -> p b n")[:, :, bass.ds(t * P, P)]).then_inc(s["loaded"], 16)
                sp.dma_start(rk[:, :, :], shift_fm.rearrange("b p n -> p b n")[:, :, bass.ds(t * P, P)]).then_inc(s["loaded"], 16)

            def store(t):
                sp.wait_ge(s["dve_out"], t + 1)
                sp.wait_ge(s["act_out"], t + 1)
                sp.dma_start(fm_both[bass.ds(t, 1)].rearrange("o p n -> p o n"),
                             fb[:, :, :, :].rearrange("p a b n -> p (a b n)").unsqueeze(1)).then_inc(s["stored"], 16)
                sp.dma_start(tm_both[bass.ds(t, 1)].rearrange("o p n -> p o n"),
                             tb[:, :, :].rearrange("p a n -> p (a n)").unsqueeze(1)).then_inc(s["stored"], 16)
                for d in range(2):
                    sp.dma_start(fm_dir[d][bass.ds(t, 1)].rearrange("o p n -> p o n"),
                                 fd[d][:, :, :, :].rearrange("p a b n -> p (a b n)").unsqueeze(1)).then_inc(s["stored"], 16)
                    sp.dma_start(tm_dir[d][bass.ds(t, 1)].rearrange("o p n -> p o n"),
                                 td[d][:, :].unsqueeze(1)).then_inc(s["stored"], 16)

            load(0)
            with sp.Fori(0, TILES - 1) as t:
                store(t)
                load(t + 1)
                sp.wait_ge(s["stored"], 96 * t + 96)
                sp.sem_inc(s["all_done"], 1)
            store(TILES - 1)
            sp.wait_ge(s["stored"], 96 * TILES)

        @block.tensor
        def _(pe):
            pe.wait_ge(s["params"], 16 * 12)
            with pe.Fori(0, TILES) as t:
                pe.wait_ge(s["loaded"], 32 * t + 32)
                for k in range(GH):
                    pe.transpose(bank[0][:, k * P:(k + 1) * P], qkv[:, 2 * GH + k, :], ident[:, :])
                for k in range(RB):
                    last = pe.transpose(bank[1][:, k * P:(k + 1) * P], rk[:, 2 * RB + k, :], ident[:, :])
                last.then_inc(s["turned"], 1)
                for d in range(2):
                    for k in range(RB):
                        last = pe.matmul(bank[5 + d][:, k * P:(k + 1) * P], a2[64 * d:64 * d + 64, k * P:(k + 1) * P],
                                         rk[64 * d:64 * d + 64, 13, :], start=True, stop=True)
                last.then_inc(s["a_product"], 1)
                pe.wait_ge(s["squared"], t + 1)
                for u in range(2):
                    pe.matmul(bank[2 + u][:, :], ones[:, :], squares[:, u * GH:(u + 1) * GH, :], start=True, stop=True)
                pe.matmul(bank[4][:, :], head_ones[:, :], squares[:, 2 * GH:3 * GH, :], start=True,
                          stop=True).then_inc(s["sums"], 1)
                pe.wait_ge(s["low_in"], t + 1)
                pe.matmul(bank[7][:, :], sg[:, :], g2[:, :], start=True, stop=True).then_inc(s["gate_product"], 1)
                pe.wait_ge(s["k_normal"], t + 1)
                for d in range(2):
                    pe.matmul(bank[d][:, :], th[64 * d:64 * d + 64, :], w2[64 * d:64 * d + 64, :], start=True, stop=False)
                    last = pe.matmul(bank[d][:, :], ones[0:1, :], w0[0:1, d * RW:(d + 1) * RW], start=False, stop=True)
                last.then_inc(s["w_product"], 1)
                for k in range(GH):
                    last = pe.transpose(bank[2][:, k * P:(k + 1) * P], fb[:, 0, k, :], ident[:, :])
                last.then_inc(s["k_turned"], 1)
                pe.wait_ge(s["bonus_in"], t + 1)
                for k in range(RB):
                    last = pe.matmul(bank[3][:, 2 * k:2 * k + 2], rksum[:, k, :], head_cols[:, :], start=True, stop=True)
                last.then_inc(s["bonus_product"], 1)

        @block.scalar
        def _(act):
            act.wait_ge(s["setup_chain"], 3)
            with act.Fori(0, TILES) as t:
                link = Chain(act, s["act_chain"], t, 4)
                act.wait_ge(s["loaded"], 32 * t + 32)
                act.wait_ge(s["all_done"], t + 1)
                link(act.activation(squares[:, 0:2 * GH, :], qkv[:, 0:2 * GH, :], ACT.Square))
                act.wait_ge(s["kk_raw"], t + 1)
                act.activation(squares[:, 2 * GH:3 * GH, :], kkr[:, :, :], ACT.Square).then_inc(s["squared"], 1)
                link(act.activation(th[:, :], rk[:, 12, :], ACT.Tanh))
                act.activation(sg[:, :], rk[:, 14, :], ACT.Sigmoid).then_inc(s["low_in"], 1)
                for d in range(2):
                    act.wait_ge(s["a_biased"], 2 * t + d + 1)
                    act.activation(a[d][:, :, :], a[d][:, :, :], ACT.Sigmoid).then_inc(s["a_done"], 1)
                act.wait_ge(s["gate_product"], t + 1)
                link(act.activation(tb[:, 3, :], bank[7][:, :], ACT.Copy))
                act.wait_ge(s["sums"], t + 1)
                for u in range(3):
                    act.activation(root[:, u, :], bank[2 + u][:, :], ACT.Sqrt, bias=eps[:, :]).then_inc(s["rooted"], 1)
                act.wait_ge(s["w_product"], t + 1)
                for d in range(2):
                    act.activation(td[d][:, :], bank[d][:, :], ACT.Sigmoid).then_inc(s["w_done"], 1)
                act.wait_ge(s["k_turned"], t + 1)
                link(act.activation(tb[:, 0, :], bank[2][:, :], ACT.Copy))
                act.wait_ge(s["w_done"], 2 * t + 2)
                act.sem_inc(s["act_out"], 1)
                link.done()

        @block.vector
        def _(dve):
            dve.memset(eps[:, :], EPS).then_inc(s["setup_chain"], 1)
            dve.wait_ge(s["params"], 16 * 12)
            dve.tensor_scalar(one_ka[:, :], k_a[:, :], -1.0, 1.0, ALU.mult, ALU.add).then_inc(s["setup_chain"], 1)
            dve.wait_ge(s["setup_chain"], 2)
            dve.sem_inc(s["setup_chain"], 1)
            dve.sem_inc(s["all_done"], 1)
            r, k, v = rk[:, 0:RB, :], rk[:, RB:2 * RB, :], None
            with dve.Fori(0, TILES) as t:
                link = Chain(dve, s["dve_chain"], t, 18)
                dve.wait_ge(s["loaded"], 32 * t + 32)
                dve.wait_ge(s["all_done"], t + 1)
                dve.tensor_tensor(kkr[:, :, :], k, bc(k_k[:, :], P), ALU.mult).then_inc(s["kk_raw"], 1)
                dve.wait_ge(s["turned"], t + 1)
                link(dve.tensor_copy(tb[:, 1, :], bank[0][:, :]))
                link(dve.tensor_copy(tb[:, 2, :], bank[1][:, :]))
                for d in range(2):
                    dve.wait_ge(s["a_product"], t + 1)
                    dve.tensor_tensor(a[d][:, :, :], bank[5 + d][:, :].rearrange("p (b n) -> p b n", b=RB),
                                      bc(a0[d][:, :], P), ALU.add).then_inc(s["a_biased"], 1)
                dve.wait_ge(s["rooted"], 3 * t + 3)
                link(dve.reciprocal(root[:, :, :], root[:, :, :]))
                rt = [root[:, u, :].rearrange("p (b n) -> p b n", b=RB) for u in range(3)]
                link(dve.scalar_tensor_tensor(fb[:, 1, :, :], qkv[:, 0:GH, :], GD ** -0.5, rt[0], ALU.mult, ALU.mult))
                dve.tensor_tensor(fb[:, 0, :, :], qkv[:, GH:2 * GH, :], rt[1], ALU.mult).then_inc(s["k_normal"], 1)
                link(dve.tensor_tensor(fb[:, 2, :, :], kkr[:, :, :], rt[2], ALU.mult))
                for d in range(2):
                    dve.wait_ge(s["a_done"], 2 * t + d + 1)
                    m = mixk[d][:, :, :]
                    link(dve.tensor_tensor(m, a[d][:, :, :], bc(k_a[:, :], P), ALU.mult))
                    link(dve.tensor_tensor(m, m, bc(one_ka[:, :], P), ALU.add))
                    link(dve.tensor_tensor(fd[d][:, 1, :, :], k, m, ALU.mult))
                    link(dve.tensor_tensor(fd[d][:, 0, :, :], fb[:, 2, :, :], a[d][:, :, :], ALU.mult))
                link(dve.tensor_tensor(rksum[:, :, :], fd[0][:, 1, :, :], fd[1][:, 1, :, :], ALU.add))
                link(dve.tensor_tensor(rksum[:, :, :], rksum[:, :, :], r, ALU.mult))
                dve.tensor_tensor(rksum[:, :, :], rksum[:, :, :], bc(r_k[:, :], P), ALU.mult).then_inc(s["bonus_in"], 1)
                dve.wait_ge(s["bonus_product"], t + 1)
                link(dve.tensor_copy(bsum[:, :], bank[3][:, 0:RH]))
                link(dve.tensor_tensor(tb[:, 4, :].rearrange("p (h n) -> p h n", h=RH),
                                       tb[:, 2, :].rearrange("p (h n) -> p h n", h=RH), bc(bsum[:, :], RN), ALU.mult))
                link(dve.tensor_copy(bsum[:, 0:1], bsum[:, 0:1]))
                dve.wait_ge(s["kk_raw"], t + 1)
                dve.sem_inc(s["dve_out"], 1)
                link.done()


def mix_scopes(nc, phase, dram, ins, acc, gates, ident, conv_fm, shift_fm, z_tm, stop):
    fm_both = dram("fm_both", [TILES, P, 3 * GW])
    fm_dir = [dram(f"fm_dir{d}", [TILES, P, 2 * RW]) for d in range(2)]
    tm_both = dram("tm_both", [TILES, P, 5 * GW])
    tm_dir = [dram(f"tm_dir{d}", [TILES, P, RW]) for d in range(2)]
    with ExitStack() as own:
        def sb(name, shape):
            return own.enter_context(nc.sbuf_tensor(name, shape, F32))
        eps = sb("eps", [P, 1])
        rates = {n: [sb(f"rate_{n}{d}", [P, TILES, GH]) for d in range(2)]
                 for n in ("g", "beta", "neg_beta", "G", "exp_G", "exp_rest", "exp_last")}
        phase("prepare", prepare_tokens, ins, ident, eps, conv_fm, shift_fm, fm_both, fm_dir, tm_both, tm_dir)
        phase("rates", gdn_rates, ins, gates, rates, eps)
        if stop > 2:
            phase("scan", recurrences, ins, ident, rates, shift_fm, fm_both, fm_dir, tm_both, tm_dir, acc)
        if stop > 3:
            phase("gate", gate_outputs, ins, acc, z_tm, tm_both)
            if stop > 4:
                phase("out0", project_out, ident, acc, ins["w_out_even"][0])


def recurrences(nc, E, ins, ident, rates, shift_fm, fm_both, fm_dir, tm_both, tm_dir, out):
    G, GR = 6, 4
    direction = [0, 1, 0, 0, 1, 1]
    width = [P, P, RN, RN, RN, RN]
    NT_ = [E.sb(f"NT{g}", [P, GR, P]) for g in range(G)]
    X = [E.sb(f"X{g}", [P, GR, P]) for g in range(G)]
    XT = [E.sb(f"XT{g}", [P, GR, P]) for g in range(G)]
    NM = [E.sb(f"NM{g}", [P, GR, P]) for g in range(2)]
    Y = [E.sb(f"Y{g}", [P, GR, P]) for g in range(2)]
    A_o = [E.sb(f"A_o{g}", [P, GR, P]) for g in range(G)]
    A_v = [None, None] + [E.sb(f"A_v{g}", [P, GR, P]) for g in range(2, G)]
    A_ov = [None, None] + [E.sb(f"A_ov{g}", [P, GR, P]) for g in range(2, G)]
    fb = [E.sb(f"fb{d}", [P, 3, GH, P]) for d in range(2)]
    rr = [E.sb(f"r{d}", [P, RB, P]) for d in range(2)]
    fd = [E.sb(f"fd{d}", [P, 2, RB, P]) for d in range(2)]
    tb = [E.sb(f"tb{d}", [P, 3, GW]) for d in range(2)]
    td = [E.sb(f"td{d}", [P, RW]) for d in range(2)]
    AR = [E.sb(f"AR{d}", [P, RB, 2, P]) for d in range(2)]
    BK = [E.sb(f"BK{d}", [P, 2, RW]) for d in range(2)]
    ends = [E.sb(f"ends{d}", [P, RB, 2]) for d in range(2)]
    S_g = [E.sb(f"S_g{d}", [P, GH, P]) for d in range(2)]
    S_r = [E.sb(f"S_r{d}", [P, RB, 2, RN]) for d in range(2)]
    rest = [E.sb(f"rest{d}", [P, RB, 2]) for d in range(2)]
    head_cols = E.sb("head_cols", [P, 2])
    e_inc, e_exc, e_neg = (E.sb(n, [P, RB, P]) for n in ("e_inc", "e_exc", "e_neg"))
    grow, decay = E.sb("grow", [P, GH, P]), E.sb("decay", [P, GH, P])
    BT, KT = Y, NM
    KD = [e_inc, e_exc]
    R = [NT_[g][:, :, 0:width[g]] for g in range(G)]
    U = [X[g][:, :, 0:width[g]] for g in range(G)]
    incl = [E.sb(f"incl{d}", [P, P]) for d in range(2)]
    excl = [E.sb(f"excl{d}", [P, P]) for d in range(2)]
    outside = [E.sb(f"outside{d}", [P, P]) for d in range(2)]
    sums = [E.sb(f"sums{d}", [P, 2 * P]) for d in range(2)]
    end_sums = [E.sb(f"end_sums{d}", [P, 2]) for d in range(2)]
    keep = [E.sb(f"keep{d}", [P, TILES]) for d in range(2)]
    levels = [E.sb(f"levels{d}", [P, LEVELS, P]) for d in range(2)]
    ones = E.sb("ones", [P, P])
    ps = E.stack.enter_context(nc.psum_tensor(f"{E.tag}_ps", [P, 8, 512], F32))
    ML = LEVELS - 1
    YC, XC = 2, 6
    PER_DVE = 53

    names = ("consts", "cleared", "g_rows", "g_sums", "g_shift", "g_decay", "gram", "gram_used", "w_sums", "w_exp",
             "w_used", "turned", "turned_out", "pairs", "pairs_used", "x_first", "masked", "x_turned", "x_out",
             "y_product", "y_out", "z_product", "x_done", "state_scaled", "right", "right_g", "right_r", "solved",
             "u_g", "u_r", "outs", "outs_used", "g_state", "turn_done", "kdec", "dve_chain", "pool_chain", "act_chain",
             "pool_tick")
    s = {n: E.sem(n) for n in names}
    early = [E.sem(f"early{d}") for d in range(2)]
    late = [E.sem(f"late{d}") for d in range(2)]

    def head_of(half, slot):
        return 4 * half + 2 * (slot % 2) + slot // 2

    def tile(d, i):
        return i if d == 0 else i * -1 + (TILES - 1)

    def heads(ap, n=P):
        return ap.rearrange("p (h n) -> p h n", n=n)

    def pairs_view(b):
        return ps[:, b:b + 2, :].rearrange("p b (h a n) -> p (b h) a n", h=2, a=2)

    def pair_slots(g, pair):
        return ps[:, g, 0:4 * RN].rearrange("p (a b n) -> p b a n", a=2, n=RN)[:, pair, :, :]

    def rate(name, d, t):
        return bc(rates[name][d][:, bass.ds(t, 1), :].rearrange("p o h -> p (o h)"), P)

    with nc.Block() as block:
        @block.sync
        def _(sp):
            for dst, name in ((incl, "c_incl"), (excl, "c_excl"), (outside, "c_outside"), (sums, "c_decay_sums"),
                              (end_sums, "c_decay_ends"), (keep, "c_keep")):
                for d in range(2):
                    sp.dma_start(dst[d][:, :], ins[name][d]).then_inc(s["consts"], 16)
            for d in range(2):
                sp.dma_start(levels[d][:, :, :], ins["c_levels"][d].rearrange("m s t -> s m t")).then_inc(s["consts"], 16)
            sp.dma_start(ones[:, :], ins["c_ones"]).then_inc(s["consts"], 16)
            sp.dma_start(head_cols[:, :], ins["c_head_cols"]).then_inc(s["consts"], 16)

            def load_early(d, i):
                t = tile(d, i)
                sp.dma_start(rr[d][:, :, :], shift_fm.rearrange("b p n -> p b n")[:, 0:RB, bass.ds(t * P, P)]).then_inc(early[d], 16)
                sp.dma_start(fd[d][:, :, :, :].rearrange("p a b n -> p (a b n)").unsqueeze(1),
                             fm_dir[d][bass.ds(t, 1)].rearrange("o p n -> p o n")).then_inc(early[d], 16)
                sp.dma_start(td[d][:, :].unsqueeze(1), tm_dir[d][bass.ds(t, 1)].rearrange("o p n -> p o n")).then_inc(early[d], 16)

            def load_late(d, i):
                t = tile(d, i)
                sp.dma_start(fb[d][:, :, :, :].rearrange("p a b n -> p (a b n)").unsqueeze(1),
                             fm_both[bass.ds(t, 1)].rearrange("o p n -> p o n")).then_inc(late[d], 16)
                sp.dma_start(tb[d][:, :, :].rearrange("p a n -> p (a n)").unsqueeze(1),
                             tm_both[bass.ds(t, 1)].rearrange("o p n -> p o n")[:, :, 0:3 * GW]).then_inc(late[d], 16)

            for d in range(2):
                load_late(d, 0)
                load_early(d, 0)
            with sp.Fori(0, TILES - 1) as i:
                for d in range(2):
                    sp.wait_ge(s["w_used"], 2 * i + d + 1)
                    load_early(d, i + 1)
                sp.wait_ge(s["kdec"], 2 * i + 2)
                sp.wait_ge(s["outs"], G * i + G)
                for d in range(2):
                    load_late(d, i + 1)

        @block.tensor
        def _(pe):
            pe.wait_ge(s["consts"], 16 * 16)
            with pe.Fori(0, TILES) as i:
                pe.wait_ge(s["turn_done"], i + 1)
                for d in range(2):
                    pe.wait_ge(s["g_rows"], 2 * i + d + 1)
                    if d == 1:
                        pe.wait_ge(s["g_shift"], 2 * i + 1)
                    pe.matmul(ps[:, 0, :], ones[:, :], grow[:, :, :], start=True, stop=True).then_inc(s["g_sums"], 1)
                    pe.wait_ge(late[d], 32 * i + 32)
                    for h in range(GH):
                        last = pe.matmul(ps[:, 1 + 2 * d + h // 2, (h % 2) * 256:(h % 2) * 256 + 256], fb[d][:, 0, h, :],
                                         fb[d][:, 0:2, h, :], start=True, stop=True)
                    last.then_inc(s["gram"], 1)
                for d in range(2):
                    pe.wait_ge(early[d], 48 * i + 48)
                    if d == 1:
                        pe.wait_ge(s["w_exp"], 2 * i + 1)
                    for k in range(RB):
                        pe.matmul(ps[:, 5 + k // 2, (k % 2) * 256:(k % 2) * 256 + 256], td[d][:, k * P:(k + 1) * P],
                                  sums[d][:, :], start=True, stop=True)
                    for k in range(RB):
                        last = pe.matmul(ps[:, 7, 2 * k:2 * k + 2], td[d][:, k * P:(k + 1) * P], end_sums[d][:, :],
                                         start=True, stop=True)
                    last.then_inc(s["w_sums"], 1)
                for d in range(2):
                    pe.wait_ge(s["w_used"], 2 * i + d + 1)
                    if d == 0:
                        pe.wait_ge(s["w_exp"], 2 * i + 2)
                        pe.wait_ge(s["gram_used"], 2 * i + 2)
                    else:
                        pe.wait_ge(s["turned_out"], 4 * i + 2)
                    for u, src in enumerate((BT[d], KT[d])):
                        for k in range(RB):
                            last = pe.transpose(ps[:, 5 + u, k * P:(k + 1) * P], src[:, k, :], ident[:, :])
                        last.then_inc(s["turned"], 1)
                    for half in range(2):
                        if d + half > 0:
                            pe.wait_ge(s["pairs_used"], 4 * i + 2 * d + half)
                        for u, src in enumerate((BT[d], KT[d])):
                            for h in range(GR):
                                head = head_of(half, h)
                                base = RN * (head % 2)
                                last = pe.matmul(ps[:, 1 + 2 * u + h // 2, (h % 2) * 256:(h % 2) * 256 + 256],
                                                 src[base:base + RN, head // 2, :], AR[d][base:base + RN, head // 2, :, :],
                                                 start=True, stop=True)
                        last.then_inc(s["pairs"], 1)
                with pe.Fori(0, ML) as m:
                    it = (i * ML + m) * G

                    def turn_x(g):
                        if g == 0:
                            pe.wait_ge(s["pairs_used"], 4 * i + 4)
                            pe.wait_ge(s["turned_out"], 4 * i + 4)
                        pe.wait_ge(s["x_first"], G * i + g + 1)
                        pe.wait_ge(s["x_done"], it + g + 1)
                        for h in range(GR):
                            last = pe.transpose(ps[:, g % 2, h * P:(h + 1) * P], XT[g][:, h, :], ident[:, :])
                        last.then_inc(s["x_turned"], 1)

                    def y(g):
                        pe.wait_ge(s["masked"], it + g + 1)
                        pe.wait_ge(s["x_out"], it + g + 1)
                        for h in range(GR):
                            last = pe.matmul(ps[:, 2 + g % 2, h * P:(h + 1) * P], NM[g % 2][:, h, :], X[g][:, h, :],
                                             start=True, stop=True)
                        last.then_inc(s["y_product"], 1)

                    def z(g):
                        pe.wait_ge(s["y_out"], it + g + 1)
                        pe.wait_ge(s["x_done"], it + g - 1 + XC)
                        for h in range(GR):
                            last = pe.matmul(ps[:, 4 + g % 2, h * P:(h + 1) * P], Y[g % 2][:, h, :], XT[g][:, h, :],
                                             start=True, stop=True)
                        last.then_inc(s["z_product"], 1)

                    for step in range(G):
                        turn_x(step)
                        if step >= 1:
                            y(step - 1)
                        if step >= 2:
                            z(step - 2)
                    y(G - 1)
                    z(G - 2)
                    z(G - 1)
                pe.wait_ge(s["x_done"], (i * ML + ML) * G + XC)
                pe.wait_ge(s["state_scaled"], i + 1)
                for g in range(G):
                    d, half = direction[g], g % 2
                    if g < 2:
                        for h in range(GR):
                            last = pe.matmul(ps[:, g, h * P:(h + 1) * P], fb[d][:, 0, h, :], S_g[d][:, h, :],
                                             start=True, stop=True)
                    else:
                        for pair in range(2):
                            pe.matmul(pair_slots(g, pair), AR[d][:, 2 * half + pair, 0, :], S_r[d][:, 2 * half + pair, :, :],
                                      start=True, stop=False)
                            for h in (pair, 2 + pair):
                                head = head_of(half, h)
                                last = pe.matmul(ps[:, g, h * RN:(h + 1) * RN], A_v[g][:, h, :],
                                                 tb[d][:, 2, head * RN:(head + 1) * RN], start=False, stop=(h == 2 + pair))
                    last.then_inc(s["right"], 1)
                for g in range(G):
                    if g < 2:
                        pe.wait_ge(s["right_g"], 2 * i + g + 1)
                    else:
                        pe.wait_ge(s["right_r"], 4 * i + g - 1)
                    n = width[g]
                    for h in range(GR):
                        last = pe.matmul(ps[:, g, h * n:(h + 1) * n], XT[g][:, h, :], R[g][:, h, :], start=True, stop=True)
                    last.then_inc(s["solved"], 1)
                for g in range(G):
                    d, half = direction[g], g % 2
                    if g < 2:
                        pe.wait_ge(s["u_g"], 2 * i + g + 1)
                        for h in range(GR):
                            pe.matmul(ps[:, g, h * P:(h + 1) * P], fb[d][:, 1, h, :], S_g[d][:, h, :], start=True, stop=True)
                        for h in range(GR):
                            last = pe.matmul(ps[:, 6 + g, h * P:(h + 1) * P], A_o[g][:, h, :], U[g][:, h, :],
                                             start=True, stop=True)
                        last.then_inc(s["outs"], 1)
                        continue
                    pe.wait_ge(s["u_r"], 4 * i + g - 1)
                    for pair in range(2):
                        pe.matmul(pair_slots(g, pair), AR[d][:, 2 * half + pair, 1, :], S_r[d][:, 2 * half + pair, :, :],
                                  start=True, stop=False)
                        for h in (pair, 2 + pair):
                            head = head_of(half, h)
                            o = ps[:, g, h * RN:(h + 1) * RN]
                            pe.matmul(o, A_o[g][:, h, :], U[g][:, h, :], start=False, stop=False)
                            pe.matmul(o, A_ov[g][:, h, :], tb[d][:, 2, head * RN:(head + 1) * RN], start=False,
                                      stop=(h == 2 + pair))
                    for pair in range(2):
                        k = 2 * half + pair
                        o = ps[:, g, 256 + pair * P:256 + (pair + 1) * P].rearrange("p (a n) -> p a n", a=2)
                        pe.matmul(o, BK[d][:, 0, k * P:(k + 1) * P], U[g].rearrange("p (a b) n -> p b a n", a=2)[:, pair, :, :],
                                  start=True, stop=False)
                        last = pe.matmul(o, BK[d][:, 1, k * P:(k + 1) * P],
                                         tb[d][:, 2, k * P:(k + 1) * P].rearrange("p (a n) -> p a n", a=2),
                                         start=False, stop=True)
                    last.then_inc(s["outs"], 1)
                pe.wait_ge(s["kdec"], 2 * i + 2)
                for d in range(2):
                    pe.wait_ge(s["outs_used"], G * i + d + 1)
                    for h in range(GR):
                        last = pe.matmul(ps[:, 6 + d, h * P:(h + 1) * P], KD[d][:, h, :], U[d][:, h, :],
                                         start=True, stop=True)
                    last.then_inc(s["g_state"], 1)

        @block.scalar
        def _(act):
            with act.Fori(0, TILES) as i:
                for d in range(2):
                    act.wait_ge(s["g_shift"], 2 * i + d + 1)
                    act.activation(decay[:, :, :], decay[:, :, :], ACT.Exp).then_inc(s["g_decay"], 1)
                for d in range(2):
                    act.wait_ge(s["w_sums"], 2 * i + d + 1)
                    if d == 1:
                        act.wait_ge(s["w_used"], 2 * i + 1)
                    act.activation(ends[d][:, :, :], ps[:, 7, 0:2 * RB].rearrange("p (b n) -> p b n", n=2),
                                   ACT.Exp).then_inc(s["act_chain"], 1)
                    v = pairs_view(5)
                    act.activation(e_exc[:, :, :], v[:, :, 1, :], ACT.Exp).then_inc(s["act_chain"], 1)
                    act.activation(e_inc[:, :, :], v[:, :, 0, :], ACT.Exp).then_inc(s["act_chain"], 1)
                    act.wait_ge(s["act_chain"], 6 * i + 3 * d + 3)
                    act.activation(e_neg[:, :, :], v[:, :, 0, :], ACT.Exp, scale=-1.0).then_inc(s["w_exp"], 1)
                for d in range(2):
                    for u in range(2):
                        act.wait_ge(s["turned"], 4 * i + 2 * d + u + 1)
                        act.activation(BK[d][:, u, :], ps[:, 5 + u, :], ACT.Copy).then_inc(s["turned_out"], 1)
                with act.Fori(0, ML) as m:
                    it = (i * ML + m) * G

                    def x_copy(g):
                        act.wait_ge(s["x_turned"], it + g + 1)
                        act.activation(X[g][:, :, :], heads(ps[:, g % 2, :]), ACT.Copy).then_inc(s["x_out"], 1)

                    def y_copy(g):
                        act.wait_ge(s["y_product"], it + g + 1 + YC)
                        act.activation(Y[g % 2][:, :, :], heads(ps[:, 2 + g % 2, :]), ACT.Copy).then_inc(s["y_out"], 1)

                    for step in range(G):
                        x_copy(step)
                        if step >= 1:
                            y_copy(step - 1)
                    y_copy(G - 1)
                for g in range(2, G):
                    act.wait_ge(s["right"], G * i + g + 1)
                    act.activation(R[g], heads(ps[:, g, 0:4 * RN], RN), ACT.Copy).then_inc(s["right_r"], 1)
                for g in range(2, G):
                    act.wait_ge(s["solved"], G * i + g + 1)
                    act.activation(U[g], heads(ps[:, g, 0:4 * RN], RN), ACT.Copy).then_inc(s["u_r"], 1)

        @block.gpsimd
        def _(pool):
            for d in range(2):
                pool.memset(S_g[d][:, :, :], 0.0).then_inc(s["cleared"], 1)
                pool.memset(S_r[d][:, :, :, :], 0.0).then_inc(s["cleared"], 1)
            pool.memset(out[:, :, :], 0.0).then_inc(s["cleared"], 1)
            pool.wait_ge(s["consts"], 16 * 16)
            with pool.Fori(0, TILES) as i:
                for d in range(2):
                    if d == 1:
                        pool.wait_ge(s["g_sums"], 2 * i + 1)
                    pool.sem_inc(s["pool_tick"], 1)
                    pool.tensor_tensor(grow[:, :, :], bcm(incl[d][:, :], GH), rate("g", d, tile(d, i)),
                                       ALU.mult).then_inc(s["g_rows"], 1)

                def x_first(g):
                    pool.tensor_tensor(XT[g][:, :, :], NT_[g][:, :, :], bcm(levels[direction[g]][:, 0, :], GR),
                                       ALU.mult).then_inc(s["pool_chain"], 1)
                    pool.wait_ge(s["pool_chain"], G * i + g + 1)
                    pool.tensor_tensor(XT[g][:, :, :], XT[g][:, :, :], bcm(ident[:, :], GR), ALU.add).then_inc(s["x_first"], 1)

                for g in range(2):
                    pool.wait_ge(s["gram_used"], 2 * i + g + 1)
                    x_first(g)
                pool.wait_ge(s["w_used"], 2 * i + 2)
                for d in range(2):
                    pool.wait_ge(late[d], 32 * i + 32)
                    pool.sem_inc(s["pool_tick"], 1)
                    pool.tensor_tensor(KD[d][:, :, :], heads(tb[d][:, 0, :]), rate("exp_rest", d, tile(d, i)),
                                       ALU.mult).then_inc(s["kdec"], 1)
                for g in range(2, G):
                    pool.wait_ge(s["pairs_used"], 4 * i + g - 1)
                    x_first(g)
                with pool.Fori(0, ML) as m:
                    it = (i * ML + m) * G
                    for g in range(G):
                        pool.wait_ge(s["y_product"], it + g + 1)
                        pool.sem_inc(s["pool_tick"], 1)
                        d = direction[g]
                        pool.tensor_tensor(NM[g % 2][:, :, :], NT_[g][:, :, :],
                                           levels[d][:, bass.ds(m + 1, 1), :].broadcast_to([P, GR, P]),
                                           ALU.mult).then_inc(s["masked"], 1)

        @block.vector
        def _(dve):
            dve.wait_ge(s["consts"], 16 * 16)
            dve.wait_ge(s["cleared"], 5)
            dve.sem_inc(s["turn_done"], 1)
            dve.sem_inc(s["x_done"], XC)
            dve.sem_inc(s["y_product"], YC)
            with dve.Fori(0, TILES) as i:
                link = Chain(dve, s["dve_chain"], i, PER_DVE)
                for d in range(2):
                    t = tile(d, i)
                    dve.wait_ge(s["g_sums"], 2 * i + d + 1)
                    link(dve.tensor_tensor(decay[:, :, :], heads(ps[:, 0, :]), rate("G", d, t), ALU.subtract))
                    dve.tensor_tensor(decay[:, :, :], decay[:, :, :], bcm(outside[d][:, :], GH),
                                      ALU.add).then_inc(s["g_shift"], 1)
                    dve.wait_ge(s["g_decay"], 2 * i + d + 1)
                    dve.wait_ge(s["gram"], 2 * i + d + 1)
                    v = pairs_view(1 + 2 * d)
                    for h in range(GH):
                        link(dve.scalar_tensor_tensor(NT_[d][:, h, :], v[:, h, 0, :],
                                                      rates["neg_beta"][d][:, bass.ds(t, 1), h], decay[:, h, :],
                                                      ALU.mult, ALU.mult))
                    dve.tensor_tensor(A_o[d][:, :, :], v[:, :, 1, :], decay[:, :, :], ALU.mult).then_inc(s["gram_used"], 1)
                    dve.wait_ge(s["gram_used"], 2 * i + d + 1)
                for d in range(2):
                    dve.wait_ge(s["w_exp"], 2 * i + d + 1)
                    dve.wait_ge(early[d], 48 * i + 48)
                    dve.wait_ge(late[d], 32 * i + 32)
                    link(dve.scalar_tensor_tensor(AR[d][:, :, 0, :], fb[d][:, 2, :, :], -1.0, e_exc[:, :, :],
                                                  ALU.mult, ALU.mult))
                    link(dve.tensor_tensor(AR[d][:, :, 1, :], rr[d][:, :, :], e_inc[:, :, :], ALU.mult))
                    link(dve.tensor_tensor(BT[d][:, :, :], fd[d][:, 0, :, :], e_neg[:, :, :], ALU.mult))
                    dve.tensor_tensor(KT[d][:, :, :], fd[d][:, 1, :, :], e_neg[:, :, :], ALU.mult).then_inc(s["w_used"], 1)
                for d in range(2):
                    flat = S_r[d][:, :, :, :].rearrange("p k a n -> p k (a n)")
                    link(dve.tensor_tensor(rest[d][:, :, :], bc(ends[d][:, :, 1], 2), bcm(head_cols[:, :], RB), ALU.mult))
                    scaled = dve.tensor_tensor(flat, flat, bc(ends[d][:, :, 0], P), ALU.mult)
                    if d == 0:
                        link(scaled)
                scaled.then_inc(s["state_scaled"], 1)
                dve.wait_ge(s["state_scaled"], i + 1)
                for g in range(2, G):
                    d = direction[g]
                    dve.wait_ge(s["pairs"], 4 * i + g - 1)
                    with_b, with_k = pairs_view(1), pairs_view(3)
                    link(dve.tensor_tensor(NT_[g][:, :, :], with_b[:, :, 0, :], bcm(excl[d][:, :], GR), ALU.mult))
                    link(dve.tensor_tensor(A_o[g][:, :, :], with_b[:, :, 1, :], bcm(incl[d][:, :], GR), ALU.mult))
                    link(dve.tensor_tensor(A_v[g][:, :, :], with_k[:, :, 0, :], bcm(excl[d][:, :], GR), ALU.mult))
                    dve.tensor_tensor(A_ov[g][:, :, :], with_k[:, :, 1, :], bcm(incl[d][:, :], GR),
                                      ALU.mult).then_inc(s["pairs_used"], 1)
                with dve.Fori(0, ML) as m:
                    it = (i * ML + m) * G
                    for g in range(G):
                        dve.wait_ge(s["z_product"], it + g + 1)
                        dve.wait_ge(s["x_done"], it + g + XC)
                        dve.tensor_tensor(XT[g][:, :, :], XT[g][:, :, :], heads(ps[:, 4 + g % 2, :]),
                                          ALU.add).then_inc(s["x_done"], 1)
                for d in range(2):
                    dve.wait_ge(s["right"], G * i + d + 1)
                    link(dve.tensor_tensor(R[d], heads(ps[:, d, :]), rate("exp_G", d, tile(d, i)), ALU.mult))
                    dve.tensor_tensor(R[d], heads(tb[d][:, 1, :]), R[d], ALU.subtract).then_inc(s["right_g"], 1)
                for d in range(2):
                    dve.wait_ge(s["solved"], G * i + d + 1)
                    dve.tensor_tensor(U[d], heads(ps[:, d, :]), rate("beta", d, tile(d, i)), ALU.mult).then_inc(s["u_g"], 1)
                for g in range(G):
                    d, half = direction[g], g % 2
                    t = tile(d, i)
                    dve.wait_ge(s["outs"], G * i + g + 1)
                    if g < 2:
                        o = out[:, bass.ds(t, 1), 0:GW].rearrange("p o (h n) -> p (o h) n", n=P)
                        link(dve.tensor_tensor(R[d], heads(ps[:, d, :]), rate("exp_G", d, t), ALU.mult))
                        link(dve.tensor_tensor(o, o, R[d], ALU.add))
                        dve.tensor_tensor(o, o, heads(ps[:, 6 + d, :]), ALU.add).then_inc(s["outs_used"], 1)
                        continue
                    o = out[:, bass.ds(t, 1), GW + half * 4 * RN:GW + (half + 1) * 4 * RN].rearrange(
                        "p o (b a n) -> p (o a) b n", a=2, n=RN)
                    state = S_r[d][:, 2 * half:2 * half + 2, :, :].rearrange("p k a n -> p (k a) n")
                    link(dve.tensor_tensor(state, state, heads(ps[:, g, 256:512], RN), ALU.add))
                    link(dve.tensor_tensor(state, state, bc(rest[d][:, 2 * half:2 * half + 2, :].rearrange("p k a -> p (k a)"), RN),
                                           ALU.mult))
                    dve.tensor_tensor(o, o, ps[:, g, 0:4 * RN].rearrange("p (a b n) -> p a b n", a=2, n=RN), ALU.add).then_inc(s["outs_used"], 1)
                dve.wait_ge(s["outs_used"], G * i + G)
                for d in range(2):
                    more = keep[d][:, bass.ds(i, 1)]
                    dve.wait_ge(s["g_state"], 2 * i + d + 1)
                    link(dve.tensor_scalar(S_r[d][:, :, :, :], S_r[d][:, :, :, :], more, None, ALU.mult))
                    link(dve.tensor_tensor(S_g[d][:, :, :], S_g[d][:, :, :], rate("exp_last", d, tile(d, i)), ALU.mult))
                    link(dve.tensor_tensor(S_g[d][:, :, :], S_g[d][:, :, :], heads(ps[:, 6 + d, :]), ALU.add))
                    link(dve.tensor_scalar(S_g[d][:, :, :], S_g[d][:, :, :], more, None, ALU.mult))
                dve.sem_inc(s["turn_done"], 1)
                link.done()


def gate_outputs(nc, E, ins, out, z_tm, tm_both):
    o_norm = E.sb("o_norm", [P, GD])
    ln_g, ln_b = E.sb("ln_g", [P, RW]), E.sb("ln_b", [P, RW])
    eps_g, eps_r = E.sb("eps_g", [P, 1]), E.sb("eps_r", [P, 1])
    z = [E.sb(f"z{j}", [P, GW]) for j in range(2)]
    gb = [E.sb(f"gb{j}", [P, 2, RW]) for j in range(2)]
    sq = [E.sb(f"sq{j}", [P, D]) for j in range(2)]
    stat = [E.sb(f"stat{j}", [P, GH + RH]) for j in range(2)]
    mean = [E.sb(f"mean{j}", [P, RH]) for j in range(2)]
    params, eps_set, centred, squared, summed, rooted, dve_chain, act_chain, used = (
        E.sem(n) for n in ("params", "eps_set", "centred", "squared", "summed", "rooted", "dve_chain", "act_chain", "used"))
    loaded = [E.sem(f"loaded{j}") for j in range(2)]
    with nc.Block() as block:
        @block.sync
        def _(sp):
            sp.dma_start(o_norm[:, :], ins["gdn_o_norm"][0].partition_broadcast(P)).then_inc(params, 16)
            sp.dma_start(ln_g[:, :], ins["rwkv_ln_g"][0].partition_broadcast(P)).then_inc(params, 16)
            sp.dma_start(ln_b[:, :], ins["rwkv_ln_b"][0].partition_broadcast(P)).then_inc(params, 16)

            def load(t, j):
                sp.dma_start(z[j][:, :].unsqueeze(1), z_tm[bass.ds(t, 1)].rearrange("o p n -> p o n")).then_inc(loaded[j], 16)
                sp.dma_start(gb[j][:, :, :].rearrange("p a n -> p (a n)").unsqueeze(1),
                             tm_both[bass.ds(t, 1)].rearrange("o p n -> p o n")[:, :, 3 * GW:5 * GW]).then_inc(loaded[j], 16)

            for j in range(2):
                load(j, j)
            with sp.Fori(0, TILES // 2 - 1) as i:
                for j in range(2):
                    sp.wait_ge(used, 2 * i + j + 1)
                    load(2 * i + 2 + j, j)

        @block.scalar
        def _(act):
            act.wait_ge(eps_set, 2)
            with act.Fori(0, TILES // 2) as i:
                for j in range(2):
                    act.wait_ge(centred, 2 * i + j + 1)
                    act.activation(sq[j][:, :].unsqueeze(1), out[:, bass.ds(2 * i + j, 1), :], ACT.Square).then_inc(squared, 1)
                for j in range(2):
                    act.wait_ge(summed, 2 * i + j + 1)
                    act.activation(stat[j][:, 0:GH], stat[j][:, 0:GH], ACT.Sqrt, bias=eps_g[:, :],
                                   scale=1.0 / GD).then_inc(act_chain, 1)
                    act.wait_ge(act_chain, 2 * i + j + 1)
                    act.activation(stat[j][:, GH:], stat[j][:, GH:], ACT.Sqrt, bias=eps_r[:, :],
                                   scale=1.0 / RN).then_inc(rooted, 1)

        @block.vector
        def _(dve):
            dve.memset(eps_g[:, :], EPS).then_inc(eps_set, 1)
            dve.memset(eps_r[:, :], LN_EPS).then_inc(eps_set, 1)
            dve.wait_ge(params, 48)
            with dve.Fori(0, TILES // 2) as i:
                link = Chain(dve, dve_chain, i, 24)
                for j in range(2):
                    orr = out[:, bass.ds(2 * i + j, 1), GW:D].rearrange("p o (h n) -> p (o h) n", n=RN)
                    link(dve.tensor_reduce(mean[j][:, :], orr, AX.X, ALU.add))
                    link(dve.tensor_scalar(mean[j][:, :], mean[j][:, :], 1.0 / RN, None, ALU.mult))
                    dve.tensor_tensor(orr, orr, bc(mean[j][:, :], RN), ALU.subtract).then_inc(centred, 1)
                for j in range(2):
                    dve.wait_ge(squared, 2 * i + j + 1)
                    link(dve.tensor_reduce(stat[j][:, 0:GH], sq[j][:, 0:GW].rearrange("p (h n) -> p h n", n=GD), AX.X, ALU.add))
                    dve.tensor_reduce(stat[j][:, GH:], sq[j][:, GW:].rearrange("p (h n) -> p h n", n=RN), AX.X,
                                      ALU.add).then_inc(summed, 1)
                for j in range(2):
                    og = out[:, bass.ds(2 * i + j, 1), 0:GW].rearrange("p o (h n) -> p (o h) n", n=GD)
                    orr = out[:, bass.ds(2 * i + j, 1), GW:D].rearrange("p o (h n) -> p (o h) n", n=RN)
                    of = out[:, bass.ds(2 * i + j, 1), GW:D]
                    dve.wait_ge(rooted, 2 * i + j + 1)
                    dve.wait_ge(loaded[j], 32 * i + 32)
                    link(dve.reciprocal(stat[j][:, :], stat[j][:, :]))
                    link(dve.tensor_tensor(og, og, bc(stat[j][:, 0:GH], GD), ALU.mult))
                    link(dve.tensor_tensor(og, og, bcm(o_norm[:, :], GH), ALU.mult))
                    link(dve.tensor_tensor(og, og, z[j][:, :].rearrange("p (h n) -> p h n", n=GD), ALU.mult))
                    link(dve.tensor_tensor(orr, orr, bc(stat[j][:, GH:], RN), ALU.mult))
                    link(dve.tensor_tensor(of, of, ln_g[:, :].unsqueeze(1), ALU.mult))
                    link(dve.tensor_tensor(of, of, ln_b[:, :].unsqueeze(1), ALU.add))
                    link(dve.tensor_tensor(of, of, gb[j][:, 1:2, :], ALU.add))
                    dve.tensor_tensor(of, of, gb[j][:, 0:1, :], ALU.mult).then_inc(used, 1)
                dve.wait_ge(used, 2 * i + 2)
                link(dve.tensor_copy(mean[0][:, 0:1], mean[0][:, 0:1]))
                link(dve.tensor_copy(mean[0][:, 0:1], mean[0][:, 0:1]))
                link.done()


def project_out(nc, E, ident, mix, w_out):
    w = E.sb("w", [P, KB, D])
    mT = [E.sb(f"mT{j}", [P, KB, P]) for j in range(2)]
    ps = [E.stack.enter_context(nc.psum_tensor(f"{E.tag}_ps{j}", [P, 2, 512], F32)) for j in range(4)]
    w_loaded, turned, turned_out, product, done = (E.sem(n) for n in ("w_loaded", "turned", "turned_out", "product", "done"))
    with nc.Block() as block:
        @block.sync
        def _(sp):
            sp.dma_start(w[:, :, :], w_out.rearrange("(k p) n -> p k n", p=P)).then_inc(w_loaded, 16)

        @block.tensor
        def _(pe):
            def turn(t):
                if t >= 2:
                    pe.wait_ge(turned_out, t - 1)
                for k in range(KB):
                    last = pe.transpose(ps[t % 2][:, k // 4, (k % 4) * P:(k % 4 + 1) * P], mix[:, t, k * P:(k + 1) * P], ident[:, :])
                last.then_inc(turned, 1)

            turn(0)
            for t in range(TILES):
                if t + 1 < TILES:
                    turn(t + 1)
                if t == 0:
                    pe.wait_ge(w_loaded, 16)
                pe.wait_ge(turned_out, t + 1)
                if t >= 2:
                    pe.wait_ge(done, t - 1)
                for half in range(2):
                    for k in range(KB):
                        last = pe.matmul(ps[2 + t % 2][:, half, :], mT[t % 2][:, k, :], w[:, k, half * 512:(half + 1) * 512],
                                         start=(k == 0), stop=(k == KB - 1))
                last.then_inc(product, 1)

        @block.vector
        def _(dve):
            for t in range(TILES):
                dve.wait_ge(turned, t + 1)
                if t >= 2:
                    dve.wait_ge(product, t - 1)
                dve.tensor_copy(mT[t % 2][:, :, :].rearrange("p (a b) n -> p a (b n)", a=2), ps[t % 2][:, :, :]).then_inc(turned_out, 1)

        @block.scalar
        def _(act):
            for t in range(TILES):
                act.wait_ge(product, t + 1)
                act.activation(mix[:, t, :].rearrange("p (a n) -> p a n", a=2), ps[2 + t % 2][:, :, :], ACT.Copy).then_inc(done, 1)
            act.wait_ge(done, TILES)


def latents(nc, E, ins, hT, qlT, kvlT, krT, cos, sin):
    n_cols = Q_LORA + KV_LORA + ROPE
    half = ROPE // 2
    w = E.sb("w", [P, KB, n_cols + ROPE])
    ones = E.sb("ones", [P, P])
    eps = E.sb("eps", [P, 1])
    g = E.sb("g", [P, 3])
    raw = E.sb("raw", [P, 3, 512])
    sq = E.sb("sq", [P, 3, 512])
    root = E.sb("root", [P, 2, 512])
    part = [E.sb(f"part{u}", [ROPE, 512]) for u in range(2)]
    bank = E.banks(8)
    loaded, eps_set, product, raw_out, squared, sums, rooted, normal, rope_done, act_chain, dve_chain = (
        E.sem(n) for n in ("loaded", "eps_set", "product", "raw_out", "squared", "sums", "rooted", "normal", "rope_done",
                           "act_chain", "dve_chain"))
    w_in = ins["w_in_odd"][0].rearrange("(k p) n -> p k n", p=P)
    rope0 = Q_LORA + KV_LORA
    with nc.Block() as block:
        @block.sync
        def _(sp):
            sp.dma_start(w[:, :, 0:n_cols], w_in).then_inc(loaded, 16)
            sp.dma_start(w[:, :, n_cols:n_cols + half], w_in[:, :, rope0 + half:rope0 + ROPE]).then_inc(loaded, 16)
            sp.dma_start(w[:, :, n_cols + half:n_cols + ROPE], w_in[:, :, rope0:rope0 + half]).then_inc(loaded, 16)
            sp.dma_start(ones[:, :], ins["c_ones"]).then_inc(loaded, 16)
            sp.dma_start(cos[:, :], ins["c_cos"]).then_inc(loaded, 16)
            sp.dma_start(sin[:, :], ins["c_sin"]).then_inc(loaded, 16)
            sp.dma_start(g[:, 0:2], ins["mla_q_norm"][0].rearrange("(k p) -> p k", p=P),
                         allow_slow_non_contiguous=True).then_inc(loaded, 16)
            sp.dma_start(g[:, 2:3], ins["mla_kv_norm"].rearrange("n p -> p n"), allow_slow_non_contiguous=True).then_inc(loaded, 16)

        @block.tensor
        def _(pe):
            pe.wait_ge(loaded, 16 * 8)
            for q, (t0, n) in enumerate(PIECES):
                if q > 0:
                    pe.wait_ge(raw_out, 3 * q)
                    pe.wait_ge(rope_done, q)
                for b in range(5):
                    c0, m = (b * P, P) if b < 3 else (rope0 + (b - 3) * ROPE, ROPE)
                    for k in range(KB):
                        last = pe.matmul(bank[b][0:m, 0:n], w[:, k, c0:c0 + m], hT[:, k, t0:t0 + n],
                                         start=(k == 0), stop=(k == KB - 1))
                    last.then_inc(product, 1)
                pe.wait_ge(squared, 3 * q + 3)
                if q > 0:
                    pe.wait_ge(rooted, 2 * q)
                pe.matmul(bank[5][:, 0:n], ones[:, :], sq[:, 0, 0:n], start=True, stop=False)
                pe.matmul(bank[5][:, 0:n], ones[:, :], sq[:, 1, 0:n], start=False, stop=True)
                pe.matmul(bank[6][:, 0:n], ones[:, :], sq[:, 2, 0:n], start=True, stop=True).then_inc(sums, 1)

        @block.scalar
        def _(act):
            act.wait_ge(eps_set, 1)
            link = Chain(act, act_chain)
            for q, (t0, n) in enumerate(PIECES):
                if q > 0:
                    act.wait_ge(normal, 3 * q)
                for b in range(3):
                    act.wait_ge(product, 5 * q + b + 1)
                    act.activation(raw[:, b, 0:n], bank[b][:, 0:n], ACT.Copy).then_inc(raw_out, 1)
                act.wait_ge(raw_out, 3 * q + 3)
                for b in range(3):
                    act.activation(sq[:, b, 0:n], raw[:, b, 0:n], ACT.Square).then_inc(squared, 1)
                act.wait_ge(sums, q + 1)
                for u, width in enumerate((Q_LORA, KV_LORA)):
                    act.activation(root[:, u, 0:n], bank[5 + u][:, 0:n], ACT.Sqrt, bias=eps[:, :],
                                   scale=1.0 / width).then_inc(rooted, 1)

        @block.vector
        def _(dve):
            dve.memset(eps[:, :], EPS).then_inc(eps_set, 1)
            link = Chain(dve, dve_chain)
            dve.wait_ge(loaded, 16 * 8)
            for q, (t0, n) in enumerate(PIECES):
                for u, table in enumerate((cos, sin)):
                    dve.wait_ge(product, 5 * q + 4 + u)
                    link(dve.tensor_tensor(part[u][:, 0:n], bank[3 + u][0:ROPE, 0:n], table[:, t0:t0 + n], ALU.mult))
                dve.tensor_tensor(krT[:, t0:t0 + n], part[0][:, 0:n], part[1][:, 0:n], ALU.add).then_inc(rope_done, 1)
                dve.wait_ge(rope_done, q + 1)
                dve.wait_ge(rooted, 2 * q + 2)
                link(dve.reciprocal(root[:, :, 0:n], root[:, :, 0:n]))
                for b in range(3):
                    dst = qlT[:, b, t0:t0 + n] if b < 2 else kvlT[:, t0:t0 + n]
                    dve.scalar_tensor_tensor(dst, raw[:, b, 0:n], g[:, b:b + 1], root[:, b // 2, 0:n],
                                             ALU.mult, ALU.mult).then_inc(normal, 1)
            dve.wait_ge(normal, 3 * len(PIECES))


def values(nc, E, ins, kvlT, V):
    w = E.sb("w", [P, MH * MV])
    bank = E.banks(8)
    loaded, product, act_out, dve_out = (E.sem(n) for n in ("loaded", "product", "act_out", "dve_out"))
    wv = ins["mla_w_kv_b"][0].rearrange("p (h n) -> p h n", n=NOPE + MV)
    with nc.Block() as block:
        @block.sync
        def _(sp):
            sp.dma_start(w[:, :].rearrange("p (h n) -> p h n", n=MV), wv[:, :, NOPE:NOPE + MV]).then_inc(loaded, 16)

        @block.tensor
        def _(pe):
            pe.wait_ge(loaded, 16)
            for t in range(TILES):
                if t >= 4:
                    pe.wait_ge(act_out, t - 3)
                    pe.wait_ge(dve_out, t - 3)
                for half in range(2):
                    pe.matmul(bank[2 * (t % 4) + half][:, :], kvlT[:, t * P:(t + 1) * P], w[:, half * 512:(half + 1) * 512],
                              start=True, stop=True).then_inc(product, 1)

        @block.scalar
        def _(act):
            for t in range(TILES):
                act.wait_ge(product, 2 * t + 1)
                act.activation(V[:, t, 0:512], bank[2 * (t % 4)][:, :], ACT.Copy).then_inc(act_out, 1)
            act.wait_ge(act_out, TILES)

        @block.vector
        def _(dve):
            for t in range(TILES):
                dve.wait_ge(product, 2 * t + 2)
                dve.tensor_copy(V[:, t, 512:1024], bank[2 * (t % 4) + 1][:, :]).then_inc(dve_out, 1)
            dve.wait_ge(dve_out, TILES)


def attend(nc, E, ins, ident, qlT, kvlT, krT, cos, sin, V, out):
    half = ROPE // 2
    SCALE = float(NOPE + ROPE) ** -0.5
    wq = E.sb("wq", [P, 2, NOPE])
    wr = E.sb("wr", [P, 2, 2, ROPE])
    wk = E.sb("wk", [P, NOPE])
    qn, kn = E.sb("qn", [P, NT]), E.sb("kn", [P, NT])
    qr = E.sb("qr", [ROPE, NT])
    part = [E.sb(f"part{u}", [ROPE, 512]) for u in range(2)]
    w_sm = [E.sb(f"w_sm{j}", [P, T_PROMPT]) for j in range(2)]
    wT = [E.sb(f"wT{j}", [P, T_PROMPT // P, P]) for j in range(2)]
    mx, neg = (E.sb(n, [P, 2]) for n in ("mx", "neg"))
    total, inv = (E.sb(n, [P, TILES]) for n in ("total", "inv"))
    ps = E.stack.enter_context(nc.psum_tensor(f"{E.tag}_ps", [P, 8, 512], F32))
    SCORES, TURN, OUT = (0, 2), 4, 6
    names = ("w_loaded", "q_product", "r_product", "k_product", "q_out", "k_out", "r_out", "scores", "shifted", "exped",
             "turned", "turned_a", "turned_b", "weighted", "written", "dve_chain")
    s = {n: E.sem(n) for n in names}
    w_q = ins["mla_w_q_b"][0].rearrange("(k p) n -> p k n", p=P)
    w_kv = ins["mla_w_kv_b"][0]
    NQ = len(PIECES)

    def keys(t):
        return (0, T_PROMPT) if t < TILES_P else (T_PROMPT, T_SAMPLE)

    with nc.Block() as block:
        @block.sync
        def _(sp):
            def load(h):
                c = h * (NOPE + ROPE)
                sp.dma_start(wq[:, :, :], w_q[:, :, bass.ds(c, NOPE)]).then_inc(s["w_loaded"], 16)
                sp.dma_start(wr[:, :, 0, :], w_q[:, :, bass.ds(c + NOPE, ROPE)]).then_inc(s["w_loaded"], 16)
                sp.dma_start(wr[:, :, 1, 0:half], w_q[:, :, bass.ds(c + NOPE + half, half)]).then_inc(s["w_loaded"], 16)
                sp.dma_start(wr[:, :, 1, half:ROPE], w_q[:, :, bass.ds(c + NOPE, half)]).then_inc(s["w_loaded"], 16)
                sp.dma_start(wk[:, :], w_kv[:, bass.ds(h * (NOPE + MV), NOPE)]).then_inc(s["w_loaded"], 16)

            load(0)
            with sp.Fori(0, MH - 1) as h:
                sp.wait_ge(s["k_product"], NQ * h + NQ)
                load(h + 1)

        @block.tensor
        def _(pe):
            with pe.Fori(0, MH) as h:
                pe.wait_ge(s["w_loaded"], 80 * h + 80)
                pe.wait_ge(s["exped"], TILES * h + 2)
                for q, (t0, n) in enumerate(PIECES):
                    if q == 2:
                        pe.wait_ge(s["q_out"], NQ * h + 1)
                        pe.wait_ge(s["k_out"], NQ * h + 1)
                    for k in range(2):
                        last = pe.matmul(ps[:, q % 2, 0:n], wq[:, k, :], qlT[:, k, t0:t0 + n], start=(k == 0), stop=(k == 1))
                    last.then_inc(s["q_product"], 1)
                    if q > 0:
                        pe.wait_ge(s["r_out"], NQ * h + q)
                    for u in range(2):
                        for k in range(2):
                            last = pe.matmul(ps[0:ROPE, 2 + u, 0:n], wr[:, k, u, :], qlT[:, k, t0:t0 + n],
                                             start=(k == 0), stop=(k == 1))
                    last.then_inc(s["r_product"], 1)
                    pe.matmul(ps[:, 4 + q % 2, 0:n], wk[:, :], kvlT[:, t0:t0 + n], start=True, stop=True).then_inc(s["k_product"], 1)
                pe.wait_ge(s["q_out"], NQ * h + NQ)
                pe.wait_ge(s["k_out"], NQ * h + NQ)
                pe.wait_ge(s["r_out"], NQ * h + NQ)

                def scores(t):
                    k0, nk = keys(t)
                    pe.wait_ge(s["exped"], TILES * h + t + 1)
                    for c in range(0, nk, 512):
                        n = min(512, nk - c)
                        o = ps[:, SCORES[t % 2] + c // 512, 0:n]
                        pe.matmul(o, qn[:, t * P:(t + 1) * P], kn[:, k0 + c:k0 + c + n], start=True, stop=False)
                        last = pe.matmul(o, qr[:, t * P:(t + 1) * P], krT[:, k0 + c:k0 + c + n], start=False, stop=True)
                    last.then_inc(s["scores"], 1)

                def turn(t):
                    nk = keys(t)[1]
                    pe.wait_ge(s["exped"], TILES * h + t + 1 + 2)
                    pe.wait_ge(s["turned_a"], TILES * h + t + 1)
                    pe.wait_ge(s["turned_b"], TILES * h + t + 1)
                    for b in range(nk // P):
                        last = pe.transpose(ps[:, TURN + b // 4, (b % 4) * P:(b % 4 + 1) * P],
                                            w_sm[t % 2][:, b * P:(b + 1) * P], ident[:, :])
                    last.then_inc(s["turned"], 1)

                def weigh(t):
                    k0, nk = keys(t)
                    pe.wait_ge(s["turned_a"], TILES * h + t + 2)
                    pe.wait_ge(s["turned_b"], TILES * h + t + 2)
                    pe.wait_ge(s["written"], TILES * h + t + 1)
                    for b in range(nk // P):
                        last = pe.matmul(ps[:, OUT + t % 2, 0:MV], wT[t % 2][:, b, :],
                                         V[:, k0 // P + b, bass.ds(h * MV, MV)], start=(b == 0), stop=(b == nk // P - 1))
                    last.then_inc(s["weighted"], 1)

                for t in range(TILES + 2):
                    if t < TILES:
                        scores(t)
                    if 1 <= t <= TILES:
                        turn(t - 1)
                    if t >= 2:
                        weigh(t - 2)

        @block.scalar
        def _(act):
            act.sem_inc(s["exped"], 2)
            act.sem_inc(s["turned_a"], 1)
            with act.Fori(0, MH) as h:
                for q, (t0, n) in enumerate(PIECES):
                    act.wait_ge(s["q_product"], NQ * h + q + 1)
                    if q == 0:
                        act.wait_ge(s["scores"], TILES * h + 1)
                    act.activation(qn[:, t0:t0 + n], ps[:, q % 2, 0:n], ACT.Copy).then_inc(s["q_out"], 1)
                    act.wait_ge(s["k_product"], NQ * h + q + 1)
                    act.activation(kn[:, t0:t0 + n], ps[:, 4 + q % 2, 0:n], ACT.Copy).then_inc(s["k_out"], 1)

                def exps(t):
                    nk = keys(t)[1]
                    act.wait_ge(s["shifted"], TILES * h + t + 1)
                    act.activation(w_sm[t % 2][:, 0:nk], ps[:, SCORES[t % 2]:SCORES[t % 2] + 2, :].rearrange("p a n -> p (a n)")[:, 0:nk],
                                   ACT.Exp, bias=neg[:, t % 2:t % 2 + 1], scale=SCALE,
                                   accum_out=total[:, t:t + 1]).then_inc(s["exped"], 1)

                def copy(t):
                    nb = keys(t)[1] // P // 2
                    act.wait_ge(s["turned"], TILES * h + t + 1)
                    act.activation(wT[t % 2][:, 0:nb, :].rearrange("p b n -> p (b n)"), ps[:, TURN, 0:nb * P],
                                   ACT.Copy).then_inc(s["turned_a"], 1)

                for t in range(TILES + 1):
                    if t < TILES:
                        exps(t)
                    if t >= 1:
                        copy(t - 1)

        @block.vector
        def _(dve):
            dve.sem_inc(s["turned_b"], 1)
            dve.sem_inc(s["scores"], 1)
            dve.sem_inc(s["written"], 2)
            with dve.Fori(0, MH) as h:
                link = Chain(dve, s["dve_chain"], h, 2 * NQ + 2 * TILES)
                for q, (t0, n) in enumerate(PIECES):
                    dve.wait_ge(s["r_product"], NQ * h + q + 1)
                    for u, table in enumerate((cos, sin)):
                        link(dve.tensor_tensor(part[u][:, 0:n], ps[0:ROPE, 2 + u, 0:n], table[:, t0:t0 + n], ALU.mult))
                    dve.tensor_tensor(qr[:, t0:t0 + n], part[0][:, 0:n], part[1][:, 0:n], ALU.add).then_inc(s["r_out"], 1)
                    dve.wait_ge(s["r_out"], NQ * h + q + 1)

                def shift(t):
                    nk = keys(t)[1]
                    dve.wait_ge(s["scores"], TILES * h + t + 2)
                    j = slice(t % 2, t % 2 + 1)
                    link(dve.reduce_max(mx[:, j], ps[:, SCORES[t % 2]:SCORES[t % 2] + 2, :].rearrange("p a n -> p (a n)")[:, 0:nk], AX.X))
                    dve.tensor_scalar(neg[:, j], mx[:, j], -SCALE, None, ALU.mult).then_inc(s["shifted"], 1)

                def copy(t):
                    nb = keys(t)[1] // P // 2
                    dve.wait_ge(s["turned"], TILES * h + t + 1)
                    bank, c0 = (TURN + 1, 0) if nb == 4 else (TURN, nb * P)
                    if nb < 4:
                        dve.wait_ge(s["turned_a"], TILES * h + t + 2)
                    dve.tensor_copy(wT[t % 2][:, nb:2 * nb, :].rearrange("p b n -> p (b n)"), ps[:, bank, c0:c0 + nb * P]
                                    ).then_inc(s["turned_b"], 1)

                def write(t):
                    j = slice(t, t + 1)
                    link(dve.reciprocal(inv[:, j], total[:, j]))
                    dve.wait_ge(s["weighted"], TILES * h + t + 1)
                    dve.tensor_scalar(out[:, t, bass.ds(h * MV, MV)], ps[:, OUT + t % 2, 0:MV], inv[:, j], None,
                                      ALU.mult).then_inc(s["written"], 1)

                for t in range(TILES + 2):
                    if t < TILES:
                        shift(t)
                    if 1 <= t <= TILES:
                        copy(t - 1)
                    if t >= 2:
                        write(t - 2)
                link.done()


def attention(nc, phase, dram, ins, acc, hT, ident):
    with ExitStack() as own:
        def sb(name, shape):
            return own.enter_context(nc.sbuf_tensor(name, shape, F32))
        qlT, kvlT, krT = sb("qlT", [P, 2, NT]), sb("kvlT", [P, NT]), sb("krT", [ROPE, NT])
        cos, sin = sb("cos", [ROPE, NT]), sb("sin", [ROPE, NT])
        phase("latent", latents, ins, hT, qlT, kvlT, krT, cos, sin)
        V = hT[:, :, :].rearrange("p k n -> p (k n)").rearrange("p (t n) -> p t n", n=MH * MV)
        phase("values", values, ins, kvlT, V)
        phase("attend", attend, ins, ident, qlT, kvlT, krT, cos, sin, V, acc)
    phase("out1", project_out, ident, acc, ins["w_out_odd"][0])


def clear_semaphores(nc, sems):
    with nc.Block() as block:
        @block.sync
        def _(sp):
            for sem in sems:
                sp.sem_clear(sem)


def program(nc, ins, outs, stop=99):
    scratch = {}

    def dram(name, shape):
        scratch[name] = nc.dram_tensor(f"s_{name}", shape, F32, kind="Internal").ap()
        return scratch[name]

    with ExitStack() as whole:
        def scope(tag):
            stack = ExitStack()
            E = Env(nc, stack, tag)
            E.sems = whole
            return stack, E

        _, top = scope("top")
        top.stack = whole
        acc = top.sb("acc", [P, TILES, D])
        gates = top.sb("gates", [P, TILES, 4 * GH])
        ident = top.sb("ident", [P, P])
        ident_loaded = top.sem("ident_loaded")
        with nc.Block() as block:
            @block.sync
            def _(sp):
                sp.dma_start(ident[:, :], ins["c_ident"]).then_inc(ident_loaded, 16)
                sp.wait_ge(ident_loaded, 16)

        conv_fm = dram("conv", [CONV_BLOCKS, P, NT])
        shift_fm = dram("shift", [RWKV_BLOCKS, P, NT])
        z_tm = dram("z", [TILES, P, GW])

        def phase(tag, f, *args, **kw):
            stack, E = scope(tag)
            with stack:
                E.sems = stack
                f(nc, E, *args, **kw)
                clear_semaphores(nc, E.made)

        with ExitStack() as wide:
            X = wide.enter_context(nc.sbuf_tensor("x_first", [P, TILES, D], F32))
            hT = wide.enter_context(nc.sbuf_tensor("hT_first", [P, KB, NT], F32))
            phase("load0", load_x, X, ins["x_prompt"], ins["x_sample"])
            phase("norm0", residual_norm, X, hT, ident, None, None, ins["norm_mix_pre"][0])
            w_in = ins["w_in_even"][0]
            phase("conv", in_proj_fm, hT, w_in, 0, CONV_BLOCKS // 3, conv_fm, ins["gdn_conv"][0], True)
            phase("shift", in_proj_fm, hT, w_in, GDN_COLS, RWKV_BLOCKS // 3, shift_fm, ins["rwkv_mu"][0], False)
            phase("gates", in_proj_tm, hT, w_in, gates, z_tm)
        if stop > 1:
            mix_scopes(nc, phase, dram, ins, acc, gates, ident, conv_fm, shift_fm, z_tm, stop)
        if stop <= 4:
            return scratch
        X = whole.enter_context(nc.sbuf_tensor("x_stream", [P, TILES, D], F32))
        hT = whole.enter_context(nc.sbuf_tensor("hT", [P, KB, NT], F32))
        phase("load1", load_x, X, ins["x_prompt"], ins["x_sample"])
        phase("norm1", residual_norm, X, hT, ident, acc, ins["norm_mix_post"][0], ins["norm_ffn_pre"][0])
        phase("ffn0", feed_forward, hT, acc, ins["w_ff1"][0], ins["w_ff2"][0])
        if stop == 5:
            return scratch
        phase("norm2", residual_norm, X, hT, ident, acc, ins["norm_ffn_post"][0], ins["norm_mix_pre"][1])
        if stop < 6:
            return scratch
        attention(nc, phase, dram, ins, acc, hT, ident)
        if stop <= 6:
            return scratch
        phase("norm3", residual_norm, X, hT, ident, acc, ins["norm_mix_post"][1], ins["norm_ffn_pre"][1])
        phase("ffn1", feed_forward, hT, acc, ins["w_ff1"][1], ins["w_ff2"][1])
        phase("norm4", residual_norm, X, hT, ident, acc, ins["norm_ffn_post"][1], None, outs)
    return scratch


def constants():
    s = np.arange(P)[:, None]
    t = np.arange(P)[None, :]
    mid = P // 2
    c = {"c_ident": np.eye(P), "c_ones": np.ones((P, P))}
    c["c_head_ones"] = (s // RN == t // RN) * 1.0
    c["c_head_cols"] = (s // RN == np.arange(2)[None, :]) * 1.0
    incl = np.stack([s <= t, s >= t]) * 1.0
    excl = np.stack([s < t, s > t]) * 1.0
    c["c_incl"], c["c_excl"] = incl, excl
    c["c_outside"] = (incl - 1.0) * 1e9
    rate = -math.exp(-0.5)
    upto_mid = incl[:, :, mid:mid + 1]
    c["c_decay_sums"] = rate * (np.concatenate([incl, excl], 2) - upto_mid)
    c["c_decay_ends"] = rate * np.concatenate([upto_mid, 1.0 - upto_mid], 2)
    levels = []
    for m in range(LEVELS):
        n = 1 << m
        lower = ((s // n) % 2 == 0) & (t // n == s // n + 1)
        levels.append(lower)
    c["c_levels"] = np.stack([np.stack(levels), np.stack(levels).transpose(0, 2, 1)]) * 1.0
    keep = np.ones((2, P, TILES))
    keep[0, :, TILES_P - 1] = 0.0
    keep[1, :, TILES - TILES_P - 1] = 0.0
    c["c_keep"] = keep
    inv = 1.0 / (np.float32(10000.0) ** (np.arange(0, ROPE, 2, dtype=np.float32) / np.float32(ROPE)))
    at = np.concatenate([np.arange(T_PROMPT), np.arange(T_SAMPLE)]).astype(np.float32)
    ang = (inv.astype(np.float32)[:, None] * at[None, :]).astype(np.float32)
    c["c_cos"] = np.concatenate([np.cos(ang), np.cos(ang)], 0)
    c["c_sin"] = np.concatenate([-np.sin(ang), np.sin(ang)], 0)
    return {k: np.ascontiguousarray(v, dtype=np.float32) for k, v in c.items()}


_OUTS = ((1, T_PROMPT, D), (1, T_SAMPLE, D))


def kernel(**inputs):
    import concourse.bacc as bacc
    from concourse.bass_utils import run_bass_kernel_spmd

    nc = bacc.Bacc("TRN2", target_bir_lowering=False, num_devices=1)
    arrays, ins = {}, {}
    for name, a in {**inputs, **constants()}.items():
        a = np.ascontiguousarray(a)
        arrays[f"in_{name}"] = a
        ins[name] = nc.dram_tensor(f"in_{name}", a.shape, F32, kind="ExternalInput").ap()
    outs = tuple(nc.dram_tensor(f"out_{i}", shape, F32, kind="ExternalOutput").ap() for i, shape in enumerate(_OUTS))
    program(nc, ins, outs)
    r = run_bass_kernel_spmd(nc, [arrays], core_ids=[0])
    return tuple(r.results[0][f"out_{i}"] for i in range(len(_OUTS)))
```

```python
import math
from contextlib import ExitStack

import numpy as np
import concourse.bass as bass
from concourse import mybir

F32 = mybir.dt.float32
F32R = mybir.dt.float32r
ACT = mybir.ActivationFunctionType
ALU = mybir.AluOpType
AX = mybir.AxisListType

P = 128
D = 1024
KB = D // P
T_PROMPT, T_SAMPLE = 1024, 256
NT = T_PROMPT + T_SAMPLE
TILES = NT // P
TILES_P = T_PROMPT // P
D_FF = 4 * D
EPS = 1e-6
GH, GD = 4, 128
GW = GH * GD
RH, RN = 8, 64
RW = RH * RN
RB = RW // P
LN_EPS = 64e-5
GDN_COLS = 4 * GW + 4 * GH
CONV_BLOCKS = 3 * GW // P
RWKV_BLOCKS = 15
TAPS = 5
PAD = 2
PADDED = PAD + T_PROMPT + PAD + T_SAMPLE + PAD
SPAN = T_PROMPT + PAD + T_SAMPLE
PIECES = ((0, 512), (512, 512), (1024, 256))
LEVELS = 7
MH, NOPE, ROPE, MV = 8, 128, 64, 128
Q_LORA, KV_LORA = 256, 128


def bc(ap, n):
    return ap.unsqueeze(2).broadcast_to([ap.shape[0], ap.shape[1], n])


def bcm(ap, m):
    return ap.unsqueeze(1).broadcast_to([ap.shape[0], m, ap.shape[1]])


class Chain:

    def __init__(self, eng, sem, i=None, per=0):
        self.eng, self.sem, self.i, self.per, self.n = eng, sem, i, per, 0

    def __call__(self, ins):
        self.n += 1
        ins.then_inc(self.sem, 1)
        self.eng.wait_ge(self.sem, self.n if self.i is None else self.i * self.per + self.n)

    def done(self):
        assert self.i is None or self.n == self.per, (self.sem, self.n, self.per)


class Env:

    def __init__(self, nc, stack, tag):
        self.nc, self.stack, self.tag, self.made = nc, stack, tag, []

    def sb(self, name, shape, dtype=F32):
        return self.stack.enter_context(self.nc.sbuf_tensor(f"{self.tag}_{name}", shape, dtype))

    def pair(self, name, shape):
        return [self.sb(f"{name}_{part}", shape, F32R) for part in ("high", "low")]

    def banks(self, n):
        return [self.stack.enter_context(self.nc.psum_tensor(f"{self.tag}_bank{i}", [P, 512], F32)) for i in range(n)]

    def sem(self, name):
        sem = self.sems.enter_context(self.nc.semaphore(f"{self.tag}_{name}"))
        self.made.append(sem)
        return sem


def token_tiles(prompt, sample):
    return tuple(v[0].rearrange("(t p) d -> p t d", p=P) for v in (prompt, sample))


def product(pe, out, stationary, moving, start, stop):
    pe.matmul(out, stationary[0], moving[0], start=start, stop=False)
    pe.matmul(out, stationary[0], moving[1], start=False, stop=False)
    return pe.matmul(out, stationary[1], moving[0], start=False, stop=stop)


def both(pair, *index):
    return tuple(part[index] for part in pair)


def residual_norm(nc, E, x_src, x_dst, hT, ident, X, g_post, g_pre):
    mixed = g_post is not None
    x_old = E.sb("x_old", [P, 2, D])
    gpost = E.sb("gpost", [P, D])
    gpre = E.sb("gpre", [P, KB])
    eps = E.sb("eps", [P, 1])
    h = [E.sb(f"h{j}", [P, D]) for j in range(2)]
    h_out = [E.sb(f"h_out{j}", [P, KB, P]) for j in range(2)]
    junk = [h_out[j][:, :, :].rearrange("p k n -> p (k n)") for j in range(2)]
    sq1, rt1, rc1, sq2, rt2, rc2 = (E.sb(n, [P, 2]) for n in ("sq1", "rt1", "rc1", "sq2", "rt2", "rc2"))
    ps = [E.stack.enter_context(nc.psum_tensor(f"{E.tag}_ps{j}", [P, KB, P], F32)) for j in range(2)]
    gains, eps_set, mix_root, x_updated, x_root, h_ready, turned, scaled, high_done, low_done, act_chain, dve_chain, stored, loaded, tick = (
        E.sem(n) for n in ("gains", "eps_set", "mix_root", "x_updated", "x_root", "h_ready", "turned", "scaled",
                           "high_done", "low_done", "act_chain", "dve_chain", "stored", "loaded", "tick"))
    n_gains = 16 * (mixed + (g_pre is not None))
    TURNS, TURNS_P = TILES // 2, TILES_P // 2
    with nc.Block() as block:
        @block.sync
        def _(sp):
            def pair_of(view, i):
                return view[:, bass.ds(2 * i, 2), :]

            if mixed:
                sp.dma_start(x_old[:, :, :], pair_of(x_src[0], 0)).then_inc(loaded, 16)
                sp.dma_start(gpost[:, :], g_post.partition_broadcast(P)).then_inc(gains, 16)
            if g_pre is not None:
                sp.dma_start(gpre[:, :], g_pre.rearrange("(k p) -> p k", p=P),
                             allow_slow_non_contiguous=True).then_inc(gains, 16)
            if mixed:
                with sp.Fori(0, TURNS_P - 1) as i:
                    sp.wait_ge(x_updated, 2 * i + 2)
                    sp.dma_start(x_old[:, :, :], pair_of(x_src[0], i + 1)).then_inc(loaded, 16)
                    sp.dma_start(pair_of(x_dst[0], i), pair_of(X, i)).then_inc(stored, 16)
                sp.wait_ge(x_updated, 2 * TURNS_P)
                sp.dma_start(x_old[:, :, :], x_src[1]).then_inc(loaded, 16)
                sp.dma_start(pair_of(x_dst[0], TURNS_P - 1), pair_of(X, TURNS_P - 1)).then_inc(stored, 16)
                sp.wait_ge(x_updated, TILES)
                sp.dma_start(x_dst[1], pair_of(X, TURNS_P)).then_inc(stored, 16)
                sp.wait_ge(stored, 16 * TURNS)
            else:
                sp.dma_start(pair_of(X, 0), pair_of(x_src[0], 0)).then_inc(loaded, 16)
                with sp.Fori(0, TURNS_P - 1) as i:
                    sp.wait_ge(loaded, 16 * i + 16)
                    sp.dma_start(pair_of(X, i + 1), pair_of(x_src[0], i + 1)).then_inc(loaded, 16)
                sp.wait_ge(loaded, 16 * TURNS_P)
                sp.dma_start(pair_of(X, TURNS_P), x_src[1]).then_inc(loaded, 16)

        @block.scalar
        def _(act):
            act.wait_ge(eps_set, 1)
            act.sem_inc(low_done, 2)
            with act.Fori(0, TURNS) as i:
                link = Chain(act, act_chain, i, 2 * mixed + 2 * (g_pre is not None))
                if mixed:
                    for j in range(2):
                        act.wait_ge(low_done, 2 * i + j + 1)
                        act.sem_inc(tick, 1)
                        link(act.activation(junk[j].unsqueeze(1), X[:, bass.ds(2 * i + j, 1), :], ACT.Square,
                                            accum_out=sq1[:, j:j + 1]))
                    for j in range(2):
                        act.activation(rt1[:, j:j + 1], sq1[:, j:j + 1], ACT.Sqrt, bias=eps[:, :],
                                       scale=1.0 / D).then_inc(mix_root, 1)
                if g_pre is not None:
                    if not mixed:
                        act.wait_ge(loaded, 16 * i + 16)
                    for j in range(2):
                        if mixed:
                            act.wait_ge(x_updated, 2 * i + j + 1)
                        act.wait_ge(low_done, 2 * i + j + 1)
                        act.sem_inc(tick, 1)
                        link(act.activation(junk[j].unsqueeze(1), X[:, bass.ds(2 * i + j, 1), :], ACT.Square,
                                            accum_out=sq2[:, j:j + 1]))
                    for j in range(2):
                        act.activation(rt2[:, j:j + 1], sq2[:, j:j + 1], ACT.Sqrt, bias=eps[:, :],
                                       scale=1.0 / D).then_inc(x_root, 1)
                    for j in range(2):
                        act.wait_ge(scaled, 2 * i + j + 1)
                        act.sem_inc(tick, 1)
                        act.activation(hT[0][:, :, bass.ds((2 * i + j) * P, P)], h_out[j][:, :, :],
                                       ACT.Copy).then_inc(high_done, 1)
                if g_pre is None:
                    act.wait_ge(x_updated, 2 * i + 2)
                    act.sem_inc(low_done, 2)
                link.done()

        @block.gpsimd
        def _(pool):
            if g_pre is not None:
                with pool.Fori(0, TURNS) as i:
                    for j in range(2):
                        pool.wait_ge(high_done, 2 * i + j + 1)
                        pool.sem_inc(tick, 1)
                        part = (slice(None), slice(None), bass.ds((2 * i + j) * P, P))
                        pool.tensor_tensor(hT[1][part], h_out[j][:, :, :], hT[0][part].bitcast(F32),
                                           ALU.subtract).then_inc(low_done, 1)

        @block.vector
        def _(dve):
            dve.memset(eps[:, :], EPS).then_inc(eps_set, 1)
            dve.wait_ge(gains, n_gains)
            with dve.Fori(0, TURNS) as i:
                link = Chain(dve, dve_chain, i, 4 * mixed + 2 * (g_pre is not None))
                if mixed:
                    for j in range(2):
                        dve.wait_ge(mix_root, 2 * i + j + 1)
                        link(dve.reciprocal(rc1[:, j:j + 1], rt1[:, j:j + 1]))
                        x = X[:, bass.ds(2 * i + j, 1), :]
                        link(dve.scalar_tensor_tensor(x, x, rc1[:, j:j + 1], gpost[:, :].unsqueeze(1),
                                                      ALU.mult, ALU.mult))
                        dve.wait_ge(loaded, 16 * i + 16)
                        dve.tensor_tensor(x, x, x_old[:, j:j + 1, :], ALU.add).then_inc(x_updated, 1)
                if g_pre is not None:
                    for j in range(2):
                        dve.wait_ge(x_root, 2 * i + j + 1)
                        link(dve.reciprocal(rc2[:, j:j + 1], rt2[:, j:j + 1]))
                        dve.tensor_scalar(h[j][:, :].unsqueeze(1), X[:, bass.ds(2 * i + j, 1), :], rc2[:, j:j + 1],
                                          None, ALU.mult).then_inc(h_ready, 1)
                    for j in range(2):
                        dve.wait_ge(turned, 2 * i + j + 1)
                        dve.tensor_tensor(h_out[j][:, :, :], ps[j][:, :, :], bc(gpre[:, :], P),
                                          ALU.mult).then_inc(scaled, 1)
                    dve.wait_ge(scaled, 2 * i + 2)
                link.done()

        @block.tensor
        def _(pe):
            if g_pre is not None:
                with pe.Fori(0, TURNS) as i:
                    for j in range(2):
                        pe.wait_ge(h_ready, 2 * i + j + 1)
                        for k in range(KB):
                            last = pe.transpose(ps[j][:, k, :], h[j][:, k * P:(k + 1) * P], ident[:, :])
                        last.then_inc(turned, 1)


def in_proj_fm(nc, E, hT, w_in, first_col, turns, dst, weights, conv):
    n_taps = TAPS if conv else 3
    reach = n_taps // 2
    n_in = TAPS if conv else 2
    w_raw = [E.sb(f"w_raw{j}", [P, KB, P]) for j in range(3)]
    w = [E.pair(f"w{j}", [P, KB, P]) for j in range(3)]
    padded = [E.sb(f"padded{j}", [P, PADDED]) for j in range(3)]
    mixed = [E.sb(f"mixed{j}", [P, SPAN]) for j in range(3)]
    bank = E.banks(8)
    BANK = (0, 1, 2, 3, 4, 5, 6, 7, 2)
    w_loaded = [E.sem(f"w_loaded{j}") for j in range(3)]
    stored = [E.sem(f"stored{j}") for j in range(3)]
    w_high, w_low, multiplied, copied, taps_done, silu_done, dve_chain, zeroed, taps_loaded, setup_chain = (
        E.sem(n) for n in ("w_high", "w_low", "multiplied", "copied", "taps_done", "silu_done", "dve_chain", "zeroed",
                           "taps_loaded", "setup_chain"))
    tap = E.sb("tap", [P, 3 * turns, n_taps])
    raw_tap = E.sb("raw_tap", [P, 3 * turns, 2])
    wv = w_in.rearrange("(k p) n -> p k n", p=P)
    CREDIT = 3

    with nc.Block() as block:
        @block.sync
        def _(sp):
            for u in range(n_in):
                sp.dma_start((tap if conv else raw_tap)[:, :, u], weights[u].rearrange("(b p) -> p b", p=P),
                             allow_slow_non_contiguous=True).then_inc(taps_loaded, 16)
            for j in range(3):
                sp.dma_start(w_raw[j][:, :, :], wv[:, :, first_col + j * P:first_col + (j + 1) * P]).then_inc(w_loaded[j], 16)

            def store(i, j):
                sp.wait_ge(silu_done if conv else taps_done, 3 * i + j + 1 + (0 if conv else CREDIT))
                blk = dst[bass.ds(i * 3 + j, 1)].rearrange("b p n -> p b n")
                sp.dma_start(blk[:, :, 0:T_PROMPT], mixed[j][:, 0:T_PROMPT].unsqueeze(1)).then_inc(stored[j], 16)
                sp.dma_start(blk[:, :, T_PROMPT:NT], mixed[j][:, T_PROMPT + PAD:SPAN].unsqueeze(1)).then_inc(stored[j], 16)

            with sp.Fori(0, turns - 1) as i:
                for j in range(3):
                    sp.wait_ge(w_low, 3 * i + j + 1)
                    sp.dma_start(w_raw[j][:, :, :], wv[:, :, bass.ds(i * (3 * P) + (first_col + (3 + j) * P), P)]
                                 ).then_inc(w_loaded[j], 16)
                for j in range(3):
                    store(i, j)
            for j in range(3):
                store(turns - 1, j)
            for j in range(3):
                sp.wait_ge(stored[j], 32 * (turns + 1))

        @block.tensor
        def _(pe):
            with pe.Fori(0, turns) as i:
                for j in range(3):
                    pe.wait_ge(w_low, 3 * i + j + 1)
                    for q, (t0, n) in enumerate(PIECES):
                        pe.wait_ge(copied, 9 * i + 3 * j + q + 1)
                        for k in range(KB):
                            last = product(pe, bank[BANK[3 * j + q]][:, 0:n], both(w[j], slice(None), k),
                                           both(hT, slice(None), k, slice(t0, t0 + n)), k == 0, k == KB - 1)
                        last.then_inc(multiplied, 1)

        @block.gpsimd
        def _(pool):
            with pool.Fori(0, turns) as i:
                for j in range(3):
                    pool.wait_ge(w_high, 3 * i + j + 1)
                    pool.tensor_tensor(w[j][1][:, :, :], w_raw[j][:, :, :], w[j][0][:, :, :].bitcast(F32),
                                       ALU.subtract).then_inc(w_low, 1)

        def silu(act, i, j):
            act.wait_ge(taps_done, 3 * i + j + 1 + CREDIT)
            act.activation(mixed[j][:, :], mixed[j][:, :], ACT.Silu).then_inc(silu_done, 1)

        @block.scalar
        def _(act):
            act.wait_ge(zeroed, 3)
            act.sem_inc(copied, CREDIT)

            def high(i, j):
                act.wait_ge(w_loaded[j], 16 * i + 16)
                act.activation(w[j][0][:, :, :], w_raw[j][:, :, :], ACT.Copy).then_inc(w_high, 1)

            def turn(i, more):
                for j in range(3):
                    act.wait_ge(taps_done, 3 * i + j + 1)
                    for q, (t0, n) in enumerate(PIECES):
                        act.wait_ge(multiplied, 9 * i + 3 * j + q + 1)
                        at = PAD + t0 if q < 2 else PAD + t0 + PAD
                        act.activation(padded[j][:, at:at + n], bank[BANK[3 * j + q]][:, 0:n], ACT.Copy).then_inc(copied, 1)
                    if more:
                        high(i + 1, j)
                    if conv and j > 0:
                        silu(act, i, j - 1)
                if conv:
                    silu(act, i, 2)

            for j in range(3):
                high(0, j)
            with act.Fori(0, turns - 1) as i:
                turn(i, True)
            turn(turns - 1, False)

        @block.vector
        def _(dve):
            dve.sem_inc(taps_done, CREDIT)
            for j in range(3):
                dve.memset(padded[j][:, :], 0.0).then_inc(zeroed, 1)
                dve.sem_inc(stored[j], 32)
            dve.wait_ge(zeroed, 3)
            dve.wait_ge(taps_loaded, 16 * n_in)
            if not conv:
                link = Chain(dve, setup_chain)
                link(dve.tensor_tensor(tap[:, :, 1], raw_tap[:, :, 0], raw_tap[:, :, 1], ALU.add))
                link(dve.tensor_scalar(tap[:, :, 1], tap[:, :, 1], -1.0, 1.0, ALU.mult, ALU.add))
                link(dve.tensor_copy(tap[:, :, 0], raw_tap[:, :, 0]))
                link(dve.tensor_copy(tap[:, :, 2], raw_tap[:, :, 1]))
            with dve.Fori(0, turns) as i:
                link = Chain(dve, dve_chain, i, 3 * (n_taps - 1))
                for j in range(3):
                    dve.wait_ge(copied, 9 * i + 3 * j + 3 + CREDIT)
                    dve.wait_ge(stored[j], 32 * i + 32)
                    b = i * 3 + j
                    out = mixed[j][:, :].unsqueeze(1)
                    for u in range(n_taps):
                        src = padded[j][:, PAD - reach + u:PAD - reach + u + SPAN].unsqueeze(1)
                        c = tap[:, bass.ds(b, 1), u]
                        if u == 0:
                            link(dve.tensor_scalar(out, src, c, None, ALU.mult))
                        elif u < n_taps - 1:
                            link(dve.scalar_tensor_tensor(out, src, c, out, ALU.mult, ALU.add))
                        else:
                            dve.scalar_tensor_tensor(out, src, c, out, ALU.mult, ALU.add).then_inc(taps_done, 1)
                link.done()


def in_proj_tm(nc, E, hT, w_in, gates, z_dst):
    n_ab = 4 * GH
    w_raw = E.sb("w_raw", [P, KB, GW + n_ab])
    w = E.pair("w", [P, KB, GW + n_ab])
    z = [E.sb(f"z{j}", [P, GW]) for j in range(2)]
    bank = E.banks(8)
    w_loaded, w_high, w_low, multiplied, silu_done, ab_done = (
        E.sem(n) for n in ("w_loaded", "w_high", "w_low", "multiplied", "silu_done", "ab_done"))
    stored = [E.sem(f"stored{j}") for j in range(2)]
    with nc.Block() as block:
        @block.sync
        def _(sp):
            sp.dma_start(w_raw[:, :, :], w_in.rearrange("(k p) n -> p k n", p=P)[:, :, 3 * GW:GDN_COLS]).then_inc(w_loaded, 16)
            for t in range(TILES):
                sp.wait_ge(silu_done, t + 1)
                sp.dma_start(z_dst[t], z[t % 2][:, :]).then_inc(stored[t % 2], 16)
            for j in range(2):
                sp.wait_ge(stored[j], 16 * (TILES // 2))

        @block.tensor
        def _(pe):
            for t in range(TILES):
                if t >= 4:
                    pe.wait_ge(silu_done, t - 3)
                    pe.wait_ge(ab_done, t - 3)
                for half, (c0, n) in enumerate(((0, GW), (GW, n_ab))):
                    for k in range(KB):
                        if t + half == 0:
                            pe.wait_ge(w_low, k + 1)
                        last = product(pe, bank[2 * (t % 4) + half][:, 0:n], both(hT, slice(None), k, slice(t * P, (t + 1) * P)),
                                       both(w, slice(None), k, slice(c0, c0 + n)), k == 0, k == KB - 1)
                last.then_inc(multiplied, 1)

        @block.scalar
        def _(act):
            act.wait_ge(w_loaded, 16)
            for k in range(KB):
                act.activation(w[0][:, k, :], w_raw[:, k, :], ACT.Copy).then_inc(w_high, 1)
            for t in range(TILES):
                act.wait_ge(multiplied, t + 1)
                if t >= 2:
                    act.wait_ge(stored[t % 2], 16 * (t // 2))
                act.activation(z[t % 2][:, :], bank[2 * (t % 4)][:, :], ACT.Silu).then_inc(silu_done, 1)

        @block.vector
        def _(dve):
            for k in range(KB):
                dve.wait_ge(w_high, k + 1)
                dve.tensor_tensor(w[1][:, k, :], w_raw[:, k, :], w[0][:, k, :].bitcast(F32), ALU.subtract).then_inc(w_low, 1)
            for t in range(TILES):
                dve.wait_ge(multiplied, t + 1)
                dve.tensor_copy(gates[:, t, :], bank[2 * (t % 4) + 1][:, 0:n_ab]).then_inc(ab_done, 1)
            dve.wait_ge(ab_done, TILES)


def feed_forward(nc, E, hT, acc, w1, w2):
    GB = 2
    GROUPS = D_FF // (GB * P)
    NQ = len(PIECES)
    w1_raw = E.sb("w1_raw", [P, KB, GB * P])
    w2_raw = E.sb("w2_raw", [P, GB, D])
    w1_sb = E.pair("w1", [P, KB, GB * P])
    w2_sb = E.pair("w2", [P, GB, D])
    f = E.pair("f", [P, GB, NT])
    relu = [E.sb(f"relu{j}", [P, 512]) for j in range(2)]
    square = [E.sb(f"square{j}", [P, 512]) for j in range(2)]
    bank = E.banks(8)
    w1_loaded, w2_loaded, w1_high, w1_low, w2_high, w2_low, up_product, relu_done, squared, f_high, f_low, down_product, added, zeroed = (
        E.sem(n) for n in ("w1_loaded", "w2_loaded", "w1_high", "w1_low", "w2_high", "w2_low", "up_product", "relu_done",
                           "squared", "f_high", "f_low", "down_product", "added", "zeroed"))
    w1v = w1.rearrange("(k p) n -> p k n", p=P)
    w2v = w2.rearrange("(b p) n -> p b n", p=P)
    UP = GB * NQ
    DOWN = TILES * 2
    UNITS = [(q, b) for q in range(NQ) for b in range(GB)]
    with nc.Block() as block:
        @block.sync
        def _(sp):
            sp.dma_start(w1_raw[:, :, :], w1v[:, :, 0:GB * P]).then_inc(w1_loaded, 16)
            sp.dma_start(w2_raw[:, :, :], w2v[:, 0:GB, :]).then_inc(w2_loaded, 16)
            with sp.Fori(0, GROUPS - 1) as i:
                sp.wait_ge(w1_low, i + 1)
                sp.dma_start(w1_raw[:, :, :], w1v[:, :, bass.ds((i + 1) * (GB * P), GB * P)]).then_inc(w1_loaded, 16)
                sp.wait_ge(w2_low, i + 1)
                sp.dma_start(w2_raw[:, :, :], w2v[:, bass.ds((i + 1) * GB, GB), :]).then_inc(w2_loaded, 16)

        @block.tensor
        def _(pe):
            with pe.Fori(0, GROUPS) as i:
                pe.wait_ge(w1_low, i + 1)
                for u, (q, b) in enumerate(UNITS):
                    t0, n = PIECES[q]
                    pe.wait_ge(relu_done, UP * i + u + 1)
                    for k in range(KB):
                        last = product(pe, bank[u % 4][:, 0:n], both(w1_sb, slice(None), k, slice(b * P, (b + 1) * P)),
                                       both(hT, slice(None), k, slice(t0, t0 + n)), k == 0, k == KB - 1)
                    last.then_inc(up_product, 1)
                pe.wait_ge(w2_low, i + 1)
                for t in range(TILES):
                    if t % 4 == 0:
                        pe.wait_ge(f_low, UP * i + GB * (t // 4 + 1) + 2)
                    for half in range(2):
                        u = 2 * t + half
                        pe.wait_ge(added, DOWN * i + u + 1)
                        for b in range(GB):
                            last = product(pe, bank[4 + u % 4][:, :], both(f, slice(None), b, slice(t * P, (t + 1) * P)),
                                           both(w2_sb, slice(None), b, slice(half * 512, (half + 1) * 512)),
                                           b == 0, b == GB - 1)
                        last.then_inc(down_product, 1)

        @block.scalar
        def _(act):
            act.sem_inc(relu_done, 4)
            act.sem_inc(squared, 2)
            act.sem_inc(f_low, 2)
            act.wait_ge(w1_loaded, 16)
            act.activation(w1_sb[0][:, :, :], w1_raw[:, :, :], ACT.Copy).then_inc(w1_high, 1)

            def group(i, more):
                def high(u):
                    q, b = UNITS[u]
                    t0, n = PIECES[q]
                    act.wait_ge(squared, UP * i + u + 1 + 2)
                    act.activation(f[0][:, b, t0:t0 + n], square[u % 2][:, 0:n], ACT.Copy).then_inc(f_high, 1)

                act.wait_ge(w2_loaded, 16 * i + 16)
                act.wait_ge(added, DOWN * i + 4)
                act.activation(w2_sb[0][:, :, :], w2_raw[:, :, :], ACT.Copy).then_inc(w2_high, 1)
                for u, (q, b) in enumerate(UNITS):
                    n = PIECES[q][1]
                    act.wait_ge(up_product, UP * i + u + 1)
                    act.wait_ge(squared, UP * i + u + 1)
                    act.activation(relu[u % 2][:, 0:n], bank[u % 4][:, 0:n], ACT.Relu).then_inc(relu_done, 1)
                    if u > 0:
                        high(u - 1)
                high(UP - 1)
                if more:
                    act.wait_ge(w1_loaded, 16 * i + 32)
                    act.activation(w1_sb[0][:, :, :], w1_raw[:, :, :], ACT.Copy).then_inc(w1_high, 1)

            with act.Fori(0, GROUPS - 1) as i:
                group(i, True)
            group(GROUPS - 1, False)

        @block.gpsimd
        def _(pool):
            with pool.Fori(0, GROUPS) as i:
                pool.wait_ge(w1_high, i + 1)
                pool.tensor_tensor(w1_sb[1][:, :, :], w1_raw[:, :, :], w1_sb[0][:, :, :].bitcast(F32),
                                   ALU.subtract).then_inc(w1_low, 1)
                pool.wait_ge(w2_high, i + 1)
                pool.tensor_tensor(w2_sb[1][:, :, :], w2_raw[:, :, :], w2_sb[0][:, :, :].bitcast(F32),
                                   ALU.subtract).then_inc(w2_low, 1)

        @block.vector
        def _(dve):
            dve.memset(acc[:, :, :], 0.0).then_inc(zeroed, 1)
            dve.wait_ge(zeroed, 1)
            dve.sem_inc(added, 4)
            with dve.Fori(0, GROUPS) as i:
                def low(u):
                    q, b = UNITS[u]
                    t0, n = PIECES[q]
                    dve.wait_ge(f_high, UP * i + u + 1)
                    dve.tensor_tensor(f[1][:, b, t0:t0 + n], square[u % 2][:, 0:n], f[0][:, b, t0:t0 + n].bitcast(F32),
                                      ALU.subtract).then_inc(f_low, 1)

                for u, (q, b) in enumerate(UNITS):
                    n = PIECES[q][1]
                    dve.wait_ge(relu_done, UP * i + u + 1 + 4)
                    dve.wait_ge(f_low, UP * i + u + 1)
                    dve.tensor_tensor(square[u % 2][:, 0:n], relu[u % 2][:, 0:n], relu[u % 2][:, 0:n],
                                      ALU.mult).then_inc(squared, 1)
                    if u > 0:
                        low(u - 1)
                low(UP - 1)
                for u in range(DOWN):
                    dve.wait_ge(down_product, DOWN * i + u + 1)
                    a = acc[:, u // 2, (u % 2) * 512:(u % 2 + 1) * 512]
                    dve.tensor_tensor(a, a, bank[4 + u % 4][:, :], ALU.add).then_inc(added, 1)
                dve.wait_ge(added, DOWN * i + DOWN + 4)


def gdn_rates(nc, E, ins, gates, rates, eps):
    incl = [E.sb(f"incl{d}", [P, P]) for d in range(2)]
    excl = [E.sb(f"excl{d}", [P, P]) for d in range(2)]
    ones = E.sb("ones", [P, P])
    a_log, dt = E.sb("a_log", [P, 2 * GH]), E.sb("dt", [P, 2 * GH])
    a, b, c = (E.sb(n, [P, TILES, 2 * GH]) for n in ("a", "b", "c"))
    bank = E.banks(8)
    loaded, dve_chain, act_chain, to_act, to_dve, summed = (
        E.sem(n) for n in ("loaded", "dve_chain", "act_chain", "to_act", "to_dve", "summed"))
    n_th = TILES * GH
    with nc.Block() as block:
        @block.sync
        def _(sp):
            for d in range(2):
                sp.dma_start(incl[d][:, :], ins["c_incl"][d]).then_inc(loaded, 16)
                sp.dma_start(excl[d][:, :], ins["c_excl"][d]).then_inc(loaded, 16)
            sp.dma_start(ones[:, :], ins["c_ones"]).then_inc(loaded, 16)
            sp.dma_start(a_log[:, :], ins["gdn_A_log"].rearrange("n d h -> (n d h)").partition_broadcast(P)).then_inc(loaded, 16)
            sp.dma_start(dt[:, :], ins["gdn_dt_bias"].rearrange("n d h -> (n d h)").partition_broadcast(P)).then_inc(loaded, 16)

        @block.vector
        def _(dve):
            link = Chain(dve, dve_chain)
            dve.wait_ge(loaded, 16 * 7)
            link(dve.tensor_tensor(c[:, :, :], gates[:, :, 0:2 * GH], bcm(dt[:, :], TILES), ALU.add))
            link(dve.tensor_scalar(a[:, :, :], c[:, :, :], 0.0, None, ALU.max))
            link(dve.tensor_scalar(b[:, :, :], c[:, :, :], 0.0, None, ALU.min))
            dve.tensor_tensor(b[:, :, :], b[:, :, :], a[:, :, :], ALU.subtract).then_inc(to_act, 1)
            dve.wait_ge(to_dve, 1)
            link(dve.tensor_tensor(a[:, :, :], a[:, :, :], b[:, :, :], ALU.add))
            link(dve.scalar_tensor_tensor(a[:, :, :], a[:, :, :], -1.0, bcm(a_log[:, :], TILES), ALU.mult, ALU.mult))
            for d in range(2):
                dve.tensor_copy(rates["g"][d][:, :, :], a[:, :, d * GH:(d + 1) * GH]).then_inc(to_act, 1)
            dve.wait_ge(to_dve, 2)
            link(dve.reciprocal(c[:, :, :], c[:, :, :]))
            for d in range(2):
                link(dve.tensor_copy(rates["beta"][d][:, :, :], c[:, :, d * GH:(d + 1) * GH]))
                link(dve.tensor_scalar(rates["neg_beta"][d][:, :, :], c[:, :, d * GH:(d + 1) * GH], -1.0, None, ALU.mult))
            for d in range(2):
                dve.wait_ge(summed, 3 * d + 3)
                link(dve.tensor_copy(rates["G"][d][:, :, :], bank[3 * d][:, 0:n_th].rearrange("p (t h) -> p t h", h=GH)))

        @block.scalar
        def _(act):
            link = Chain(act, act_chain)
            act.wait_ge(loaded, 16 * 7)
            link(act.activation(a_log[:, :], a_log[:, :], ACT.Exp))
            act.wait_ge(to_act, 1)
            link(act.activation(b[:, :, :], b[:, :, :], ACT.Exp))
            act.activation(b[:, :, :], b[:, :, :], ACT.Ln, bias=ones[:, 0:1]).then_inc(to_dve, 1)
            act.wait_ge(to_act, 3)
            link(act.activation(c[:, :, :], gates[:, :, 2 * GH:4 * GH], ACT.Exp, scale=-1.0))
            act.activation(c[:, :, :], c[:, :, :], ACT.Identity, bias=ones[:, 0:1]).then_inc(to_dve, 1)
            for d in range(2):
                act.wait_ge(summed, 3 * d + 3)
                act.wait_ge(dve_chain, 11 + d)
                for u, name in enumerate(("exp_G", "exp_rest", "exp_last")):
                    link(act.activation(rates[name][d][:, :, :],
                                        bank[3 * d + u][:, 0:n_th].rearrange("p (t h) -> p t h", h=GH), ACT.Exp))

        @block.tensor
        def _(pe):
            for d in range(2):
                pe.wait_ge(to_act, 2 + d)
                g = rates["g"][d][:, :, :].rearrange("p t h -> p (t h)")
                for u, sums in enumerate((incl[d], excl[1 - d], ones)):
                    pe.matmul(bank[3 * d + u][:, 0:n_th], sums[:, :], g, start=True, stop=True).then_inc(summed, 1)


def prepare_tokens(nc, E, ins, ident, eps, conv_fm, shift_fm, fm_both, fm_dir, tm_both, tm_dir):
    qkv = E.sb("qkv", [P, CONV_BLOCKS, P])
    rk = E.sb("rk", [P, RWKV_BLOCKS, P])
    squares = E.sb("squares", [P, 3 * GH, P])
    root = E.sb("root", [P, 3, GW])
    fb = E.sb("fb", [P, 3, GH, P])
    fd = [E.sb(f"fd{d}", [P, 2, RB, P]) for d in range(2)]
    tb = E.sb("tb", [P, 5, GW])
    td = [E.sb(f"td{d}", [P, RW]) for d in range(2)]
    a = [E.sb(f"a{d}", [P, RB, P]) for d in range(2)]
    mixk = [E.sb(f"mixk{d}", [P, RB, P]) for d in range(2)]
    kkr = E.sb("kkr", [P, RB, P])
    rksum = E.sb("rksum", [P, RB, P])
    th, sg = E.sb("th", [P, P]), E.sb("sg", [P, P])
    bsum = E.sb("bsum", [P, RH])
    ones, head_ones, head_cols = E.sb("ones", [P, P]), E.sb("head_ones", [P, P]), E.sb("head_cols", [P, 2])
    w2, a2, g2 = (E.sb(n, [P, RW]) for n in ("w2", "a2", "g2"))
    w0 = E.sb("w0", [1, 2 * RW])
    a0 = [E.sb(f"a0_{d}", [P, RB]) for d in range(2)]
    k_k, k_a, r_k, one_ka = (E.sb(n, [P, RB]) for n in ("k_k", "k_a", "r_k", "one_ka"))
    bank = E.banks(8)
    names = ("params", "loaded", "turned", "kk_raw", "squared", "sums", "rooted", "low_in", "a_product", "a_biased",
             "a_done", "k_normal", "bonus_in", "gate_product", "w_product", "w_done", "bonus_product", "k_turned",
             "dve_chain", "act_chain", "pool_chain", "setup_chain", "dve_out", "stored", "all_done", "act_out")
    s = {n: E.sem(n) for n in names}
    fb_names = []
    PARAMS = 14

    def fm_vec(v):
        return v.rearrange("(b p) -> p b", p=P)

    with nc.Block() as block:
        @block.sync
        def _(sp):
            for dst, src in ((ones, ins["c_ones"]), (head_ones, ins["c_head_ones"]), (head_cols, ins["c_head_cols"]),
                             (w2, ins["rwkv_w2"][0].rearrange("d l c -> (d l) c")),
                             (a2, ins["rwkv_a2"][0].rearrange("d l c -> (d l) c")), (g2, ins["rwkv_g2"][0]),
                             (w0, ins["rwkv_w0"].rearrange("n d c -> n (d c)"))):
                sp.dma_start(dst[:, :], src).then_inc(s["params"], 16)
            for dst, src in ((a0[0], ins["rwkv_a0"][0][0]), (a0[1], ins["rwkv_a0"][0][1]), (k_k, ins["rwkv_k_k"][0]),
                             (k_a, ins["rwkv_k_a"][0]), (r_k, ins["rwkv_r_k"][0].rearrange("h n -> (h n)"))):
                sp.dma_start(dst[:, :], fm_vec(src), allow_slow_non_contiguous=True).then_inc(s["params"], 16)

            def load(t):
                sp.dma_start(qkv[:, :, :], conv_fm.rearrange("b p n -> p b n")[:, :, bass.ds(t * P, P)]).then_inc(s["loaded"], 16)
                sp.dma_start(rk[:, :, :], shift_fm.rearrange("b p n -> p b n")[:, :, bass.ds(t * P, P)]).then_inc(s["loaded"], 16)

            def store(t):
                sp.wait_ge(s["dve_out"], t + 1)
                sp.wait_ge(s["act_out"], t + 1)
                sp.dma_start(fm_both[bass.ds(t, 1)].rearrange("o p n -> p o n"),
                             fb[:, :, :, :].rearrange("p a b n -> p (a b n)").unsqueeze(1)).then_inc(s["stored"], 16)
                sp.dma_start(tm_both[bass.ds(t, 1)].rearrange("o p n -> p o n"),
                             tb[:, :, :].rearrange("p a n -> p (a n)").unsqueeze(1)).then_inc(s["stored"], 16)
                for d in range(2):
                    sp.dma_start(fm_dir[d][bass.ds(t, 1)].rearrange("o p n -> p o n"),
                                 fd[d][:, :, :, :].rearrange("p a b n -> p (a b n)").unsqueeze(1)).then_inc(s["stored"], 16)
                    sp.dma_start(tm_dir[d][bass.ds(t, 1)].rearrange("o p n -> p o n"),
                                 td[d][:, :].unsqueeze(1)).then_inc(s["stored"], 16)

            load(0)
            with sp.Fori(0, TILES - 1) as t:
                store(t)
                load(t + 1)
                sp.wait_ge(s["stored"], 96 * t + 96)
                sp.sem_inc(s["all_done"], 1)
            store(TILES - 1)
            sp.wait_ge(s["stored"], 96 * TILES)

        @block.tensor
        def _(pe):
            pe.wait_ge(s["params"], 16 * 12)
            with pe.Fori(0, TILES) as t:
                pe.wait_ge(s["loaded"], 32 * t + 32)
                for k in range(GH):
                    pe.transpose(bank[0][:, k * P:(k + 1) * P], qkv[:, 2 * GH + k, :], ident[:, :])
                for k in range(RB):
                    last = pe.transpose(bank[1][:, k * P:(k + 1) * P], rk[:, 2 * RB + k, :], ident[:, :])
                last.then_inc(s["turned"], 1)
                for d in range(2):
                    for k in range(RB):
                        last = pe.matmul(bank[5 + d][:, k * P:(k + 1) * P], a2[64 * d:64 * d + 64, k * P:(k + 1) * P],
                                         rk[64 * d:64 * d + 64, 13, :], start=True, stop=True)
                last.then_inc(s["a_product"], 1)
                pe.wait_ge(s["squared"], t + 1)
                for u in range(2):
                    pe.matmul(bank[2 + u][:, :], ones[:, :], squares[:, u * GH:(u + 1) * GH, :], start=True, stop=True)
                pe.matmul(bank[4][:, :], head_ones[:, :], squares[:, 2 * GH:3 * GH, :], start=True,
                          stop=True).then_inc(s["sums"], 1)
                pe.wait_ge(s["low_in"], t + 1)
                pe.matmul(bank[7][:, :], sg[:, :], g2[:, :], start=True, stop=True).then_inc(s["gate_product"], 1)
                pe.wait_ge(s["k_normal"], t + 1)
                for d in range(2):
                    pe.matmul(bank[d][:, :], th[64 * d:64 * d + 64, :], w2[64 * d:64 * d + 64, :], start=True, stop=False)
                    last = pe.matmul(bank[d][:, :], ones[0:1, :], w0[0:1, d * RW:(d + 1) * RW], start=False, stop=True)
                last.then_inc(s["w_product"], 1)
                for k in range(GH):
                    last = pe.transpose(bank[2][:, k * P:(k + 1) * P], fb[:, 0, k, :], ident[:, :])
                last.then_inc(s["k_turned"], 1)
                pe.wait_ge(s["bonus_in"], t + 1)
                for k in range(RB):
                    last = pe.matmul(bank[3][:, 2 * k:2 * k + 2], rksum[:, k, :], head_cols[:, :], start=True, stop=True)
                last.then_inc(s["bonus_product"], 1)

        @block.scalar
        def _(act):
            act.wait_ge(s["setup_chain"], 3)
            with act.Fori(0, TILES) as t:
                link = Chain(act, s["act_chain"], t, 4)
                act.wait_ge(s["loaded"], 32 * t + 32)
                act.wait_ge(s["all_done"], t + 1)
                link(act.activation(squares[:, 0:2 * GH, :], qkv[:, 0:2 * GH, :], ACT.Square))
                act.wait_ge(s["kk_raw"], t + 1)
                act.activation(squares[:, 2 * GH:3 * GH, :], kkr[:, :, :], ACT.Square).then_inc(s["squared"], 1)
                link(act.activation(th[:, :], rk[:, 12, :], ACT.Tanh))
                act.activation(sg[:, :], rk[:, 14, :], ACT.Sigmoid).then_inc(s["low_in"], 1)
                for d in range(2):
                    act.wait_ge(s["a_biased"], 2 * t + d + 1)
                    act.activation(a[d][:, :, :], a[d][:, :, :], ACT.Sigmoid).then_inc(s["a_done"], 1)
                act.wait_ge(s["gate_product"], t + 1)
                link(act.activation(tb[:, 3, :], bank[7][:, :], ACT.Copy))
                act.wait_ge(s["sums"], t + 1)
                for u in range(3):
                    act.activation(root[:, u, :], bank[2 + u][:, :], ACT.Sqrt, bias=eps[:, :]).then_inc(s["rooted"], 1)
                act.wait_ge(s["w_product"], t + 1)
                for d in range(2):
                    act.activation(td[d][:, :], bank[d][:, :], ACT.Sigmoid).then_inc(s["w_done"], 1)
                act.wait_ge(s["k_turned"], t + 1)
                link(act.activation(tb[:, 0, :], bank[2][:, :], ACT.Copy))
                act.wait_ge(s["w_done"], 2 * t + 2)
                act.sem_inc(s["act_out"], 1)
                link.done()

        @block.vector
        def _(dve):
            dve.memset(eps[:, :], EPS).then_inc(s["setup_chain"], 1)
            dve.wait_ge(s["params"], 16 * 12)
            dve.tensor_scalar(one_ka[:, :], k_a[:, :], -1.0, 1.0, ALU.mult, ALU.add).then_inc(s["setup_chain"], 1)
            dve.wait_ge(s["setup_chain"], 2)
            dve.sem_inc(s["setup_chain"], 1)
            dve.sem_inc(s["all_done"], 1)
            r, k, v = rk[:, 0:RB, :], rk[:, RB:2 * RB, :], None
            with dve.Fori(0, TILES) as t:
                link = Chain(dve, s["dve_chain"], t, 18)
                dve.wait_ge(s["loaded"], 32 * t + 32)
                dve.wait_ge(s["all_done"], t + 1)
                dve.tensor_tensor(kkr[:, :, :], k, bc(k_k[:, :], P), ALU.mult).then_inc(s["kk_raw"], 1)
                dve.wait_ge(s["turned"], t + 1)
                link(dve.tensor_copy(tb[:, 1, :], bank[0][:, :]))
                link(dve.tensor_copy(tb[:, 2, :], bank[1][:, :]))
                for d in range(2):
                    dve.wait_ge(s["a_product"], t + 1)
                    dve.tensor_tensor(a[d][:, :, :], bank[5 + d][:, :].rearrange("p (b n) -> p b n", b=RB),
                                      bc(a0[d][:, :], P), ALU.add).then_inc(s["a_biased"], 1)
                dve.wait_ge(s["rooted"], 3 * t + 3)
                link(dve.reciprocal(root[:, :, :], root[:, :, :]))
                rt = [root[:, u, :].rearrange("p (b n) -> p b n", b=RB) for u in range(3)]
                link(dve.scalar_tensor_tensor(fb[:, 1, :, :], qkv[:, 0:GH, :], GD ** -0.5, rt[0], ALU.mult, ALU.mult))
                dve.tensor_tensor(fb[:, 0, :, :], qkv[:, GH:2 * GH, :], rt[1], ALU.mult).then_inc(s["k_normal"], 1)
                link(dve.tensor_tensor(fb[:, 2, :, :], kkr[:, :, :], rt[2], ALU.mult))
                for d in range(2):
                    dve.wait_ge(s["a_done"], 2 * t + d + 1)
                    m = mixk[d][:, :, :]
                    link(dve.tensor_tensor(m, a[d][:, :, :], bc(k_a[:, :], P), ALU.mult))
                    link(dve.tensor_tensor(m, m, bc(one_ka[:, :], P), ALU.add))
                    link(dve.tensor_tensor(fd[d][:, 1, :, :], k, m, ALU.mult))
                    link(dve.tensor_tensor(fd[d][:, 0, :, :], fb[:, 2, :, :], a[d][:, :, :], ALU.mult))
                link(dve.tensor_tensor(rksum[:, :, :], fd[0][:, 1, :, :], fd[1][:, 1, :, :], ALU.add))
                link(dve.tensor_tensor(rksum[:, :, :], rksum[:, :, :], r, ALU.mult))
                dve.tensor_tensor(rksum[:, :, :], rksum[:, :, :], bc(r_k[:, :], P), ALU.mult).then_inc(s["bonus_in"], 1)
                dve.wait_ge(s["bonus_product"], t + 1)
                link(dve.tensor_copy(bsum[:, :], bank[3][:, 0:RH]))
                link(dve.tensor_tensor(tb[:, 4, :].rearrange("p (h n) -> p h n", h=RH),
                                       tb[:, 2, :].rearrange("p (h n) -> p h n", h=RH), bc(bsum[:, :], RN), ALU.mult))
                link(dve.tensor_copy(bsum[:, 0:1], bsum[:, 0:1]))
                dve.wait_ge(s["kk_raw"], t + 1)
                dve.sem_inc(s["dve_out"], 1)
                link.done()


def mix_scopes(nc, phase, dram, ins, acc, gates, ident, conv_fm, shift_fm, z_tm, stop):
    fm_both = dram("fm_both", [TILES, P, 3 * GW])
    fm_dir = [dram(f"fm_dir{d}", [TILES, P, 2 * RW]) for d in range(2)]
    tm_both = dram("tm_both", [TILES, P, 5 * GW])
    tm_dir = [dram(f"tm_dir{d}", [TILES, P, RW]) for d in range(2)]
    with ExitStack() as own:
        def sb(name, shape):
            return own.enter_context(nc.sbuf_tensor(name, shape, F32))
        eps = sb("eps", [P, 1])
        rates = {n: [sb(f"rate_{n}{d}", [P, TILES, GH]) for d in range(2)]
                 for n in ("g", "beta", "neg_beta", "G", "exp_G", "exp_rest", "exp_last")}
        phase("prepare", prepare_tokens, ins, ident, eps, conv_fm, shift_fm, fm_both, fm_dir, tm_both, tm_dir)
        phase("rates", gdn_rates, ins, gates, rates, eps)
        if stop > 2:
            phase("scan", recurrences, ins, ident, rates, shift_fm, fm_both, fm_dir, tm_both, tm_dir, acc)
        if stop > 3:
            phase("gate", gate_outputs, ins, acc, z_tm, tm_both)
            if stop > 4:
                phase("out0", project_out, ident, acc, ins["w_out_even"][0])


def recurrences(nc, E, ins, ident, rates, shift_fm, fm_both, fm_dir, tm_both, tm_dir, out):
    G, GR = 6, 4
    direction = [0, 1, 0, 0, 1, 1]
    width = [P, P, RN, RN, RN, RN]
    NT_ = [E.sb(f"NT{g}", [P, GR, P]) for g in range(G)]
    X = [E.sb(f"X{g}", [P, GR, P]) for g in range(G)]
    XT = [E.sb(f"XT{g}", [P, GR, P]) for g in range(G)]
    NM = [E.sb(f"NM{g}", [P, GR, P]) for g in range(2)]
    Y = [E.sb(f"Y{g}", [P, GR, P]) for g in range(2)]
    A_o = [E.sb(f"A_o{g}", [P, GR, P]) for g in range(G)]
    A_v = [None, None] + [E.sb(f"A_v{g}", [P, GR, P]) for g in range(2, G)]
    A_ov = [None, None] + [E.sb(f"A_ov{g}", [P, GR, P]) for g in range(2, G)]
    fb = [E.sb(f"fb{d}", [P, 3, GH, P]) for d in range(2)]
    rr = [E.sb(f"r{d}", [P, RB, P]) for d in range(2)]
    fd = [E.sb(f"fd{d}", [P, 2, RB, P]) for d in range(2)]
    tb = [E.sb(f"tb{d}", [P, 3, GW]) for d in range(2)]
    td = [E.sb(f"td{d}", [P, RW]) for d in range(2)]
    AR = [E.sb(f"AR{d}", [P, RB, 2, P]) for d in range(2)]
    BK = [E.sb(f"BK{d}", [P, 2, RW]) for d in range(2)]
    ends = [E.sb(f"ends{d}", [P, RB, 2]) for d in range(2)]
    S_g = [E.sb(f"S_g{d}", [P, GH, P]) for d in range(2)]
    S_r = [E.sb(f"S_r{d}", [P, RB, 2, RN]) for d in range(2)]
    rest = [E.sb(f"rest{d}", [P, RB, 2]) for d in range(2)]
    head_cols = E.sb("head_cols", [P, 2])
    e_inc, e_exc, e_neg = (E.sb(n, [P, RB, P]) for n in ("e_inc", "e_exc", "e_neg"))
    grow, decay = E.sb("grow", [P, GH, P]), E.sb("decay", [P, GH, P])
    BT, KT = Y, NM
    KD = [e_inc, e_exc]
    R = [NT_[g][:, :, 0:width[g]] for g in range(G)]
    U = [X[g][:, :, 0:width[g]] for g in range(G)]
    incl = [E.sb(f"incl{d}", [P, P]) for d in range(2)]
    excl = [E.sb(f"excl{d}", [P, P]) for d in range(2)]
    outside = [E.sb(f"outside{d}", [P, P]) for d in range(2)]
    sums = [E.sb(f"sums{d}", [P, 2 * P]) for d in range(2)]
    end_sums = [E.sb(f"end_sums{d}", [P, 2]) for d in range(2)]
    keep = [E.sb(f"keep{d}", [P, TILES]) for d in range(2)]
    levels = [E.sb(f"levels{d}", [P, LEVELS, P]) for d in range(2)]
    ones = E.sb("ones", [P, P])
    ps = E.stack.enter_context(nc.psum_tensor(f"{E.tag}_ps", [P, 8, 512], F32))
    ML = LEVELS - 1
    YC, XC = 2, 6
    PER_DVE = 53

    names = ("consts", "cleared", "g_rows", "g_sums", "g_shift", "g_decay", "gram", "gram_used", "w_sums", "w_exp",
             "w_used", "turned", "turned_out", "pairs", "pairs_used", "x_first", "masked", "x_turned", "x_out",
             "y_product", "y_out", "z_product", "x_done", "state_scaled", "right", "right_g", "right_r", "solved",
             "u_g", "u_r", "outs", "outs_used", "g_state", "turn_done", "kdec", "dve_chain", "pool_chain", "act_chain",
             "pool_tick")
    s = {n: E.sem(n) for n in names}
    early = [E.sem(f"early{d}") for d in range(2)]
    late = [E.sem(f"late{d}") for d in range(2)]

    def head_of(half, slot):
        return 4 * half + 2 * (slot % 2) + slot // 2

    def tile(d, i):
        return i if d == 0 else i * -1 + (TILES - 1)

    def heads(ap, n=P):
        return ap.rearrange("p (h n) -> p h n", n=n)

    def pairs_view(b):
        return ps[:, b:b + 2, :].rearrange("p b (h a n) -> p (b h) a n", h=2, a=2)

    def pair_slots(g, pair):
        return ps[:, g, 0:4 * RN].rearrange("p (a b n) -> p b a n", a=2, n=RN)[:, pair, :, :]

    def rate(name, d, t):
        return bc(rates[name][d][:, bass.ds(t, 1), :].rearrange("p o h -> p (o h)"), P)

    with nc.Block() as block:
        @block.sync
        def _(sp):
            for dst, name in ((incl, "c_incl"), (excl, "c_excl"), (outside, "c_outside"), (sums, "c_decay_sums"),
                              (end_sums, "c_decay_ends"), (keep, "c_keep")):
                for d in range(2):
                    sp.dma_start(dst[d][:, :], ins[name][d]).then_inc(s["consts"], 16)
            for d in range(2):
                sp.dma_start(levels[d][:, :, :], ins["c_levels"][d].rearrange("m s t -> s m t")).then_inc(s["consts"], 16)
            sp.dma_start(ones[:, :], ins["c_ones"]).then_inc(s["consts"], 16)
            sp.dma_start(head_cols[:, :], ins["c_head_cols"]).then_inc(s["consts"], 16)

            def load_early(d, i):
                t = tile(d, i)
                sp.dma_start(rr[d][:, :, :], shift_fm.rearrange("b p n -> p b n")[:, 0:RB, bass.ds(t * P, P)]).then_inc(early[d], 16)
                sp.dma_start(fd[d][:, :, :, :].rearrange("p a b n -> p (a b n)").unsqueeze(1),
                             fm_dir[d][bass.ds(t, 1)].rearrange("o p n -> p o n")).then_inc(early[d], 16)
                sp.dma_start(td[d][:, :].unsqueeze(1), tm_dir[d][bass.ds(t, 1)].rearrange("o p n -> p o n")).then_inc(early[d], 16)

            def load_late(d, i):
                t = tile(d, i)
                sp.dma_start(fb[d][:, :, :, :].rearrange("p a b n -> p (a b n)").unsqueeze(1),
                             fm_both[bass.ds(t, 1)].rearrange("o p n -> p o n")).then_inc(late[d], 16)
                sp.dma_start(tb[d][:, :, :].rearrange("p a n -> p (a n)").unsqueeze(1),
                             tm_both[bass.ds(t, 1)].rearrange("o p n -> p o n")[:, :, 0:3 * GW]).then_inc(late[d], 16)

            for d in range(2):
                load_late(d, 0)
                load_early(d, 0)
            with sp.Fori(0, TILES - 1) as i:
                for d in range(2):
                    sp.wait_ge(s["w_used"], 2 * i + d + 1)
                    load_early(d, i + 1)
                sp.wait_ge(s["kdec"], 2 * i + 2)
                sp.wait_ge(s["outs"], G * i + G)
                for d in range(2):
                    load_late(d, i + 1)

        @block.tensor
        def _(pe):
            pe.wait_ge(s["consts"], 16 * 16)
            with pe.Fori(0, TILES) as i:
                pe.wait_ge(s["turn_done"], i + 1)
                for d in range(2):
                    pe.wait_ge(s["g_rows"], 2 * i + d + 1)
                    if d == 1:
                        pe.wait_ge(s["g_shift"], 2 * i + 1)
                    pe.matmul(ps[:, 0, :], ones[:, :], grow[:, :, :], start=True, stop=True).then_inc(s["g_sums"], 1)
                    pe.wait_ge(late[d], 32 * i + 32)
                    for h in range(GH):
                        last = pe.matmul(ps[:, 1 + 2 * d + h // 2, (h % 2) * 256:(h % 2) * 256 + 256], fb[d][:, 0, h, :],
                                         fb[d][:, 0:2, h, :], start=True, stop=True)
                    last.then_inc(s["gram"], 1)
                for d in range(2):
                    pe.wait_ge(early[d], 48 * i + 48)
                    if d == 1:
                        pe.wait_ge(s["w_exp"], 2 * i + 1)
                    for k in range(RB):
                        pe.matmul(ps[:, 5 + k // 2, (k % 2) * 256:(k % 2) * 256 + 256], td[d][:, k * P:(k + 1) * P],
                                  sums[d][:, :], start=True, stop=True)
                    for k in range(RB):
                        last = pe.matmul(ps[:, 7, 2 * k:2 * k + 2], td[d][:, k * P:(k + 1) * P], end_sums[d][:, :],
                                         start=True, stop=True)
                    last.then_inc(s["w_sums"], 1)
                for d in range(2):
                    pe.wait_ge(s["w_used"], 2 * i + d + 1)
                    if d == 0:
                        pe.wait_ge(s["w_exp"], 2 * i + 2)
                        pe.wait_ge(s["gram_used"], 2 * i + 2)
                    else:
                        pe.wait_ge(s["turned_out"], 4 * i + 2)
                    for u, src in enumerate((BT[d], KT[d])):
                        for k in range(RB):
                            last = pe.transpose(ps[:, 5 + u, k * P:(k + 1) * P], src[:, k, :], ident[:, :])
                        last.then_inc(s["turned"], 1)
                    for half in range(2):
                        if d + half > 0:
                            pe.wait_ge(s["pairs_used"], 4 * i + 2 * d + half)
                        for u, src in enumerate((BT[d], KT[d])):
                            for h in range(GR):
                                head = head_of(half, h)
                                base = RN * (head % 2)
                                last = pe.matmul(ps[:, 1 + 2 * u + h // 2, (h % 2) * 256:(h % 2) * 256 + 256],
                                                 src[base:base + RN, head // 2, :], AR[d][base:base + RN, head // 2, :, :],
                                                 start=True, stop=True)
                        last.then_inc(s["pairs"], 1)
                with pe.Fori(0, ML) as m:
                    it = (i * ML + m) * G

                    def turn_x(g):
                        if g == 0:
                            pe.wait_ge(s["pairs_used"], 4 * i + 4)
                            pe.wait_ge(s["turned_out"], 4 * i + 4)
                        pe.wait_ge(s["x_first"], G * i + g + 1)
                        pe.wait_ge(s["x_done"], it + g + 1)
                        for h in range(GR):
                            last = pe.transpose(ps[:, g % 2, h * P:(h + 1) * P], XT[g][:, h, :], ident[:, :])
                        last.then_inc(s["x_turned"], 1)

                    def y(g):
                        pe.wait_ge(s["masked"], it + g + 1)
                        pe.wait_ge(s["x_out"], it + g + 1)
                        for h in range(GR):
                            last = pe.matmul(ps[:, 2 + g % 2, h * P:(h + 1) * P], NM[g % 2][:, h, :], X[g][:, h, :],
                                             start=True, stop=True)
                        last.then_inc(s["y_product"], 1)

                    def z(g):
                        pe.wait_ge(s["y_out"], it + g + 1)
                        pe.wait_ge(s["x_done"], it + g - 1 + XC)
                        for h in range(GR):
                            last = pe.matmul(ps[:, 4 + g % 2, h * P:(h + 1) * P], Y[g % 2][:, h, :], XT[g][:, h, :],
                                             start=True, stop=True)
                        last.then_inc(s["z_product"], 1)

                    for step in range(G):
                        turn_x(step)
                        if step >= 1:
                            y(step - 1)
                        if step >= 2:
                            z(step - 2)
                    y(G - 1)
                    z(G - 2)
                    z(G - 1)
                pe.wait_ge(s["x_done"], (i * ML + ML) * G + XC)
                pe.wait_ge(s["state_scaled"], i + 1)
                for g in range(G):
                    d, half = direction[g], g % 2
                    if g < 2:
                        for h in range(GR):
                            last = pe.matmul(ps[:, g, h * P:(h + 1) * P], fb[d][:, 0, h, :], S_g[d][:, h, :],
                                             start=True, stop=True)
                    else:
                        for pair in range(2):
                            pe.matmul(pair_slots(g, pair), AR[d][:, 2 * half + pair, 0, :], S_r[d][:, 2 * half + pair, :, :],
                                      start=True, stop=False)
                            for h in (pair, 2 + pair):
                                head = head_of(half, h)
                                last = pe.matmul(ps[:, g, h * RN:(h + 1) * RN], A_v[g][:, h, :],
                                                 tb[d][:, 2, head * RN:(head + 1) * RN], start=False, stop=(h == 2 + pair))
                    last.then_inc(s["right"], 1)
                for g in range(G):
                    if g < 2:
                        pe.wait_ge(s["right_g"], 2 * i + g + 1)
                    else:
                        pe.wait_ge(s["right_r"], 4 * i + g - 1)
                    n = width[g]
                    for h in range(GR):
                        last = pe.matmul(ps[:, g, h * n:(h + 1) * n], XT[g][:, h, :], R[g][:, h, :], start=True, stop=True)
                    last.then_inc(s["solved"], 1)
                for g in range(G):
                    d, half = direction[g], g % 2
                    if g < 2:
                        pe.wait_ge(s["u_g"], 2 * i + g + 1)
                        for h in range(GR):
                            pe.matmul(ps[:, g, h * P:(h + 1) * P], fb[d][:, 1, h, :], S_g[d][:, h, :], start=True, stop=True)
                        for h in range(GR):
                            last = pe.matmul(ps[:, 6 + g, h * P:(h + 1) * P], A_o[g][:, h, :], U[g][:, h, :],
                                             start=True, stop=True)
                        last.then_inc(s["outs"], 1)
                        continue
                    pe.wait_ge(s["u_r"], 4 * i + g - 1)
                    for pair in range(2):
                        pe.matmul(pair_slots(g, pair), AR[d][:, 2 * half + pair, 1, :], S_r[d][:, 2 * half + pair, :, :],
                                  start=True, stop=False)
                        for h in (pair, 2 + pair):
                            head = head_of(half, h)
                            o = ps[:, g, h * RN:(h + 1) * RN]
                            pe.matmul(o, A_o[g][:, h, :], U[g][:, h, :], start=False, stop=False)
                            pe.matmul(o, A_ov[g][:, h, :], tb[d][:, 2, head * RN:(head + 1) * RN], start=False,
                                      stop=(h == 2 + pair))
                    for pair in range(2):
                        k = 2 * half + pair
                        o = ps[:, g, 256 + pair * P:256 + (pair + 1) * P].rearrange("p (a n) -> p a n", a=2)
                        pe.matmul(o, BK[d][:, 0, k * P:(k + 1) * P], U[g].rearrange("p (a b) n -> p b a n", a=2)[:, pair, :, :],
                                  start=True, stop=False)
                        last = pe.matmul(o, BK[d][:, 1, k * P:(k + 1) * P],
                                         tb[d][:, 2, k * P:(k + 1) * P].rearrange("p (a n) -> p a n", a=2),
                                         start=False, stop=True)
                    last.then_inc(s["outs"], 1)
                pe.wait_ge(s["kdec"], 2 * i + 2)
                for d in range(2):
                    pe.wait_ge(s["outs_used"], G * i + d + 1)
                    for h in range(GR):
                        last = pe.matmul(ps[:, 6 + d, h * P:(h + 1) * P], KD[d][:, h, :], U[d][:, h, :],
                                         start=True, stop=True)
                    last.then_inc(s["g_state"], 1)

        @block.scalar
        def _(act):
            with act.Fori(0, TILES) as i:
                for d in range(2):
                    act.wait_ge(s["g_shift"], 2 * i + d + 1)
                    act.activation(decay[:, :, :], decay[:, :, :], ACT.Exp).then_inc(s["g_decay"], 1)
                for d in range(2):
                    act.wait_ge(s["w_sums"], 2 * i + d + 1)
                    if d == 1:
                        act.wait_ge(s["w_used"], 2 * i + 1)
                    act.activation(ends[d][:, :, :], ps[:, 7, 0:2 * RB].rearrange("p (b n) -> p b n", n=2),
                                   ACT.Exp).then_inc(s["act_chain"], 1)
                    v = pairs_view(5)
                    act.activation(e_exc[:, :, :], v[:, :, 1, :], ACT.Exp).then_inc(s["act_chain"], 1)
                    act.activation(e_inc[:, :, :], v[:, :, 0, :], ACT.Exp).then_inc(s["act_chain"], 1)
                    act.wait_ge(s["act_chain"], 6 * i + 3 * d + 3)
                    act.activation(e_neg[:, :, :], v[:, :, 0, :], ACT.Exp, scale=-1.0).then_inc(s["w_exp"], 1)
                for d in range(2):
                    for u in range(2):
                        act.wait_ge(s["turned"], 4 * i + 2 * d + u + 1)
                        act.activation(BK[d][:, u, :], ps[:, 5 + u, :], ACT.Copy).then_inc(s["turned_out"], 1)
                with act.Fori(0, ML) as m:
                    it = (i * ML + m) * G

                    def x_copy(g):
                        act.wait_ge(s["x_turned"], it + g + 1)
                        act.activation(X[g][:, :, :], heads(ps[:, g % 2, :]), ACT.Copy).then_inc(s["x_out"], 1)

                    def y_copy(g):
                        act.wait_ge(s["y_product"], it + g + 1 + YC)
                        act.activation(Y[g % 2][:, :, :], heads(ps[:, 2 + g % 2, :]), ACT.Copy).then_inc(s["y_out"], 1)

                    for step in range(G):
                        x_copy(step)
                        if step >= 1:
                            y_copy(step - 1)
                    y_copy(G - 1)
                for g in range(2, G):
                    act.wait_ge(s["right"], G * i + g + 1)
                    act.activation(R[g], heads(ps[:, g, 0:4 * RN], RN), ACT.Copy).then_inc(s["right_r"], 1)
                for g in range(2, G):
                    act.wait_ge(s["solved"], G * i + g + 1)
                    act.activation(U[g], heads(ps[:, g, 0:4 * RN], RN), ACT.Copy).then_inc(s["u_r"], 1)

        @block.gpsimd
        def _(pool):
            for d in range(2):
                pool.memset(S_g[d][:, :, :], 0.0).then_inc(s["cleared"], 1)
                pool.memset(S_r[d][:, :, :, :], 0.0).then_inc(s["cleared"], 1)
            pool.memset(out[:, :, :], 0.0).then_inc(s["cleared"], 1)
            pool.wait_ge(s["consts"], 16 * 16)
            with pool.Fori(0, TILES) as i:
                for d in range(2):
                    if d == 1:
                        pool.wait_ge(s["g_sums"], 2 * i + 1)
                    pool.sem_inc(s["pool_tick"], 1)
                    pool.tensor_tensor(grow[:, :, :], bcm(incl[d][:, :], GH), rate("g", d, tile(d, i)),
                                       ALU.mult).then_inc(s["g_rows"], 1)

                def x_first(g):
                    pool.tensor_tensor(XT[g][:, :, :], NT_[g][:, :, :], bcm(levels[direction[g]][:, 0, :], GR),
                                       ALU.mult).then_inc(s["pool_chain"], 1)
                    pool.wait_ge(s["pool_chain"], G * i + g + 1)
                    pool.tensor_tensor(XT[g][:, :, :], XT[g][:, :, :], bcm(ident[:, :], GR), ALU.add).then_inc(s["x_first"], 1)

                for g in range(2):
                    pool.wait_ge(s["gram_used"], 2 * i + g + 1)
                    x_first(g)
                pool.wait_ge(s["w_used"], 2 * i + 2)
                for d in range(2):
                    pool.wait_ge(late[d], 32 * i + 32)
                    pool.sem_inc(s["pool_tick"], 1)
                    pool.tensor_tensor(KD[d][:, :, :], heads(tb[d][:, 0, :]), rate("exp_rest", d, tile(d, i)),
                                       ALU.mult).then_inc(s["kdec"], 1)
                for g in range(2, G):
                    pool.wait_ge(s["pairs_used"], 4 * i + g - 1)
                    x_first(g)
                with pool.Fori(0, ML) as m:
                    it = (i * ML + m) * G
                    for g in range(G):
                        pool.wait_ge(s["y_product"], it + g + 1)
                        pool.sem_inc(s["pool_tick"], 1)
                        d = direction[g]
                        pool.tensor_tensor(NM[g % 2][:, :, :], NT_[g][:, :, :],
                                           levels[d][:, bass.ds(m + 1, 1), :].broadcast_to([P, GR, P]),
                                           ALU.mult).then_inc(s["masked"], 1)

        @block.vector
        def _(dve):
            dve.wait_ge(s["consts"], 16 * 16)
            dve.wait_ge(s["cleared"], 5)
            dve.sem_inc(s["turn_done"], 1)
            dve.sem_inc(s["x_done"], XC)
            dve.sem_inc(s["y_product"], YC)
            with dve.Fori(0, TILES) as i:
                link = Chain(dve, s["dve_chain"], i, PER_DVE)
                for d in range(2):
                    t = tile(d, i)
                    dve.wait_ge(s["g_sums"], 2 * i + d + 1)
                    link(dve.tensor_tensor(decay[:, :, :], heads(ps[:, 0, :]), rate("G", d, t), ALU.subtract))
                    dve.tensor_tensor(decay[:, :, :], decay[:, :, :], bcm(outside[d][:, :], GH),
                                      ALU.add).then_inc(s["g_shift"], 1)
                    dve.wait_ge(s["g_decay"], 2 * i + d + 1)
                    dve.wait_ge(s["gram"], 2 * i + d + 1)
                    v = pairs_view(1 + 2 * d)
                    for h in range(GH):
                        link(dve.scalar_tensor_tensor(NT_[d][:, h, :], v[:, h, 0, :],
                                                      rates["neg_beta"][d][:, bass.ds(t, 1), h], decay[:, h, :],
                                                      ALU.mult, ALU.mult))
                    dve.tensor_tensor(A_o[d][:, :, :], v[:, :, 1, :], decay[:, :, :], ALU.mult).then_inc(s["gram_used"], 1)
                    dve.wait_ge(s["gram_used"], 2 * i + d + 1)
                for d in range(2):
                    dve.wait_ge(s["w_exp"], 2 * i + d + 1)
                    dve.wait_ge(early[d], 48 * i + 48)
                    dve.wait_ge(late[d], 32 * i + 32)
                    link(dve.scalar_tensor_tensor(AR[d][:, :, 0, :], fb[d][:, 2, :, :], -1.0, e_exc[:, :, :],
                                                  ALU.mult, ALU.mult))
                    link(dve.tensor_tensor(AR[d][:, :, 1, :], rr[d][:, :, :], e_inc[:, :, :], ALU.mult))
                    link(dve.tensor_tensor(BT[d][:, :, :], fd[d][:, 0, :, :], e_neg[:, :, :], ALU.mult))
                    dve.tensor_tensor(KT[d][:, :, :], fd[d][:, 1, :, :], e_neg[:, :, :], ALU.mult).then_inc(s["w_used"], 1)
                for d in range(2):
                    flat = S_r[d][:, :, :, :].rearrange("p k a n -> p k (a n)")
                    link(dve.tensor_tensor(rest[d][:, :, :], bc(ends[d][:, :, 1], 2), bcm(head_cols[:, :], RB), ALU.mult))
                    scaled = dve.tensor_tensor(flat, flat, bc(ends[d][:, :, 0], P), ALU.mult)
                    if d == 0:
                        link(scaled)
                scaled.then_inc(s["state_scaled"], 1)
                dve.wait_ge(s["state_scaled"], i + 1)
                for g in range(2, G):
                    d = direction[g]
                    dve.wait_ge(s["pairs"], 4 * i + g - 1)
                    with_b, with_k = pairs_view(1), pairs_view(3)
                    link(dve.tensor_tensor(NT_[g][:, :, :], with_b[:, :, 0, :], bcm(excl[d][:, :], GR), ALU.mult))
                    link(dve.tensor_tensor(A_o[g][:, :, :], with_b[:, :, 1, :], bcm(incl[d][:, :], GR), ALU.mult))
                    link(dve.tensor_tensor(A_v[g][:, :, :], with_k[:, :, 0, :], bcm(excl[d][:, :], GR), ALU.mult))
                    dve.tensor_tensor(A_ov[g][:, :, :], with_k[:, :, 1, :], bcm(incl[d][:, :], GR),
                                      ALU.mult).then_inc(s["pairs_used"], 1)
                with dve.Fori(0, ML) as m:
                    it = (i * ML + m) * G
                    for g in range(G):
                        dve.wait_ge(s["z_product"], it + g + 1)
                        dve.wait_ge(s["x_done"], it + g + XC)
                        dve.tensor_tensor(XT[g][:, :, :], XT[g][:, :, :], heads(ps[:, 4 + g % 2, :]),
                                          ALU.add).then_inc(s["x_done"], 1)
                for d in range(2):
                    dve.wait_ge(s["right"], G * i + d + 1)
                    link(dve.tensor_tensor(R[d], heads(ps[:, d, :]), rate("exp_G", d, tile(d, i)), ALU.mult))
                    dve.tensor_tensor(R[d], heads(tb[d][:, 1, :]), R[d], ALU.subtract).then_inc(s["right_g"], 1)
                for d in range(2):
                    dve.wait_ge(s["solved"], G * i + d + 1)
                    dve.tensor_tensor(U[d], heads(ps[:, d, :]), rate("beta", d, tile(d, i)), ALU.mult).then_inc(s["u_g"], 1)
                for g in range(G):
                    d, half = direction[g], g % 2
                    t = tile(d, i)
                    dve.wait_ge(s["outs"], G * i + g + 1)
                    if g < 2:
                        o = out[:, bass.ds(t, 1), 0:GW].rearrange("p o (h n) -> p (o h) n", n=P)
                        link(dve.tensor_tensor(R[d], heads(ps[:, d, :]), rate("exp_G", d, t), ALU.mult))
                        link(dve.tensor_tensor(o, o, R[d], ALU.add))
                        dve.tensor_tensor(o, o, heads(ps[:, 6 + d, :]), ALU.add).then_inc(s["outs_used"], 1)
                        continue
                    o = out[:, bass.ds(t, 1), GW + half * 4 * RN:GW + (half + 1) * 4 * RN].rearrange(
                        "p o (b a n) -> p (o a) b n", a=2, n=RN)
                    state = S_r[d][:, 2 * half:2 * half + 2, :, :].rearrange("p k a n -> p (k a) n")
                    link(dve.tensor_tensor(state, state, heads(ps[:, g, 256:512], RN), ALU.add))
                    link(dve.tensor_tensor(state, state, bc(rest[d][:, 2 * half:2 * half + 2, :].rearrange("p k a -> p (k a)"), RN),
                                           ALU.mult))
                    dve.tensor_tensor(o, o, ps[:, g, 0:4 * RN].rearrange("p (a b n) -> p a b n", a=2, n=RN), ALU.add).then_inc(s["outs_used"], 1)
                dve.wait_ge(s["outs_used"], G * i + G)
                for d in range(2):
                    more = keep[d][:, bass.ds(i, 1)]
                    dve.wait_ge(s["g_state"], 2 * i + d + 1)
                    link(dve.tensor_scalar(S_r[d][:, :, :, :], S_r[d][:, :, :, :], more, None, ALU.mult))
                    link(dve.tensor_tensor(S_g[d][:, :, :], S_g[d][:, :, :], rate("exp_last", d, tile(d, i)), ALU.mult))
                    link(dve.tensor_tensor(S_g[d][:, :, :], S_g[d][:, :, :], heads(ps[:, 6 + d, :]), ALU.add))
                    link(dve.tensor_scalar(S_g[d][:, :, :], S_g[d][:, :, :], more, None, ALU.mult))
                dve.sem_inc(s["turn_done"], 1)
                link.done()


def gate_outputs(nc, E, ins, out, z_tm, tm_both):
    o_norm = E.sb("o_norm", [P, GD])
    ln_g, ln_b = E.sb("ln_g", [P, RW]), E.sb("ln_b", [P, RW])
    eps_g, eps_r = E.sb("eps_g", [P, 1]), E.sb("eps_r", [P, 1])
    z = [E.sb(f"z{j}", [P, GW]) for j in range(2)]
    gb = [E.sb(f"gb{j}", [P, 2, RW]) for j in range(2)]
    sq = [E.sb(f"sq{j}", [P, D]) for j in range(2)]
    stat = [E.sb(f"stat{j}", [P, GH + RH]) for j in range(2)]
    mean = [E.sb(f"mean{j}", [P, RH]) for j in range(2)]
    params, eps_set, centred, squared, summed, rooted, dve_chain, act_chain, used = (
        E.sem(n) for n in ("params", "eps_set", "centred", "squared", "summed", "rooted", "dve_chain", "act_chain", "used"))
    loaded = [E.sem(f"loaded{j}") for j in range(2)]
    with nc.Block() as block:
        @block.sync
        def _(sp):
            sp.dma_start(o_norm[:, :], ins["gdn_o_norm"][0].partition_broadcast(P)).then_inc(params, 16)
            sp.dma_start(ln_g[:, :], ins["rwkv_ln_g"][0].partition_broadcast(P)).then_inc(params, 16)
            sp.dma_start(ln_b[:, :], ins["rwkv_ln_b"][0].partition_broadcast(P)).then_inc(params, 16)

            def load(t, j):
                sp.dma_start(z[j][:, :].unsqueeze(1), z_tm[bass.ds(t, 1)].rearrange("o p n -> p o n")).then_inc(loaded[j], 16)
                sp.dma_start(gb[j][:, :, :].rearrange("p a n -> p (a n)").unsqueeze(1),
                             tm_both[bass.ds(t, 1)].rearrange("o p n -> p o n")[:, :, 3 * GW:5 * GW]).then_inc(loaded[j], 16)

            for j in range(2):
                load(j, j)
            with sp.Fori(0, TILES // 2 - 1) as i:
                for j in range(2):
                    sp.wait_ge(used, 2 * i + j + 1)
                    load(2 * i + 2 + j, j)

        @block.scalar
        def _(act):
            act.wait_ge(eps_set, 2)
            with act.Fori(0, TILES // 2) as i:
                for j in range(2):
                    act.wait_ge(centred, 2 * i + j + 1)
                    act.activation(sq[j][:, :].unsqueeze(1), out[:, bass.ds(2 * i + j, 1), :], ACT.Square).then_inc(squared, 1)
                for j in range(2):
                    act.wait_ge(summed, 2 * i + j + 1)
                    act.activation(stat[j][:, 0:GH], stat[j][:, 0:GH], ACT.Sqrt, bias=eps_g[:, :],
                                   scale=1.0 / GD).then_inc(act_chain, 1)
                    act.wait_ge(act_chain, 2 * i + j + 1)
                    act.activation(stat[j][:, GH:], stat[j][:, GH:], ACT.Sqrt, bias=eps_r[:, :],
                                   scale=1.0 / RN).then_inc(rooted, 1)

        @block.vector
        def _(dve):
            dve.memset(eps_g[:, :], EPS).then_inc(eps_set, 1)
            dve.memset(eps_r[:, :], LN_EPS).then_inc(eps_set, 1)
            dve.wait_ge(params, 48)
            with dve.Fori(0, TILES // 2) as i:
                link = Chain(dve, dve_chain, i, 24)
                for j in range(2):
                    orr = out[:, bass.ds(2 * i + j, 1), GW:D].rearrange("p o (h n) -> p (o h) n", n=RN)
                    link(dve.tensor_reduce(mean[j][:, :], orr, AX.X, ALU.add))
                    link(dve.tensor_scalar(mean[j][:, :], mean[j][:, :], 1.0 / RN, None, ALU.mult))
                    dve.tensor_tensor(orr, orr, bc(mean[j][:, :], RN), ALU.subtract).then_inc(centred, 1)
                for j in range(2):
                    dve.wait_ge(squared, 2 * i + j + 1)
                    link(dve.tensor_reduce(stat[j][:, 0:GH], sq[j][:, 0:GW].rearrange("p (h n) -> p h n", n=GD), AX.X, ALU.add))
                    dve.tensor_reduce(stat[j][:, GH:], sq[j][:, GW:].rearrange("p (h n) -> p h n", n=RN), AX.X,
                                      ALU.add).then_inc(summed, 1)
                for j in range(2):
                    og = out[:, bass.ds(2 * i + j, 1), 0:GW].rearrange("p o (h n) -> p (o h) n", n=GD)
                    orr = out[:, bass.ds(2 * i + j, 1), GW:D].rearrange("p o (h n) -> p (o h) n", n=RN)
                    of = out[:, bass.ds(2 * i + j, 1), GW:D]
                    dve.wait_ge(rooted, 2 * i + j + 1)
                    dve.wait_ge(loaded[j], 32 * i + 32)
                    link(dve.reciprocal(stat[j][:, :], stat[j][:, :]))
                    link(dve.tensor_tensor(og, og, bc(stat[j][:, 0:GH], GD), ALU.mult))
                    link(dve.tensor_tensor(og, og, bcm(o_norm[:, :], GH), ALU.mult))
                    link(dve.tensor_tensor(og, og, z[j][:, :].rearrange("p (h n) -> p h n", n=GD), ALU.mult))
                    link(dve.tensor_tensor(orr, orr, bc(stat[j][:, GH:], RN), ALU.mult))
                    link(dve.tensor_tensor(of, of, ln_g[:, :].unsqueeze(1), ALU.mult))
                    link(dve.tensor_tensor(of, of, ln_b[:, :].unsqueeze(1), ALU.add))
                    link(dve.tensor_tensor(of, of, gb[j][:, 1:2, :], ALU.add))
                    dve.tensor_tensor(of, of, gb[j][:, 0:1, :], ALU.mult).then_inc(used, 1)
                dve.wait_ge(used, 2 * i + 2)
                link(dve.tensor_copy(mean[0][:, 0:1], mean[0][:, 0:1]))
                link(dve.tensor_copy(mean[0][:, 0:1], mean[0][:, 0:1]))
                link.done()


def project_out(nc, E, ident, mix, w_out):
    w = E.sb("w", [P, KB, D])
    mT = [E.sb(f"mT{j}", [P, KB, P]) for j in range(2)]
    ps = [E.stack.enter_context(nc.psum_tensor(f"{E.tag}_ps{j}", [P, 2, 512], F32)) for j in range(4)]
    w_loaded, turned, turned_out, product, done = (E.sem(n) for n in ("w_loaded", "turned", "turned_out", "product", "done"))
    with nc.Block() as block:
        @block.sync
        def _(sp):
            sp.dma_start(w[:, :, :], w_out.rearrange("(k p) n -> p k n", p=P)).then_inc(w_loaded, 16)

        @block.tensor
        def _(pe):
            def turn(t):
                if t >= 2:
                    pe.wait_ge(turned_out, t - 1)
                for k in range(KB):
                    last = pe.transpose(ps[t % 2][:, k // 4, (k % 4) * P:(k % 4 + 1) * P], mix[:, t, k * P:(k + 1) * P], ident[:, :])
                last.then_inc(turned, 1)

            turn(0)
            for t in range(TILES):
                if t + 1 < TILES:
                    turn(t + 1)
                if t == 0:
                    pe.wait_ge(w_loaded, 16)
                pe.wait_ge(turned_out, t + 1)
                if t >= 2:
                    pe.wait_ge(done, t - 1)
                for half in range(2):
                    for k in range(KB):
                        last = pe.matmul(ps[2 + t % 2][:, half, :], mT[t % 2][:, k, :], w[:, k, half * 512:(half + 1) * 512],
                                         start=(k == 0), stop=(k == KB - 1))
                last.then_inc(product, 1)

        @block.vector
        def _(dve):
            for t in range(TILES):
                dve.wait_ge(turned, t + 1)
                if t >= 2:
                    dve.wait_ge(product, t - 1)
                dve.tensor_copy(mT[t % 2][:, :, :].rearrange("p (a b) n -> p a (b n)", a=2), ps[t % 2][:, :, :]).then_inc(turned_out, 1)

        @block.scalar
        def _(act):
            for t in range(TILES):
                act.wait_ge(product, t + 1)
                act.activation(mix[:, t, :].rearrange("p (a n) -> p a n", a=2), ps[2 + t % 2][:, :, :], ACT.Copy).then_inc(done, 1)
            act.wait_ge(done, TILES)


def latents(nc, E, ins, hT, spare, qlT, kvlT, krT, cos, sin):
    n_cols = Q_LORA + KV_LORA + ROPE
    half = ROPE // 2
    w_raw = spare[:, 0:KB // 2, :].rearrange("p t (a n) -> p (t a) n", a=2)
    w = E.pair("w", [P, KB, n_cols + ROPE])
    ones = E.sb("ones", [P, P])
    eps = E.sb("eps", [P, 1])
    g = E.sb("g", [P, 3])
    raw = E.sb("raw", [P, 3, 512])
    sq = E.sb("sq", [P, 3, 512])
    root = E.sb("root", [P, 2, 512])
    part = [E.sb(f"part{u}", [ROPE, 512]) for u in range(2)]
    bank = E.banks(8)
    w_loaded, w_high, w_low = (E.sem(n) for n in ("w_loaded", "w_high", "w_low"))
    loaded, eps_set, multiplied, raw_out, squared, sums, rooted, normal, rope_done, dve_chain = (
        E.sem(n) for n in ("loaded", "eps_set", "multiplied", "raw_out", "squared", "sums", "rooted", "normal", "rope_done",
                           "dve_chain"))
    w_in = ins["w_in_odd"][0].rearrange("(k p) n -> p k n", p=P)
    rope0 = Q_LORA + KV_LORA
    with nc.Block() as block:
        @block.sync
        def _(sp):
            sp.dma_start(w_raw[:, :, 0:n_cols], w_in).then_inc(w_loaded, 16)
            sp.dma_start(w_raw[:, :, n_cols:n_cols + half], w_in[:, :, rope0 + half:rope0 + ROPE]).then_inc(w_loaded, 16)
            sp.dma_start(w_raw[:, :, n_cols + half:n_cols + ROPE], w_in[:, :, rope0:rope0 + half]).then_inc(w_loaded, 16)
            sp.dma_start(ones[:, :], ins["c_ones"]).then_inc(loaded, 16)
            sp.dma_start(cos[:, :], ins["c_cos"]).then_inc(loaded, 16)
            sp.dma_start(sin[:, :], ins["c_sin"]).then_inc(loaded, 16)
            sp.dma_start(g[:, 0:2], ins["mla_q_norm"][0].rearrange("(k p) -> p k", p=P),
                         allow_slow_non_contiguous=True).then_inc(loaded, 16)
            sp.dma_start(g[:, 2:3], ins["mla_kv_norm"].rearrange("n p -> p n"), allow_slow_non_contiguous=True).then_inc(loaded, 16)

        @block.tensor
        def _(pe):
            pe.wait_ge(loaded, 16 * 5)
            for q, (t0, n) in enumerate(PIECES):
                if q > 0:
                    pe.wait_ge(raw_out, 3 * q)
                    pe.wait_ge(rope_done, q)
                for b in range(5):
                    c0, m = (b * P, P) if b < 3 else (rope0 + (b - 3) * ROPE, ROPE)
                    for k in range(KB):
                        if q + b == 0:
                            pe.wait_ge(w_low, k + 1)
                        last = product(pe, bank[b][0:m, 0:n], both(w, slice(None), k, slice(c0, c0 + m)),
                                       both(hT, slice(None), k, slice(t0, t0 + n)), k == 0, k == KB - 1)
                    last.then_inc(multiplied, 1)
                pe.wait_ge(squared, 3 * q + 3)
                if q > 0:
                    pe.wait_ge(rooted, 2 * q)
                pe.matmul(bank[5][:, 0:n], ones[:, :], sq[:, 0, 0:n], start=True, stop=False)
                pe.matmul(bank[5][:, 0:n], ones[:, :], sq[:, 1, 0:n], start=False, stop=True)
                pe.matmul(bank[6][:, 0:n], ones[:, :], sq[:, 2, 0:n], start=True, stop=True).then_inc(sums, 1)

        @block.scalar
        def _(act):
            act.wait_ge(eps_set, 1)
            act.wait_ge(w_loaded, 48)
            for k in range(KB):
                act.activation(w[0][:, k, :], w_raw[:, k, :], ACT.Copy).then_inc(w_high, 1)
            for q, (t0, n) in enumerate(PIECES):
                if q > 0:
                    act.wait_ge(normal, 3 * q)
                for b in range(3):
                    act.wait_ge(multiplied, 5 * q + b + 1)
                    act.activation(raw[:, b, 0:n], bank[b][:, 0:n], ACT.Copy).then_inc(raw_out, 1)
                act.wait_ge(raw_out, 3 * q + 3)
                for b in range(3):
                    act.activation(sq[:, b, 0:n], raw[:, b, 0:n], ACT.Square).then_inc(squared, 1)
                act.wait_ge(sums, q + 1)
                for u, width in enumerate((Q_LORA, KV_LORA)):
                    act.activation(root[:, u, 0:n], bank[5 + u][:, 0:n], ACT.Sqrt, bias=eps[:, :],
                                   scale=1.0 / width).then_inc(rooted, 1)

        @block.vector
        def _(dve):
            dve.memset(eps[:, :], EPS).then_inc(eps_set, 1)
            link = Chain(dve, dve_chain)
            dve.wait_ge(loaded, 16 * 5)
            for k in range(KB):
                dve.wait_ge(w_high, k + 1)
                dve.tensor_tensor(w[1][:, k, :], w_raw[:, k, :], w[0][:, k, :].bitcast(F32), ALU.subtract).then_inc(w_low, 1)
            for q, (t0, n) in enumerate(PIECES):
                for u, table in enumerate((cos, sin)):
                    dve.wait_ge(multiplied, 5 * q + 4 + u)
                    link(dve.tensor_tensor(part[u][:, 0:n], bank[3 + u][0:ROPE, 0:n], table[:, t0:t0 + n], ALU.mult))
                dve.tensor_tensor(krT[:, t0:t0 + n], part[0][:, 0:n], part[1][:, 0:n], ALU.add).then_inc(rope_done, 1)
                dve.wait_ge(rope_done, q + 1)
                dve.wait_ge(rooted, 2 * q + 2)
                link(dve.reciprocal(root[:, :, 0:n], root[:, :, 0:n]))
                for b in range(3):
                    dst = qlT[:, b, t0:t0 + n] if b < 2 else kvlT[:, t0:t0 + n]
                    dve.scalar_tensor_tensor(dst, raw[:, b, 0:n], g[:, b:b + 1], root[:, b // 2, 0:n],
                                             ALU.mult, ALU.mult).then_inc(normal, 1)
            dve.wait_ge(normal, 3 * len(PIECES))


def values(nc, E, ins, kvlT, V):
    w = E.sb("w", [P, MH * MV])
    bank = E.banks(8)
    loaded, product, act_out, dve_out = (E.sem(n) for n in ("loaded", "product", "act_out", "dve_out"))
    wv = ins["mla_w_kv_b"][0].rearrange("p (h n) -> p h n", n=NOPE + MV)
    with nc.Block() as block:
        @block.sync
        def _(sp):
            sp.dma_start(w[:, :].rearrange("p (h n) -> p h n", n=MV), wv[:, :, NOPE:NOPE + MV]).then_inc(loaded, 16)

        @block.tensor
        def _(pe):
            pe.wait_ge(loaded, 16)
            for t in range(TILES):
                if t >= 4:
                    pe.wait_ge(act_out, t - 3)
                    pe.wait_ge(dve_out, t - 3)
                for half in range(2):
                    pe.matmul(bank[2 * (t % 4) + half][:, :], kvlT[:, t * P:(t + 1) * P], w[:, half * 512:(half + 1) * 512],
                              start=True, stop=True).then_inc(product, 1)

        @block.scalar
        def _(act):
            for t in range(TILES):
                act.wait_ge(product, 2 * t + 1)
                act.activation(V[:, t, 0:512], bank[2 * (t % 4)][:, :], ACT.Copy).then_inc(act_out, 1)
            act.wait_ge(act_out, TILES)

        @block.vector
        def _(dve):
            for t in range(TILES):
                dve.wait_ge(product, 2 * t + 2)
                dve.tensor_copy(V[:, t, 512:1024], bank[2 * (t % 4) + 1][:, :]).then_inc(dve_out, 1)
            dve.wait_ge(dve_out, TILES)


def attend(nc, E, ins, ident, qlT, kvlT, krT, cos, sin, V, out):
    half = ROPE // 2
    SCALE = float(NOPE + ROPE) ** -0.5
    wq = E.sb("wq", [P, 2, NOPE])
    wr = E.sb("wr", [P, 2, 2, ROPE])
    wk = E.sb("wk", [P, NOPE])
    qn, kn = E.sb("qn", [P, NT]), E.sb("kn", [P, NT])
    qr = E.sb("qr", [ROPE, NT])
    part = [E.sb(f"part{u}", [ROPE, 512]) for u in range(2)]
    w_sm = [E.sb(f"w_sm{j}", [P, T_PROMPT]) for j in range(2)]
    wT = [E.sb(f"wT{j}", [P, T_PROMPT // P, P]) for j in range(2)]
    mx, neg = (E.sb(n, [P, 2]) for n in ("mx", "neg"))
    total, inv = (E.sb(n, [P, TILES]) for n in ("total", "inv"))
    ps = E.stack.enter_context(nc.psum_tensor(f"{E.tag}_ps", [P, 8, 512], F32))
    SCORES, TURN, OUT = (0, 2), 4, 6
    names = ("w_loaded", "q_product", "r_product", "k_product", "q_out", "k_out", "r_out", "scores", "shifted", "exped",
             "turned", "turned_a", "turned_b", "weighted", "written", "dve_chain")
    s = {n: E.sem(n) for n in names}
    w_q = ins["mla_w_q_b"][0].rearrange("(k p) n -> p k n", p=P)
    w_kv = ins["mla_w_kv_b"][0]
    NQ = len(PIECES)

    def keys(t):
        return (0, T_PROMPT) if t < TILES_P else (T_PROMPT, T_SAMPLE)

    with nc.Block() as block:
        @block.sync
        def _(sp):
            def load(h):
                c = h * (NOPE + ROPE)
                sp.dma_start(wq[:, :, :], w_q[:, :, bass.ds(c, NOPE)]).then_inc(s["w_loaded"], 16)
                sp.dma_start(wr[:, :, 0, :], w_q[:, :, bass.ds(c + NOPE, ROPE)]).then_inc(s["w_loaded"], 16)
                sp.dma_start(wr[:, :, 1, 0:half], w_q[:, :, bass.ds(c + NOPE + half, half)]).then_inc(s["w_loaded"], 16)
                sp.dma_start(wr[:, :, 1, half:ROPE], w_q[:, :, bass.ds(c + NOPE, half)]).then_inc(s["w_loaded"], 16)
                sp.dma_start(wk[:, :], w_kv[:, bass.ds(h * (NOPE + MV), NOPE)]).then_inc(s["w_loaded"], 16)

            load(0)
            with sp.Fori(0, MH - 1) as h:
                sp.wait_ge(s["k_product"], NQ * h + NQ)
                load(h + 1)

        @block.tensor
        def _(pe):
            with pe.Fori(0, MH) as h:
                pe.wait_ge(s["w_loaded"], 80 * h + 80)
                pe.wait_ge(s["exped"], TILES * h + 2)
                for q, (t0, n) in enumerate(PIECES):
                    if q == 2:
                        pe.wait_ge(s["q_out"], NQ * h + 1)
                        pe.wait_ge(s["k_out"], NQ * h + 1)
                    for k in range(2):
                        last = pe.matmul(ps[:, q % 2, 0:n], wq[:, k, :], qlT[:, k, t0:t0 + n], start=(k == 0), stop=(k == 1))
                    last.then_inc(s["q_product"], 1)
                    if q > 0:
                        pe.wait_ge(s["r_out"], NQ * h + q)
                    for u in range(2):
                        for k in range(2):
                            last = pe.matmul(ps[0:ROPE, 2 + u, 0:n], wr[:, k, u, :], qlT[:, k, t0:t0 + n],
                                             start=(k == 0), stop=(k == 1))
                    last.then_inc(s["r_product"], 1)
                    pe.matmul(ps[:, 4 + q % 2, 0:n], wk[:, :], kvlT[:, t0:t0 + n], start=True, stop=True).then_inc(s["k_product"], 1)
                pe.wait_ge(s["q_out"], NQ * h + NQ)
                pe.wait_ge(s["k_out"], NQ * h + NQ)
                pe.wait_ge(s["r_out"], NQ * h + NQ)

                def scores(t):
                    k0, nk = keys(t)
                    pe.wait_ge(s["exped"], TILES * h + t + 1)
                    for c in range(0, nk, 512):
                        n = min(512, nk - c)
                        o = ps[:, SCORES[t % 2] + c // 512, 0:n]
                        pe.matmul(o, qn[:, t * P:(t + 1) * P], kn[:, k0 + c:k0 + c + n], start=True, stop=False)
                        last = pe.matmul(o, qr[:, t * P:(t + 1) * P], krT[:, k0 + c:k0 + c + n], start=False, stop=True)
                    last.then_inc(s["scores"], 1)

                def turn(t):
                    nk = keys(t)[1]
                    pe.wait_ge(s["exped"], TILES * h + t + 1 + 2)
                    pe.wait_ge(s["turned_a"], TILES * h + t + 1)
                    pe.wait_ge(s["turned_b"], TILES * h + t + 1)
                    for b in range(nk // P):
                        last = pe.transpose(ps[:, TURN + b // 4, (b % 4) * P:(b % 4 + 1) * P],
                                            w_sm[t % 2][:, b * P:(b + 1) * P], ident[:, :])
                    last.then_inc(s["turned"], 1)

                def weigh(t):
                    k0, nk = keys(t)
                    pe.wait_ge(s["turned_a"], TILES * h + t + 2)
                    pe.wait_ge(s["turned_b"], TILES * h + t + 2)
                    pe.wait_ge(s["written"], TILES * h + t + 1)
                    for b in range(nk // P):
                        last = pe.matmul(ps[:, OUT + t % 2, 0:MV], wT[t % 2][:, b, :],
                                         V[:, k0 // P + b, bass.ds(h * MV, MV)], start=(b == 0), stop=(b == nk // P - 1))
                    last.then_inc(s["weighted"], 1)

                for t in range(TILES + 2):
                    if t < TILES:
                        scores(t)
                    if 1 <= t <= TILES:
                        turn(t - 1)
                    if t >= 2:
                        weigh(t - 2)

        @block.scalar
        def _(act):
            act.sem_inc(s["exped"], 2)
            act.sem_inc(s["turned_a"], 1)
            with act.Fori(0, MH) as h:
                for q, (t0, n) in enumerate(PIECES):
                    act.wait_ge(s["q_product"], NQ * h + q + 1)
                    if q == 0:
                        act.wait_ge(s["scores"], TILES * h + 1)
                    act.activation(qn[:, t0:t0 + n], ps[:, q % 2, 0:n], ACT.Copy).then_inc(s["q_out"], 1)
                    act.wait_ge(s["k_product"], NQ * h + q + 1)
                    act.activation(kn[:, t0:t0 + n], ps[:, 4 + q % 2, 0:n], ACT.Copy).then_inc(s["k_out"], 1)

                def exps(t):
                    nk = keys(t)[1]
                    act.wait_ge(s["shifted"], TILES * h + t + 1)
                    act.activation(w_sm[t % 2][:, 0:nk], ps[:, SCORES[t % 2]:SCORES[t % 2] + 2, :].rearrange("p a n -> p (a n)")[:, 0:nk],
                                   ACT.Exp, bias=neg[:, t % 2:t % 2 + 1], scale=SCALE,
                                   accum_out=total[:, t:t + 1]).then_inc(s["exped"], 1)

                def copy(t):
                    nb = keys(t)[1] // P // 2
                    act.wait_ge(s["turned"], TILES * h + t + 1)
                    act.activation(wT[t % 2][:, 0:nb, :].rearrange("p b n -> p (b n)"), ps[:, TURN, 0:nb * P],
                                   ACT.Copy).then_inc(s["turned_a"], 1)

                for t in range(TILES + 1):
                    if t < TILES:
                        exps(t)
                    if t >= 1:
                        copy(t - 1)

        @block.vector
        def _(dve):
            dve.sem_inc(s["turned_b"], 1)
            dve.sem_inc(s["scores"], 1)
            dve.sem_inc(s["written"], 2)
            with dve.Fori(0, MH) as h:
                link = Chain(dve, s["dve_chain"], h, 2 * NQ + 2 * TILES)
                for q, (t0, n) in enumerate(PIECES):
                    dve.wait_ge(s["r_product"], NQ * h + q + 1)
                    for u, table in enumerate((cos, sin)):
                        link(dve.tensor_tensor(part[u][:, 0:n], ps[0:ROPE, 2 + u, 0:n], table[:, t0:t0 + n], ALU.mult))
                    dve.tensor_tensor(qr[:, t0:t0 + n], part[0][:, 0:n], part[1][:, 0:n], ALU.add).then_inc(s["r_out"], 1)
                    dve.wait_ge(s["r_out"], NQ * h + q + 1)

                def shift(t):
                    nk = keys(t)[1]
                    dve.wait_ge(s["scores"], TILES * h + t + 2)
                    j = slice(t % 2, t % 2 + 1)
                    link(dve.reduce_max(mx[:, j], ps[:, SCORES[t % 2]:SCORES[t % 2] + 2, :].rearrange("p a n -> p (a n)")[:, 0:nk], AX.X))
                    dve.tensor_scalar(neg[:, j], mx[:, j], -SCALE, None, ALU.mult).then_inc(s["shifted"], 1)

                def copy(t):
                    nb = keys(t)[1] // P // 2
                    dve.wait_ge(s["turned"], TILES * h + t + 1)
                    bank, c0 = (TURN + 1, 0) if nb == 4 else (TURN, nb * P)
                    if nb < 4:
                        dve.wait_ge(s["turned_a"], TILES * h + t + 2)
                    dve.tensor_copy(wT[t % 2][:, nb:2 * nb, :].rearrange("p b n -> p (b n)"), ps[:, bank, c0:c0 + nb * P]
                                    ).then_inc(s["turned_b"], 1)

                def write(t):
                    j = slice(t, t + 1)
                    link(dve.reciprocal(inv[:, j], total[:, j]))
                    dve.wait_ge(s["weighted"], TILES * h + t + 1)
                    dve.tensor_scalar(out[:, t, bass.ds(h * MV, MV)], ps[:, OUT + t % 2, 0:MV], inv[:, j], None,
                                      ALU.mult).then_inc(s["written"], 1)

                for t in range(TILES + 2):
                    if t < TILES:
                        shift(t)
                    if 1 <= t <= TILES:
                        copy(t - 1)
                    if t >= 2:
                        write(t - 2)
                link.done()


def latent_tensors(nc, stack):
    return [stack.enter_context(nc.sbuf_tensor(name, shape, F32))
            for name, shape in (("qlT", [P, 2, NT]), ("kvlT", [P, NT]), ("krT", [ROPE, NT]), ("cos", [ROPE, NT]),
                                ("sin", [ROPE, NT]))]


def clear_semaphores(nc, sems):
    with nc.Block() as block:
        @block.sync
        def _(sp):
            for sem in sems:
                sp.sem_clear(sem)


def program(nc, ins, outs, stop=99):
    scratch = {}

    def dram(name, shape):
        scratch[name] = nc.dram_tensor(f"s_{name}", shape, F32, kind="Internal").ap()
        return scratch[name]

    with ExitStack() as whole:
        def scope(tag):
            stack = ExitStack()
            E = Env(nc, stack, tag)
            E.sems = whole
            return stack, E

        _, top = scope("top")
        top.stack = whole
        acc = top.sb("acc", [P, TILES, D])
        gates = top.sb("gates", [P, TILES, 4 * GH])
        ident = top.sb("ident", [P, P])
        ident_loaded = top.sem("ident_loaded")
        with nc.Block() as block:
            @block.sync
            def _(sp):
                sp.dma_start(ident[:, :], ins["c_ident"]).then_inc(ident_loaded, 16)
                sp.wait_ge(ident_loaded, 16)

        conv_fm = dram("conv", [CONV_BLOCKS, P, NT])
        shift_fm = dram("shift", [RWKV_BLOCKS, P, NT])
        z_tm = dram("z", [TILES, P, GW])

        def phase(tag, f, *args, **kw):
            stack, E = scope(tag)
            with stack:
                E.sems = stack
                f(nc, E, *args, **kw)
                clear_semaphores(nc, E.made)

        x_in = token_tiles(ins["x_prompt"], ins["x_sample"])
        x_tm = dram("x", [TILES, P, D]).rearrange("t p d -> p t d")
        x_mid = (x_tm[:, 0:TILES_P, :], x_tm[:, TILES_P:TILES, :])
        x_out = token_tiles(*outs)

        def pair(stack, name):
            return [stack.enter_context(nc.sbuf_tensor(f"{name}_{part}", [P, KB, NT], F32R)) for part in ("high", "low")]

        with ExitStack() as wide:
            hT = pair(wide, "hT_first")
            phase("norm0", residual_norm, x_in, None, hT, ident, acc, None, ins["norm_mix_pre"][0])
            w_in = ins["w_in_even"][0]
            phase("conv", in_proj_fm, hT, w_in, 0, CONV_BLOCKS // 3, conv_fm, ins["gdn_conv"][0], True)
            phase("shift", in_proj_fm, hT, w_in, GDN_COLS, RWKV_BLOCKS // 3, shift_fm, ins["rwkv_mu"][0], False)
            phase("gates", in_proj_tm, hT, w_in, gates, z_tm)
        if stop > 1:
            mix_scopes(nc, phase, dram, ins, acc, gates, ident, conv_fm, shift_fm, z_tm, stop)
        if stop <= 4:
            return scratch
        with ExitStack() as wide:
            hT = pair(wide, "hT_ffn0")
            phase("norm1", residual_norm, x_in, x_mid, hT, ident, acc, ins["norm_mix_post"][0], ins["norm_ffn_pre"][0])
            phase("ffn0", feed_forward, hT, acc, ins["w_ff1"][0], ins["w_ff2"][0])
        if stop == 5:
            return scratch
        with ExitStack() as own:
            latent = latent_tensors(nc, own)
            with ExitStack() as wide:
                hT = pair(wide, "hT_attention")
                phase("norm2", residual_norm, x_mid, x_mid, hT, ident, acc, ins["norm_ffn_post"][0], ins["norm_mix_pre"][1])
                phase("latent", latents, ins, hT, acc, *latent)
            V = own.enter_context(nc.sbuf_tensor("V", [P, TILES, MH * MV], F32))
            phase("values", values, ins, latent[1], V)
            phase("attend", attend, ins, ident, *latent, V, acc)
        phase("out1", project_out, ident, acc, ins["w_out_odd"][0])
        if stop <= 6:
            return scratch
        with ExitStack() as wide:
            hT = pair(wide, "hT_ffn1")
            phase("norm3", residual_norm, x_mid, x_mid, hT, ident, acc, ins["norm_mix_post"][1], ins["norm_ffn_pre"][1])
            phase("ffn1", feed_forward, hT, acc, ins["w_ff1"][1], ins["w_ff2"][1])
        phase("norm4", residual_norm, x_mid, x_out, None, ident, acc, ins["norm_ffn_post"][1], None)
    return scratch


def constants():
    s = np.arange(P)[:, None]
    t = np.arange(P)[None, :]
    mid = P // 2
    c = {"c_ident": np.eye(P), "c_ones": np.ones((P, P))}
    c["c_head_ones"] = (s // RN == t // RN) * 1.0
    c["c_head_cols"] = (s // RN == np.arange(2)[None, :]) * 1.0
    incl = np.stack([s <= t, s >= t]) * 1.0
    excl = np.stack([s < t, s > t]) * 1.0
    c["c_incl"], c["c_excl"] = incl, excl
    c["c_outside"] = (incl - 1.0) * 1e9
    rate = -math.exp(-0.5)
    upto_mid = incl[:, :, mid:mid + 1]
    c["c_decay_sums"] = rate * (np.concatenate([incl, excl], 2) - upto_mid)
    c["c_decay_ends"] = rate * np.concatenate([upto_mid, 1.0 - upto_mid], 2)
    levels = []
    for m in range(LEVELS):
        n = 1 << m
        lower = ((s // n) % 2 == 0) & (t // n == s // n + 1)
        levels.append(lower)
    c["c_levels"] = np.stack([np.stack(levels), np.stack(levels).transpose(0, 2, 1)]) * 1.0
    keep = np.ones((2, P, TILES))
    keep[0, :, TILES_P - 1] = 0.0
    keep[1, :, TILES - TILES_P - 1] = 0.0
    c["c_keep"] = keep
    inv = 1.0 / (np.float32(10000.0) ** (np.arange(0, ROPE, 2, dtype=np.float32) / np.float32(ROPE)))
    at = np.concatenate([np.arange(T_PROMPT), np.arange(T_SAMPLE)]).astype(np.float32)
    ang = (inv.astype(np.float32)[:, None] * at[None, :]).astype(np.float32)
    c["c_cos"] = np.concatenate([np.cos(ang), np.cos(ang)], 0)
    c["c_sin"] = np.concatenate([-np.sin(ang), np.sin(ang)], 0)
    return {k: np.ascontiguousarray(v, dtype=np.float32) for k, v in c.items()}


_OUTS = ((1, T_PROMPT, D), (1, T_SAMPLE, D))


def kernel(**inputs):
    import concourse.bacc as bacc
    from concourse.bass_utils import run_bass_kernel_spmd

    nc = bacc.Bacc("TRN2", target_bir_lowering=False, num_devices=1)
    arrays, ins = {}, {}
    for name, a in {**inputs, **constants()}.items():
        a = np.ascontiguousarray(a)
        arrays[f"in_{name}"] = a
        ins[name] = nc.dram_tensor(f"in_{name}", a.shape, F32, kind="ExternalInput").ap()
    outs = tuple(nc.dram_tensor(f"out_{i}", shape, F32, kind="ExternalOutput").ap() for i, shape in enumerate(_OUTS))
    program(nc, ins, outs)
    r = run_bass_kernel_spmd(nc, [arrays], core_ids=[0])
    return tuple(r.results[0][f"out_{i}"] for i in range(len(_OUTS)))
```

```python
import math
from contextlib import ExitStack

import numpy as np
import concourse.bass as bass
from concourse import mybir

F32 = mybir.dt.float32
F32R = mybir.dt.float32r
ACT = mybir.ActivationFunctionType
ALU = mybir.AluOpType
AX = mybir.AxisListType

P = 128
D = 1024
KB = D // P
T_PROMPT, T_SAMPLE = 1024, 256
NT = T_PROMPT + T_SAMPLE
TILES = NT // P
TILES_P = T_PROMPT // P
D_FF = 4 * D
EPS = 1e-6
GH, GD = 4, 128
GW = GH * GD
RH, RN = 8, 64
RW = RH * RN
RB = RW // P
LN_EPS = 64e-5
GDN_COLS = 4 * GW + 4 * GH
CONV_BLOCKS = 3 * GW // P
RWKV_BLOCKS = 15
NORMS = 2 * GH + RH
TAPS = 5
PAD = 2
PADDED = PAD + T_PROMPT + PAD + T_SAMPLE + PAD
SPAN = T_PROMPT + PAD + T_SAMPLE
PIECES = ((0, 512), (512, 512), (1024, 256))
LEVELS = 7
MH, NOPE, ROPE, MV = 8, 128, 64, 128
Q_LORA, KV_LORA = 256, 128


def bc(ap, n):
    return ap.unsqueeze(2).broadcast_to([ap.shape[0], ap.shape[1], n])


def bcm(ap, m):
    return ap.unsqueeze(1).broadcast_to([ap.shape[0], m, ap.shape[1]])


class Chain:

    def __init__(self, eng, sem, i=None, per=0):
        self.eng, self.sem, self.i, self.per, self.n = eng, sem, i, per, 0

    def __call__(self, ins):
        self.n += 1
        ins.then_inc(self.sem, 1)
        self.eng.wait_ge(self.sem, self.n if self.i is None else self.i * self.per + self.n)

    def done(self):
        assert self.i is None or self.n == self.per, (self.sem, self.n, self.per)


class Env:

    def __init__(self, nc, stack, tag):
        self.nc, self.stack, self.tag, self.made = nc, stack, tag, []

    def sb(self, name, shape, dtype=F32):
        return self.stack.enter_context(self.nc.sbuf_tensor(f"{self.tag}_{name}", shape, dtype))

    def pair(self, name, shape):
        return [self.sb(f"{name}_{part}", shape, F32R) for part in ("high", "low")]

    def banks(self, n):
        return [self.stack.enter_context(self.nc.psum_tensor(f"{self.tag}_bank{i}", [P, 512], F32)) for i in range(n)]

    def sem(self, name):
        sem = self.sems.enter_context(self.nc.semaphore(f"{self.tag}_{name}"))
        self.made.append(sem)
        return sem


def token_tiles(prompt, sample):
    return tuple(v[0].rearrange("(t p) d -> p t d", p=P) for v in (prompt, sample))


def product(pe, out, stationary, moving, start, stop):
    pe.matmul(out, stationary[0], moving[0], start=start, stop=False)
    pe.matmul(out, stationary[0], moving[1], start=False, stop=False)
    return pe.matmul(out, stationary[1], moving[0], start=False, stop=stop)


def both(pair, *index):
    return tuple(part[index] for part in pair)


def residual_norm(nc, E, x_src, x_dst, hT, ident, X, g_post, g_pre):
    mixed = g_post is not None
    x_old = E.sb("x_old", [P, 2, D])
    gpost = E.sb("gpost", [P, D])
    gpre = E.sb("gpre", [P, KB])
    eps = E.sb("eps", [P, 1])
    h = [E.sb(f"h{j}", [P, D]) for j in range(2)]
    h_out = [E.sb(f"h_out{j}", [P, KB, P]) for j in range(2)]
    squares = [E.sb(f"squares{u}", [P, D]) for u in range(2)]
    sq1, rt1, rc1, sq2, rt2, rc2 = (E.sb(n, [P, 2]) for n in ("sq1", "rt1", "rc1", "sq2", "rt2", "rc2"))
    ps = [E.stack.enter_context(nc.psum_tensor(f"{E.tag}_ps{j}", [P, KB, P], F32)) for j in range(2)]
    names = ("gains", "eps_set", "mix_squares", "mix_root", "mix_chain", "mix_scaled", "x_updated", "x_squares", "x_root",
             "x_chain", "h_ready", "turned", "scaled", "high_done", "low_done", "stored", "loaded", "tick")
    (gains, eps_set, mix_squares, mix_root, mix_chain, mix_scaled, x_updated, x_squares, x_root, x_chain, h_ready, turned,
     scaled, high_done, low_done, stored, loaded, tick) = (E.sem(n) for n in names)
    n_gains = 16 * (mixed + (g_pre is not None))
    TURNS, TURNS_P = TILES // 2, TILES_P // 2
    with nc.Block() as block:
        @block.sync
        def _(sp):
            def pair_of(view, i):
                return view[:, bass.ds(2 * i, 2), :]

            if mixed:
                sp.dma_start(x_old[:, :, :], pair_of(x_src[0], 0)).then_inc(loaded, 16)
                sp.dma_start(gpost[:, :], g_post.partition_broadcast(P)).then_inc(gains, 16)
            if g_pre is not None:
                sp.dma_start(gpre[:, :], g_pre.rearrange("(k p) -> p k", p=P),
                             allow_slow_non_contiguous=True).then_inc(gains, 16)
            if mixed:
                with sp.Fori(0, TURNS_P - 1) as i:
                    sp.wait_ge(x_updated, 2 * i + 2)
                    sp.dma_start(x_old[:, :, :], pair_of(x_src[0], i + 1)).then_inc(loaded, 16)
                    sp.dma_start(pair_of(x_dst[0], i), pair_of(X, i)).then_inc(stored, 16)
                sp.wait_ge(x_updated, 2 * TURNS_P)
                sp.dma_start(x_old[:, :, :], x_src[1]).then_inc(loaded, 16)
                sp.dma_start(pair_of(x_dst[0], TURNS_P - 1), pair_of(X, TURNS_P - 1)).then_inc(stored, 16)
                sp.wait_ge(x_updated, TILES)
                sp.dma_start(x_dst[1], pair_of(X, TURNS_P)).then_inc(stored, 16)
                sp.wait_ge(stored, 16 * TURNS)
            else:
                sp.dma_start(pair_of(X, 0), pair_of(x_src[0], 0)).then_inc(loaded, 16)
                with sp.Fori(0, TURNS_P - 1) as i:
                    sp.wait_ge(loaded, 16 * i + 16)
                    sp.dma_start(pair_of(X, i + 1), pair_of(x_src[0], i + 1)).then_inc(loaded, 16)
                sp.wait_ge(loaded, 16 * TURNS_P)
                sp.dma_start(pair_of(X, TURNS_P), x_src[1]).then_inc(loaded, 16)

        def in_turns(eng, begin, mixer, finish):
            if g_pre is None:
                with eng.Fori(0, TURNS) as i:
                    mixer(i)
                return
            if mixed:
                mixer(0)
            with eng.Fori(0, TURNS - 1) as i:
                begin(i)
                if mixed:
                    mixer(i + 1)
                finish(i)
            begin(TURNS - 1)
            finish(TURNS - 1)

        @block.scalar
        def _(act):
            def mixer(i):
                for j in range(2):
                    act.wait_ge(mix_scaled, 2 * i + j + 1)
                    act.sem_inc(tick, 1)
                    act.activation(squares[0][:, :].unsqueeze(1), X[:, bass.ds(2 * i + j, 1), :], ACT.Square,
                                   accum_out=sq1[:, j:j + 1]).then_inc(mix_squares, 1)
                    act.wait_ge(mix_squares, 2 * i + j + 1)
                for j in range(2):
                    act.activation(rt1[:, j:j + 1], sq1[:, j:j + 1], ACT.Sqrt, bias=eps[:, :],
                                   scale=1.0 / D).then_inc(mix_root, 1)

            def begin(i):
                for j in range(2):
                    if mixed:
                        act.wait_ge(x_updated, 2 * i + j + 1)
                    elif j == 0:
                        act.wait_ge(loaded, 16 * i + 16)
                    act.sem_inc(tick, 1)
                    act.activation(squares[1][:, :].unsqueeze(1), X[:, bass.ds(2 * i + j, 1), :], ACT.Square,
                                   accum_out=sq2[:, j:j + 1]).then_inc(x_squares, 1)
                    act.wait_ge(x_squares, 2 * i + j + 1)
                for j in range(2):
                    act.activation(rt2[:, j:j + 1], sq2[:, j:j + 1], ACT.Sqrt, bias=eps[:, :],
                                   scale=1.0 / D).then_inc(x_root, 1)

            def finish(i):
                for j in range(2):
                    act.wait_ge(scaled, 2 * i + j + 1)
                    act.sem_inc(tick, 1)
                    act.activation(hT[0][:, :, bass.ds((2 * i + j) * P, P)], h_out[j][:, :, :],
                                   ACT.Copy).then_inc(high_done, 1)

            act.wait_ge(eps_set, 1)
            in_turns(act, begin, mixer, finish)

        @block.gpsimd
        def _(pool):
            def mixer(i):
                pool.wait_ge(loaded, 16 * i + 16)
                for j in range(2):
                    x = X[:, bass.ds(2 * i + j, 1), :]
                    pool.wait_ge(mix_scaled, 2 * i + j + 1 + 2)
                    pool.sem_inc(tick, 1)
                    pool.tensor_tensor(x, x, x_old[:, j:j + 1, :], ALU.add).then_inc(x_updated, 1)

            def finish(i):
                for j in range(2):
                    part = (slice(None), slice(None), bass.ds((2 * i + j) * P, P))
                    pool.wait_ge(high_done, 2 * i + j + 1)
                    pool.sem_inc(tick, 1)
                    pool.tensor_tensor(hT[1][part], h_out[j][:, :, :], hT[0][part].bitcast(F32),
                                       ALU.subtract).then_inc(low_done, 1)

            in_turns(pool, lambda i: None, mixer, finish)

        @block.vector
        def _(dve):
            def mixer(i):
                for j in range(2):
                    x = X[:, bass.ds(2 * i + j, 1), :]
                    dve.wait_ge(mix_root, 2 * i + j + 1)
                    dve.reciprocal(rc1[:, j:j + 1], rt1[:, j:j + 1]).then_inc(mix_chain, 1)
                    dve.wait_ge(mix_chain, 2 * i + j + 1)
                    dve.scalar_tensor_tensor(x, x, rc1[:, j:j + 1], gpost[:, :].unsqueeze(1), ALU.mult,
                                             ALU.mult).then_inc(mix_scaled, 1)

            def begin(i):
                for j in range(2):
                    dve.wait_ge(x_root, 2 * i + j + 1)
                    dve.reciprocal(rc2[:, j:j + 1], rt2[:, j:j + 1]).then_inc(x_chain, 1)
                    dve.wait_ge(x_chain, 2 * i + j + 1)
                    dve.tensor_scalar(h[j][:, :].unsqueeze(1), X[:, bass.ds(2 * i + j, 1), :], rc2[:, j:j + 1],
                                      None, ALU.mult).then_inc(h_ready, 1)

            def finish(i):
                for j in range(2):
                    dve.wait_ge(turned, 2 * i + j + 1)
                    dve.wait_ge(low_done, 2 * i + j + 1)
                    dve.tensor_tensor(h_out[j][:, :, :], ps[j][:, :, :], bc(gpre[:, :], P), ALU.mult).then_inc(scaled, 1)
                dve.wait_ge(scaled, 2 * i + 2)

            dve.memset(eps[:, :], EPS).then_inc(eps_set, 1)
            dve.sem_inc(low_done, 2)
            dve.sem_inc(mix_scaled, 2)
            dve.wait_ge(gains, n_gains)
            in_turns(dve, begin, mixer, finish)

        @block.tensor
        def _(pe):
            def finish(i):
                for j in range(2):
                    pe.wait_ge(h_ready, 2 * i + j + 1)
                    for k in range(KB):
                        last = pe.transpose(ps[j][:, k, :], h[j][:, k * P:(k + 1) * P], ident[:, :])
                    last.then_inc(turned, 1)

            if g_pre is not None:
                in_turns(pe, lambda i: None, lambda i: None, finish)


def in_proj_fm(nc, E, hT, w_in, first_col, turns, dst, weights, conv):
    n_taps = TAPS if conv else 3
    reach = n_taps // 2
    n_in = TAPS if conv else 2
    w_raw = [E.sb(f"w_raw{j}", [P, KB, P]) for j in range(3)]
    w = [E.pair(f"w{j}", [P, KB, P]) for j in range(3)]
    padded = [E.sb(f"padded{j}", [P, PADDED]) for j in range(3)]
    mixed = [E.sb(f"mixed{j}", [P, SPAN]) for j in range(3)]
    bank = E.banks(8)
    BANK = (0, 1, 2, 3, 4, 5, 6, 7, 2)
    w_loaded = [E.sem(f"w_loaded{j}") for j in range(3)]
    stored = [E.sem(f"stored{j}") for j in range(3)]
    w_high, w_low, multiplied, copied, taps_done, silu_done, dve_chain, zeroed, taps_loaded, setup_chain = (
        E.sem(n) for n in ("w_high", "w_low", "multiplied", "copied", "taps_done", "silu_done", "dve_chain", "zeroed",
                           "taps_loaded", "setup_chain"))
    tap = E.sb("tap", [P, 3 * turns, n_taps])
    raw_tap = E.sb("raw_tap", [P, 3 * turns, 2])
    wv = w_in.rearrange("(k p) n -> p k n", p=P)
    CREDIT = 3

    with nc.Block() as block:
        @block.sync
        def _(sp):
            for u in range(n_in):
                sp.dma_start((tap if conv else raw_tap)[:, :, u], weights[u].rearrange("(b p) -> p b", p=P),
                             allow_slow_non_contiguous=True).then_inc(taps_loaded, 16)
            for j in range(3):
                sp.dma_start(w_raw[j][:, :, :], wv[:, :, first_col + j * P:first_col + (j + 1) * P]).then_inc(w_loaded[j], 16)

            def store(i, j):
                sp.wait_ge(silu_done if conv else taps_done, 3 * i + j + 1 + (0 if conv else CREDIT))
                blk = dst[bass.ds(i * 3 + j, 1)].rearrange("b p n -> p b n")
                sp.dma_start(blk[:, :, 0:T_PROMPT], mixed[j][:, 0:T_PROMPT].unsqueeze(1)).then_inc(stored[j], 16)
                sp.dma_start(blk[:, :, T_PROMPT:NT], mixed[j][:, T_PROMPT + PAD:SPAN].unsqueeze(1)).then_inc(stored[j], 16)

            with sp.Fori(0, turns - 1) as i:
                for j in range(3):
                    sp.wait_ge(w_low, 3 * i + j + 1)
                    sp.dma_start(w_raw[j][:, :, :], wv[:, :, bass.ds(i * (3 * P) + (first_col + (3 + j) * P), P)]
                                 ).then_inc(w_loaded[j], 16)
                for j in range(3):
                    store(i, j)
            for j in range(3):
                store(turns - 1, j)
            for j in range(3):
                sp.wait_ge(stored[j], 32 * (turns + 1))

        @block.tensor
        def _(pe):
            with pe.Fori(0, turns) as i:
                for j in range(3):
                    pe.wait_ge(w_low, 3 * i + j + 1)
                    for q, (t0, n) in enumerate(PIECES):
                        pe.wait_ge(copied, 9 * i + 3 * j + q + 1)
                        for k in range(KB):
                            last = product(pe, bank[BANK[3 * j + q]][:, 0:n], both(w[j], slice(None), k),
                                           both(hT, slice(None), k, slice(t0, t0 + n)), k == 0, k == KB - 1)
                        last.then_inc(multiplied, 1)

        @block.gpsimd
        def _(pool):
            with pool.Fori(0, turns) as i:
                for j in range(3):
                    pool.wait_ge(w_high, 3 * i + j + 1)
                    pool.tensor_tensor(w[j][1][:, :, :], w_raw[j][:, :, :], w[j][0][:, :, :].bitcast(F32),
                                       ALU.subtract).then_inc(w_low, 1)

        def silu(act, i, j):
            act.wait_ge(taps_done, 3 * i + j + 1 + CREDIT)
            act.activation(mixed[j][:, :], mixed[j][:, :], ACT.Silu).then_inc(silu_done, 1)

        @block.scalar
        def _(act):
            act.wait_ge(zeroed, 3)
            act.sem_inc(copied, CREDIT)

            def high(i, j):
                act.wait_ge(w_loaded[j], 16 * i + 16)
                act.activation(w[j][0][:, :, :], w_raw[j][:, :, :], ACT.Copy).then_inc(w_high, 1)

            def turn(i, more):
                for j in range(3):
                    act.wait_ge(taps_done, 3 * i + j + 1)
                    for q, (t0, n) in enumerate(PIECES):
                        act.wait_ge(multiplied, 9 * i + 3 * j + q + 1)
                        at = PAD + t0 if q < 2 else PAD + t0 + PAD
                        act.activation(padded[j][:, at:at + n], bank[BANK[3 * j + q]][:, 0:n], ACT.Copy).then_inc(copied, 1)
                    if more:
                        high(i + 1, j)
                    if conv and j > 0:
                        silu(act, i, j - 1)
                if conv:
                    silu(act, i, 2)

            for j in range(3):
                high(0, j)
            with act.Fori(0, turns - 1) as i:
                turn(i, True)
            turn(turns - 1, False)

        @block.vector
        def _(dve):
            dve.sem_inc(taps_done, CREDIT)
            for j in range(3):
                dve.memset(padded[j][:, :], 0.0).then_inc(zeroed, 1)
                dve.sem_inc(stored[j], 32)
            dve.wait_ge(zeroed, 3)
            dve.wait_ge(taps_loaded, 16 * n_in)
            if not conv:
                link = Chain(dve, setup_chain)
                link(dve.tensor_tensor(tap[:, :, 1], raw_tap[:, :, 0], raw_tap[:, :, 1], ALU.add))
                link(dve.tensor_scalar(tap[:, :, 1], tap[:, :, 1], -1.0, 1.0, ALU.mult, ALU.add))
                link(dve.tensor_copy(tap[:, :, 0], raw_tap[:, :, 0]))
                link(dve.tensor_copy(tap[:, :, 2], raw_tap[:, :, 1]))
            with dve.Fori(0, turns) as i:
                link = Chain(dve, dve_chain, i, 3 * (n_taps - 1))
                for j in range(3):
                    dve.wait_ge(copied, 9 * i + 3 * j + 3 + CREDIT)
                    dve.wait_ge(stored[j], 32 * i + 32)
                    b = i * 3 + j
                    out = mixed[j][:, :].unsqueeze(1)
                    for u in range(n_taps):
                        src = padded[j][:, PAD - reach + u:PAD - reach + u + SPAN].unsqueeze(1)
                        c = tap[:, bass.ds(b, 1), u]
                        if u == 0:
                            link(dve.tensor_scalar(out, src, c, None, ALU.mult))
                        elif u < n_taps - 1:
                            link(dve.scalar_tensor_tensor(out, src, c, out, ALU.mult, ALU.add))
                        else:
                            dve.scalar_tensor_tensor(out, src, c, out, ALU.mult, ALU.add).then_inc(taps_done, 1)
                link.done()


def in_proj_tm(nc, E, hT, w_in, gates, z_dst):
    n_ab = 4 * GH
    w_raw = E.sb("w_raw", [P, KB, GW + n_ab])
    w = E.pair("w", [P, KB, GW + n_ab])
    z = [E.sb(f"z{j}", [P, GW]) for j in range(2)]
    bank = E.banks(8)
    w_loaded, w_high, w_low, multiplied, silu_done, ab_done = (
        E.sem(n) for n in ("w_loaded", "w_high", "w_low", "multiplied", "silu_done", "ab_done"))
    stored = [E.sem(f"stored{j}") for j in range(2)]
    with nc.Block() as block:
        @block.sync
        def _(sp):
            sp.dma_start(w_raw[:, :, :], w_in.rearrange("(k p) n -> p k n", p=P)[:, :, 3 * GW:GDN_COLS]).then_inc(w_loaded, 16)
            for t in range(TILES):
                sp.wait_ge(silu_done, t + 1)
                sp.dma_start(z_dst[t], z[t % 2][:, :]).then_inc(stored[t % 2], 16)
            for j in range(2):
                sp.wait_ge(stored[j], 16 * (TILES // 2))

        @block.tensor
        def _(pe):
            for t in range(TILES):
                if t >= 4:
                    pe.wait_ge(silu_done, t - 3)
                    pe.wait_ge(ab_done, t - 3)
                for half, (c0, n) in enumerate(((0, GW), (GW, n_ab))):
                    for k in range(KB):
                        if t + half == 0:
                            pe.wait_ge(w_low, k + 1)
                        last = product(pe, bank[2 * (t % 4) + half][:, 0:n], both(hT, slice(None), k, slice(t * P, (t + 1) * P)),
                                       both(w, slice(None), k, slice(c0, c0 + n)), k == 0, k == KB - 1)
                last.then_inc(multiplied, 1)

        @block.scalar
        def _(act):
            act.wait_ge(w_loaded, 16)
            for k in range(KB):
                act.activation(w[0][:, k, :], w_raw[:, k, :], ACT.Copy).then_inc(w_high, 1)
            for t in range(TILES):
                act.wait_ge(multiplied, t + 1)
                if t >= 2:
                    act.wait_ge(stored[t % 2], 16 * (t // 2))
                act.activation(z[t % 2][:, :], bank[2 * (t % 4)][:, :], ACT.Silu).then_inc(silu_done, 1)

        @block.vector
        def _(dve):
            for k in range(KB):
                dve.wait_ge(w_high, k + 1)
                dve.tensor_tensor(w[1][:, k, :], w_raw[:, k, :], w[0][:, k, :].bitcast(F32), ALU.subtract).then_inc(w_low, 1)
            for t in range(TILES):
                dve.wait_ge(multiplied, t + 1)
                dve.tensor_copy(gates[:, t, :], bank[2 * (t % 4) + 1][:, 0:n_ab]).then_inc(ab_done, 1)
            dve.wait_ge(ab_done, TILES)


def feed_forward(nc, E, hT, acc, w1, w2):
    GB = 2
    GROUPS = D_FF // (GB * P)
    NQ = len(PIECES)
    w1_raw = E.sb("w1_raw", [P, KB, GB * P])
    w2_raw = E.sb("w2_raw", [P, GB, D])
    w1_sb = E.pair("w1", [P, KB, GB * P])
    w2_sb = E.pair("w2", [P, GB, D])
    f = E.pair("f", [P, GB, NT])
    relu = [E.sb(f"relu{j}", [P, 512]) for j in range(2)]
    square = [E.sb(f"square{j}", [P, 512]) for j in range(2)]
    bank = E.banks(8)
    w1_loaded, w2_loaded, w1_high, w1_low, w2_high, w2_low, up_product, relu_done, squared, f_high, f_low, down_product, added, zeroed = (
        E.sem(n) for n in ("w1_loaded", "w2_loaded", "w1_high", "w1_low", "w2_high", "w2_low", "up_product", "relu_done",
                           "squared", "f_high", "f_low", "down_product", "added", "zeroed"))
    w1v = w1.rearrange("(k p) n -> p k n", p=P)
    w2v = w2.rearrange("(b p) n -> p b n", p=P)
    UP = GB * NQ
    DOWN = TILES * 2
    UNITS = [(q, b) for q in range(NQ) for b in range(GB)]
    with nc.Block() as block:
        @block.sync
        def _(sp):
            sp.dma_start(w1_raw[:, :, :], w1v[:, :, 0:GB * P]).then_inc(w1_loaded, 16)
            sp.dma_start(w2_raw[:, :, :], w2v[:, 0:GB, :]).then_inc(w2_loaded, 16)
            with sp.Fori(0, GROUPS - 1) as i:
                sp.wait_ge(w1_low, i + 1)
                sp.dma_start(w1_raw[:, :, :], w1v[:, :, bass.ds((i + 1) * (GB * P), GB * P)]).then_inc(w1_loaded, 16)
                sp.wait_ge(w2_low, i + 1)
                sp.dma_start(w2_raw[:, :, :], w2v[:, bass.ds((i + 1) * GB, GB), :]).then_inc(w2_loaded, 16)

        @block.tensor
        def _(pe):
            with pe.Fori(0, GROUPS) as i:
                pe.wait_ge(w1_low, i + 1)
                for u, (q, b) in enumerate(UNITS):
                    t0, n = PIECES[q]
                    pe.wait_ge(relu_done, UP * i + u + 1)
                    for k in range(KB):
                        last = product(pe, bank[u % 4][:, 0:n], both(w1_sb, slice(None), k, slice(b * P, (b + 1) * P)),
                                       both(hT, slice(None), k, slice(t0, t0 + n)), k == 0, k == KB - 1)
                    last.then_inc(up_product, 1)
                pe.wait_ge(w2_low, i + 1)
                for t in range(TILES):
                    if t % 4 == 0:
                        pe.wait_ge(f_low, UP * i + GB * (t // 4 + 1) + 2)
                    for half in range(2):
                        u = 2 * t + half
                        pe.wait_ge(added, DOWN * i + u + 1)
                        for b in range(GB):
                            last = product(pe, bank[4 + u % 4][:, :], both(f, slice(None), b, slice(t * P, (t + 1) * P)),
                                           both(w2_sb, slice(None), b, slice(half * 512, (half + 1) * 512)),
                                           b == 0, b == GB - 1)
                        last.then_inc(down_product, 1)

        @block.scalar
        def _(act):
            act.sem_inc(relu_done, 4)
            act.sem_inc(squared, 2)
            act.sem_inc(f_low, 2)
            act.wait_ge(w1_loaded, 16)
            act.activation(w1_sb[0][:, :, :], w1_raw[:, :, :], ACT.Copy).then_inc(w1_high, 1)

            def group(i, more):
                def high(u):
                    q, b = UNITS[u]
                    t0, n = PIECES[q]
                    act.wait_ge(squared, UP * i + u + 1 + 2)
                    act.activation(f[0][:, b, t0:t0 + n], square[u % 2][:, 0:n], ACT.Copy).then_inc(f_high, 1)

                act.wait_ge(w2_loaded, 16 * i + 16)
                act.wait_ge(added, DOWN * i + 4)
                act.activation(w2_sb[0][:, :, :], w2_raw[:, :, :], ACT.Copy).then_inc(w2_high, 1)
                for u, (q, b) in enumerate(UNITS):
                    n = PIECES[q][1]
                    act.wait_ge(up_product, UP * i + u + 1)
                    act.wait_ge(squared, UP * i + u + 1)
                    act.activation(relu[u % 2][:, 0:n], bank[u % 4][:, 0:n], ACT.Relu).then_inc(relu_done, 1)
                    if u > 0:
                        high(u - 1)
                high(UP - 1)
                if more:
                    act.wait_ge(w1_loaded, 16 * i + 32)
                    act.activation(w1_sb[0][:, :, :], w1_raw[:, :, :], ACT.Copy).then_inc(w1_high, 1)

            with act.Fori(0, GROUPS - 1) as i:
                group(i, True)
            group(GROUPS - 1, False)

        @block.gpsimd
        def _(pool):
            def w2_split(i):
                pool.wait_ge(w2_high, i + 1)
                pool.tensor_tensor(w2_sb[1][:, :, :], w2_raw[:, :, :], w2_sb[0][:, :, :].bitcast(F32),
                                   ALU.subtract).then_inc(w2_low, 1)

            pool.memset(acc[:, :, :], 0.0).then_inc(zeroed, 1)
            w2_split(0)
            with pool.Fori(0, GROUPS - 1) as i:
                pool.wait_ge(w1_high, i + 2)
                pool.tensor_tensor(w1_sb[1][:, :, :], w1_raw[:, :, :], w1_sb[0][:, :, :].bitcast(F32),
                                   ALU.subtract).then_inc(w1_low, 1)
                w2_split(i + 1)

        @block.vector
        def _(dve):
            dve.sem_inc(added, 4)
            dve.wait_ge(w1_high, 1)
            dve.tensor_tensor(w1_sb[1][:, :, :], w1_raw[:, :, :], w1_sb[0][:, :, :].bitcast(F32),
                              ALU.subtract).then_inc(w1_low, 1)
            dve.wait_ge(zeroed, 1)
            with dve.Fori(0, GROUPS) as i:
                def low(u):
                    q, b = UNITS[u]
                    t0, n = PIECES[q]
                    dve.wait_ge(f_high, UP * i + u + 1)
                    dve.tensor_tensor(f[1][:, b, t0:t0 + n], square[u % 2][:, 0:n], f[0][:, b, t0:t0 + n].bitcast(F32),
                                      ALU.subtract).then_inc(f_low, 1)

                for u, (q, b) in enumerate(UNITS):
                    n = PIECES[q][1]
                    dve.wait_ge(relu_done, UP * i + u + 1 + 4)
                    dve.wait_ge(f_low, UP * i + u + 1)
                    dve.tensor_tensor(square[u % 2][:, 0:n], relu[u % 2][:, 0:n], relu[u % 2][:, 0:n],
                                      ALU.mult).then_inc(squared, 1)
                    if u > 0:
                        low(u - 1)
                low(UP - 1)
                for u in range(DOWN):
                    dve.wait_ge(down_product, DOWN * i + u + 1)
                    a = acc[:, u // 2, (u % 2) * 512:(u % 2 + 1) * 512]
                    dve.tensor_tensor(a, a, bank[4 + u % 4][:, :], ALU.add).then_inc(added, 1)
                dve.wait_ge(added, DOWN * i + DOWN + 4)


def gdn_rates(nc, E, ins, gates, rates, eps):
    incl = [E.sb(f"incl{d}", [P, P]) for d in range(2)]
    excl = [E.sb(f"excl{d}", [P, P]) for d in range(2)]
    ones = E.sb("ones", [P, P])
    a_log, dt = E.sb("a_log", [P, 2 * GH]), E.sb("dt", [P, 2 * GH])
    a, b, c = (E.sb(n, [P, TILES, 2 * GH]) for n in ("a", "b", "c"))
    bank = E.banks(8)
    loaded, dve_chain, act_chain, to_act, to_dve, summed = (
        E.sem(n) for n in ("loaded", "dve_chain", "act_chain", "to_act", "to_dve", "summed"))
    n_th = TILES * GH
    with nc.Block() as block:
        @block.sync
        def _(sp):
            for d in range(2):
                sp.dma_start(incl[d][:, :], ins["c_incl"][d]).then_inc(loaded, 16)
                sp.dma_start(excl[d][:, :], ins["c_excl"][d]).then_inc(loaded, 16)
            sp.dma_start(ones[:, :], ins["c_ones"]).then_inc(loaded, 16)
            sp.dma_start(a_log[:, :], ins["gdn_A_log"].rearrange("n d h -> (n d h)").partition_broadcast(P)).then_inc(loaded, 16)
            sp.dma_start(dt[:, :], ins["gdn_dt_bias"].rearrange("n d h -> (n d h)").partition_broadcast(P)).then_inc(loaded, 16)

        @block.vector
        def _(dve):
            link = Chain(dve, dve_chain)
            dve.wait_ge(loaded, 16 * 7)
            link(dve.tensor_tensor(c[:, :, :], gates[:, :, 0:2 * GH], bcm(dt[:, :], TILES), ALU.add))
            link(dve.tensor_scalar(a[:, :, :], c[:, :, :], 0.0, None, ALU.max))
            link(dve.tensor_scalar(b[:, :, :], c[:, :, :], 0.0, None, ALU.min))
            dve.tensor_tensor(b[:, :, :], b[:, :, :], a[:, :, :], ALU.subtract).then_inc(to_act, 1)
            dve.wait_ge(to_dve, 1)
            link(dve.tensor_tensor(a[:, :, :], a[:, :, :], b[:, :, :], ALU.add))
            link(dve.scalar_tensor_tensor(a[:, :, :], a[:, :, :], -1.0, bcm(a_log[:, :], TILES), ALU.mult, ALU.mult))
            for d in range(2):
                dve.tensor_copy(rates["g"][d][:, :, :], a[:, :, d * GH:(d + 1) * GH]).then_inc(to_act, 1)
            dve.wait_ge(to_dve, 2)
            link(dve.reciprocal(c[:, :, :], c[:, :, :]))
            for d in range(2):
                link(dve.tensor_copy(rates["beta"][d][:, :, :], c[:, :, d * GH:(d + 1) * GH]))
                link(dve.tensor_scalar(rates["neg_beta"][d][:, :, :], c[:, :, d * GH:(d + 1) * GH], -1.0, None, ALU.mult))
            for d in range(2):
                dve.wait_ge(summed, 3 * d + 3)
                link(dve.tensor_copy(rates["G"][d][:, :, :], bank[3 * d][:, 0:n_th].rearrange("p (t h) -> p t h", h=GH)))

        @block.scalar
        def _(act):
            link = Chain(act, act_chain)
            act.wait_ge(loaded, 16 * 7)
            link(act.activation(a_log[:, :], a_log[:, :], ACT.Exp))
            act.wait_ge(to_act, 1)
            link(act.activation(b[:, :, :], b[:, :, :], ACT.Exp))
            act.activation(b[:, :, :], b[:, :, :], ACT.Ln, bias=ones[:, 0:1]).then_inc(to_dve, 1)
            act.wait_ge(to_act, 3)
            link(act.activation(c[:, :, :], gates[:, :, 2 * GH:4 * GH], ACT.Exp, scale=-1.0))
            act.activation(c[:, :, :], c[:, :, :], ACT.Identity, bias=ones[:, 0:1]).then_inc(to_dve, 1)
            for d in range(2):
                act.wait_ge(summed, 3 * d + 3)
                act.wait_ge(dve_chain, 11 + d)
                for u, name in enumerate(("exp_G", "exp_rest", "exp_last")):
                    link(act.activation(rates[name][d][:, :, :],
                                        bank[3 * d + u][:, 0:n_th].rearrange("p (t h) -> p t h", h=GH), ACT.Exp))

        @block.tensor
        def _(pe):
            for d in range(2):
                pe.wait_ge(to_act, 2 + d)
                g = rates["g"][d][:, :, :].rearrange("p t h -> p (t h)")
                for u, sums in enumerate((incl[d], excl[1 - d], ones)):
                    pe.matmul(bank[3 * d + u][:, 0:n_th], sums[:, :], g, start=True, stop=True).then_inc(summed, 1)


def prepare_tokens(nc, E, ins, ident, eps, conv_fm, shift_fm, fm_both, fm_dir, tm_both, tm_dir):
    def two(name, shape):
        return [E.sb(f"{name}_{j}", shape) for j in range(2)]

    qkv = two("qkv", [P, CONV_BLOCKS, P])
    rk = two("rk", [P, RWKV_BLOCKS, P])
    squares = two("squares", [P, 3 * GH, P])
    root = two("root", [NORMS, P])
    fb = two("fb", [P, 3, GH, P])
    fd = [two(f"fd{d}", [P, 2, RB, P]) for d in range(2)]
    tb = two("tb", [P, 5, GW])
    td = [two(f"td{d}", [P, RW]) for d in range(2)]
    a = [two(f"a{d}", [P, RB, P]) for d in range(2)]
    kk_raw, k_a_part, k_rest, r_weighed, rksum = (
        two(n, [P, RB, P]) for n in ("kk_raw", "k_a_part", "k_rest", "r_weighed", "rksum"))
    th, sg = two("th", [P, P]), two("sg", [P, P])
    ones, head_cols = E.sb("ones", [P, P]), E.sb("head_cols", [P, 2])
    norm_cols, norm_rows = E.sb("norm_cols", [P, 3 * GH, NORMS]), E.sb("norm_rows", [NORMS, 3 * GH, P])
    w2, a2, g2 = (E.sb(n, [P, RW]) for n in ("w2", "a2", "g2"))
    w0 = E.sb("w0", [1, 2 * RW])
    a0 = [E.sb(f"a_bias{d}", [P, RB]) for d in range(2)]
    k_k, k_a, r_k, one_ka = (E.sb(n, [P, RB]) for n in ("k_k", "k_a", "r_k", "one_ka"))
    banks = E.banks(8)
    names = ("params", "setup", "turned", "a_product", "from_k", "squared", "low", "turned_out", "a_out", "sums", "rooted",
             "inverse", "spread", "gate_product", "gate_out", "normal", "b_out", "bonus_in", "w_product", "w_out",
             "k_turned", "k_out", "bonus_product", "bonus_out", "dve_chain", "tick")
    s = {n: E.sem(n) for n in names}
    loaded = [E.sem(f"loaded{j}") for j in range(2)]
    stored = [E.sem(f"stored{j}") for j in range(2)]
    STORES = 16 * 6
    PARAMS = 16 * 13
    FREE = 2
    TURNS = TILES // 2

    def bank(j, u):
        return banks[4 * j + u]

    def blocks(ap):
        return ap.rearrange("p (b n) -> p b n", n=P)

    def fm_vec(v):
        return v.rearrange("(b p) -> p b", p=P)

    def row(dram, t):
        return dram[bass.ds(t, 1)].rearrange("o p n -> p o n")

    with nc.Block() as block:
        @block.sync
        def _(sp):
            def load(i, j):
                t = 2 * i + j
                sp.dma_start(qkv[j][:, :, :], conv_fm.rearrange("b p n -> p b n")[:, :, bass.ds(t * P, P)]).then_inc(loaded[j], 16)
                sp.dma_start(rk[j][:, :, :], shift_fm.rearrange("b p n -> p b n")[:, :, bass.ds(t * P, P)]).then_inc(loaded[j], 16)

            for j in range(2):
                load(0, j)
            for dst, src in ((ones, ins["c_ones"]), (head_cols, ins["c_head_cols"]),
                             (w2, ins["rwkv_w2"][0].rearrange("d l c -> (d l) c")),
                             (a2, ins["rwkv_a2"][0].rearrange("d l c -> (d l) c")), (g2, ins["rwkv_g2"][0]),
                             (w0, ins["rwkv_w0"].rearrange("n d c -> n (d c)"))):
                sp.dma_start(dst[:, :], src).then_inc(s["params"], 16)
            sp.dma_start(norm_cols[:, :, :], ins["c_norm_cols"]).then_inc(s["params"], 16)
            sp.dma_start(norm_rows[:, :, :], ins["c_norm_rows"]).then_inc(s["params"], 16)
            for dst, src in ((a0[0], ins["rwkv_a0"][0][0]), (a0[1], ins["rwkv_a0"][0][1]), (k_k, ins["rwkv_k_k"][0]), (k_a, ins["rwkv_k_a"][0]),
                             (r_k, ins["rwkv_r_k"][0].rearrange("h n -> (h n)"))):
                sp.dma_start(dst[:, :], fm_vec(src), allow_slow_non_contiguous=True).then_inc(s["params"], 16)

            def wait(name, value):
                sp.wait_ge(s[name], value)
                sp.sem_inc(s["tick"], 1)

            def reload(i, j):
                n = 2 * i + j
                wait("normal", 3 * n + 3)
                wait("low", 2 * n + 2)
                wait("from_k", 4 * n + 4)
                load(i + 1, j)

            def store(i, j):
                n = 2 * i + j
                for name, per_tile in (("turned_out", 2), ("gate_out", 1), ("w_out", 2)):
                    wait(name, per_tile * n + per_tile)
                wait("k_out", n + 1 + FREE)
                wait("b_out", 2 * n + 2 + 2 * FREE)
                wait("bonus_in", n + 1 + FREE)
                wait("bonus_out", n + 1 + FREE)
                sp.dma_start(row(fm_both, n), fb[j][:, :, :, :].rearrange("p a b n -> p (a b n)").unsqueeze(1)).then_inc(stored[j], 16)
                sp.dma_start(row(tm_both, n), tb[j][:, :, :].rearrange("p a n -> p (a n)").unsqueeze(1)).then_inc(stored[j], 16)
                for d in range(2):
                    sp.dma_start(row(fm_dir[d], n), fd[d][j][:, :, :, :].rearrange("p a b n -> p (a b n)").unsqueeze(1)
                                 ).then_inc(stored[j], 16)
                    sp.dma_start(row(tm_dir[d], n), td[d][j][:, :].unsqueeze(1)).then_inc(stored[j], 16)

            with sp.Fori(0, TURNS - 1) as i:
                for j in range(2):
                    reload(i, j)
                for j in range(2):
                    store(i, j)
            for j in range(2):
                store(TURNS - 1, j)
            for j in range(2):
                sp.wait_ge(stored[j], STORES * (TURNS + 1))

        @block.tensor
        def _(pe):
            pe.wait_ge(s["params"], PARAMS)
            with pe.Fori(0, TURNS) as i:
                for j in range(2):
                    n = 2 * i + j
                    pe.wait_ge(loaded[j], 32 * i + 32)
                    pe.wait_ge(s["bonus_out"], n + 1)
                    pe.wait_ge(s["k_out"], n + 1)
                    for k in range(GH):
                        pe.transpose(bank(j, 0)[:, k * P:(k + 1) * P], qkv[j][:, 2 * GH + k, :], ident[:, :])
                    for k in range(RB):
                        last = pe.transpose(bank(j, 1)[:, k * P:(k + 1) * P], rk[j][:, 2 * RB + k, :], ident[:, :])
                    last.then_inc(s["turned"], 1)
                    for d in range(2):
                        for k in range(RB):
                            last = pe.matmul(bank(j, 2 + d)[:, k * P:(k + 1) * P], a2[64 * d:64 * d + 64, k * P:(k + 1) * P],
                                             rk[j][64 * d:64 * d + 64, 13, :], start=True, stop=True)
                    last.then_inc(s["a_product"], 1)
                for j in range(2):
                    n = 2 * i + j
                    pe.wait_ge(s["squared"], 2 * n + 2)
                    pe.wait_ge(s["a_out"], 2 * n + 2)
                    for b in range(3 * GH):
                        last = pe.matmul(bank(j, 3)[0:NORMS, 0:P], norm_cols[:, b, :], squares[j][:, b, :],
                                         start=(b == 0), stop=(b == 3 * GH - 1))
                    last.then_inc(s["sums"], 1)
                for j in range(2):
                    n = 2 * i + j
                    pe.wait_ge(s["inverse"], n + 1)
                    pe.wait_ge(s["turned_out"], 2 * n + 2)
                    for b in range(3 * GH):
                        last = pe.matmul(bank(j, b // GH)[:, (b % GH) * P:(b % GH + 1) * P], norm_rows[:, b, :],
                                         root[j][:, :], start=True, stop=True)
                    last.then_inc(s["spread"], 1)
                    pe.wait_ge(s["low"], 2 * n + 2)
                    pe.matmul(bank(j, 3)[:, :], sg[j][:, :], g2[:, :], start=True, stop=True).then_inc(s["gate_product"], 1)
                for j in range(2):
                    n = 2 * i + j
                    pe.wait_ge(s["normal"], 3 * n + 3)
                    for d in range(2):
                        pe.matmul(bank(j, d)[:, :], th[j][64 * d:64 * d + 64, :], w2[64 * d:64 * d + 64, :], start=True, stop=False)
                        last = pe.matmul(bank(j, d)[:, :], ones[0:1, :], w0[0:1, d * RW:(d + 1) * RW], start=False, stop=True)
                    last.then_inc(s["w_product"], 1)
                    for k in range(GH):
                        last = pe.transpose(bank(j, 2)[:, k * P:(k + 1) * P], fb[j][:, 0, k, :], ident[:, :])
                    last.then_inc(s["k_turned"], 1)
                for j in range(2):
                    n = 2 * i + j
                    pe.wait_ge(s["bonus_in"], n + 1 + FREE)
                    pe.wait_ge(s["gate_out"], n + 1)
                    for k in range(RB):
                        last = pe.matmul(bank(j, 3)[:, 2 * k:2 * k + 2], rksum[j][:, k, :], head_cols[:, :], start=True, stop=True)
                    last.then_inc(s["bonus_product"], 1)

        @block.scalar
        def _(act):
            act.wait_ge(s["setup"], 2)
            act.wait_ge(s["params"], PARAMS)
            with act.Fori(0, TURNS) as i:
                for j in range(2):
                    n = 2 * i + j
                    act.wait_ge(loaded[j], 32 * i + 32)
                    act.activation(squares[j][:, 0:2 * GH, :], qkv[j][:, 0:2 * GH, :], ACT.Square).then_inc(s["squared"], 1)
                    act.wait_ge(s["turned"], n + 1)
                    act.wait_ge(stored[j], STORES * i + STORES)
                    for u in range(2):
                        act.activation(tb[j][:, 1 + u, :], bank(j, u)[:, :], ACT.Copy).then_inc(s["turned_out"], 1)
                    act.wait_ge(s["from_k"], 4 * n + 1)
                    act.activation(squares[j][:, 2 * GH:3 * GH, :], kk_raw[j][:, :, :], ACT.Square).then_inc(s["squared"], 1)
                for j in range(2):
                    n = 2 * i + j
                    act.activation(th[j][:, :], rk[j][:, 12, :], ACT.Tanh).then_inc(s["low"], 1)
                    act.activation(sg[j][:, :], rk[j][:, 14, :], ACT.Sigmoid).then_inc(s["low"], 1)
                    act.wait_ge(s["a_product"], n + 1)
                    act.wait_ge(s["bonus_in"], n + 1)
                    act.wait_ge(s["b_out"], 2 * n + 2)
                    for d in range(2):
                        for k in range(RB):
                            last = act.activation(a[d][j][:, k, :], bank(j, 2 + d)[:, k * P:(k + 1) * P], ACT.Sigmoid,
                                                  bias=a0[d][:, k:k + 1])
                        last.then_inc(s["a_out"], 1)
                for j in range(2):
                    act.wait_ge(s["sums"], 2 * i + j + 1)
                    act.activation(root[j][:, :], bank(j, 3)[0:NORMS, 0:P], ACT.Sqrt, bias=eps[0:NORMS, :]).then_inc(s["rooted"], 1)
                for j in range(2):
                    act.wait_ge(s["gate_product"], 2 * i + j + 1)
                    act.activation(tb[j][:, 3, :], bank(j, 3)[:, :], ACT.Copy).then_inc(s["gate_out"], 1)
                for j in range(2):
                    act.wait_ge(s["w_product"], 2 * i + j + 1)
                    for d in range(2):
                        act.activation(td[d][j][:, :], bank(j, d)[:, :], ACT.Sigmoid).then_inc(s["w_out"], 1)
                    act.wait_ge(s["k_turned"], 2 * i + j + 1)
                    act.activation(tb[j][:, 0, :], bank(j, 2)[:, :], ACT.Copy).then_inc(s["k_out"], 1)

        @block.gpsimd
        def _(pool):
            pool.wait_ge(s["params"], PARAMS)
            pool.wait_ge(s["setup"], 2)
            with pool.Fori(0, TURNS) as i:
                for j in range(2):
                    pool.wait_ge(loaded[j], 32 * i + 32)
                    pool.wait_ge(s["bonus_in"], 2 * i + j + 1)
                    r, k = rk[j][:, 0:RB, :], rk[j][:, RB:2 * RB, :]
                    for dst, src, weight in ((kk_raw, k, k_k), (k_a_part, k, k_a), (k_rest, k, one_ka), (r_weighed, r, r_k)):
                        pool.tensor_tensor(dst[j][:, :, :], src, bc(weight[:, :], P), ALU.mult).then_inc(s["from_k"], 1)
                for j in range(2):
                    pool.wait_ge(s["normal"], 6 * i + 3 * j + 3)
                    pool.wait_ge(s["a_out"], 4 * i + 2 * j + 2)
                    for d in range(2):
                        pool.tensor_tensor(fd[d][j][:, 0, :, :], fb[j][:, 2, :, :], a[d][j][:, :, :], ALU.mult).then_inc(s["b_out"], 1)

        @block.vector
        def _(dve):
            dve.memset(eps[:, :], EPS).then_inc(s["setup"], 1)
            dve.wait_ge(s["params"], PARAMS)
            dve.tensor_scalar(one_ka[:, :], k_a[:, :], -1.0, 1.0, ALU.mult, ALU.add).then_inc(s["setup"], 1)
            dve.sem_inc(s["bonus_in"], FREE)
            dve.sem_inc(s["bonus_out"], FREE)
            dve.sem_inc(s["b_out"], 2 * FREE)
            dve.sem_inc(s["k_out"], FREE)
            for j in range(2):
                dve.sem_inc(stored[j], STORES)
            with dve.Fori(0, TURNS) as i:
                link = Chain(dve, s["dve_chain"], i, 10)
                for j in range(2):
                    dve.wait_ge(s["rooted"], 2 * i + j + 1)
                    dve.reciprocal(root[j][:, :], root[j][:, :]).then_inc(s["inverse"], 1)
                for j in range(2):
                    dve.wait_ge(s["spread"], 2 * i + j + 1)
                    dve.wait_ge(stored[j], STORES * i + STORES)
                    dve.scalar_tensor_tensor(fb[j][:, 1, :, :], qkv[j][:, 0:GH, :], GD ** -0.5, blocks(bank(j, 0)[:, :]),
                                             ALU.mult, ALU.mult).then_inc(s["normal"], 1)
                    dve.tensor_tensor(fb[j][:, 0, :, :], qkv[j][:, GH:2 * GH, :], blocks(bank(j, 1)[:, :]),
                                      ALU.mult).then_inc(s["normal"], 1)
                    dve.tensor_tensor(fb[j][:, 2, :, :], kk_raw[j][:, :, :], blocks(bank(j, 2)[:, :]),
                                      ALU.mult).then_inc(s["normal"], 1)
                for j in range(2):
                    dve.wait_ge(s["from_k"], 8 * i + 4 * j + 4)
                    dve.wait_ge(s["a_out"], 4 * i + 2 * j + 2)
                    for d in range(2):
                        k_dir = fd[d][j][:, 1, :, :]
                        link(dve.tensor_tensor(k_dir, a[d][j][:, :, :], k_a_part[j][:, :, :], ALU.mult))
                        link(dve.tensor_tensor(k_dir, k_dir, k_rest[j][:, :, :], ALU.add))
                    link(dve.tensor_tensor(rksum[j][:, :, :], fd[0][j][:, 1, :, :], fd[1][j][:, 1, :, :], ALU.add))
                    dve.tensor_tensor(rksum[j][:, :, :], rksum[j][:, :, :], r_weighed[j][:, :, :], ALU.mult).then_inc(s["bonus_in"], 1)
                for j in range(2):
                    dve.wait_ge(s["bonus_product"], 2 * i + j + 1)
                    dve.wait_ge(s["turned_out"], 4 * i + 2 * j + 2)
                    dve.tensor_tensor(tb[j][:, 4, :].rearrange("p (h n) -> p h n", h=RH),
                                      tb[j][:, 2, :].rearrange("p (h n) -> p h n", h=RH), bc(bank(j, 3)[:, 0:RH], RN),
                                      ALU.mult).then_inc(s["bonus_out"], 1)
                link.done()


def mix_scopes(nc, phase, dram, ins, acc, gates, ident, conv_fm, shift_fm, z_tm, stop):
    fm_both = dram("fm_both", [TILES, P, 3 * GW])
    fm_dir = [dram(f"fm_dir{d}", [TILES, P, 2 * RW]) for d in range(2)]
    tm_both = dram("tm_both", [TILES, P, 5 * GW])
    tm_dir = [dram(f"tm_dir{d}", [TILES, P, RW]) for d in range(2)]
    with ExitStack() as own:
        def sb(name, shape):
            return own.enter_context(nc.sbuf_tensor(name, shape, F32))
        eps = sb("eps", [P, 1])
        rates = {n: [sb(f"rate_{n}{d}", [P, TILES, GH]) for d in range(2)]
                 for n in ("g", "beta", "neg_beta", "G", "exp_G", "exp_rest", "exp_last")}
        phase("prepare", prepare_tokens, ins, ident, eps, conv_fm, shift_fm, fm_both, fm_dir, tm_both, tm_dir)
        phase("rates", gdn_rates, ins, gates, rates, eps)
        if stop > 2:
            phase("scan", recurrences, ins, ident, rates, shift_fm, fm_both, fm_dir, tm_both, tm_dir, acc)
        if stop > 3:
            phase("gate", gate_outputs, ins, acc, z_tm, tm_both)
            if stop > 4:
                phase("out0", project_out, ident, acc, ins["w_out_even"][0])


def recurrences(nc, E, ins, ident, rates, shift_fm, fm_both, fm_dir, tm_both, tm_dir, out):
    G, GR = 6, 4
    direction = [0, 1, 0, 0, 1, 1]
    width = [P, P, RN, RN, RN, RN]
    NT_ = [E.sb(f"NT{g}", [P, GR, P]) for g in range(G)]
    X = [E.sb(f"X{g}", [P, GR, P]) for g in range(G)]
    XT = [E.sb(f"XT{g}", [P, GR, P]) for g in range(G)]
    NM = [E.sb(f"NM{g}", [P, GR, P]) for g in range(2)]
    Y = [E.sb(f"Y{g}", [P, GR, P]) for g in range(2)]
    A_o = [E.sb(f"A_o{g}", [P, GR, P]) for g in range(G)]
    A_v = [None, None] + [E.sb(f"A_v{g}", [P, GR, P]) for g in range(2, G)]
    A_ov = [None, None] + [E.sb(f"A_ov{g}", [P, GR, P]) for g in range(2, G)]
    fb = [E.sb(f"fb{d}", [P, 3, GH, P]) for d in range(2)]
    rr = [E.sb(f"r{d}", [P, RB, P]) for d in range(2)]
    fd = [E.sb(f"fd{d}", [P, 2, RB, P]) for d in range(2)]
    tb = [E.sb(f"tb{d}", [P, 3, GW]) for d in range(2)]
    td = [E.sb(f"td{d}", [P, RW]) for d in range(2)]
    AR = [E.sb(f"AR{d}", [P, RB, 2, P]) for d in range(2)]
    BK = [E.sb(f"BK{d}", [P, 2, RW]) for d in range(2)]
    ends = [E.sb(f"ends{d}", [P, RB, 2]) for d in range(2)]
    S_g = [E.sb(f"S_g{d}", [P, GH, P]) for d in range(2)]
    S_r = [E.sb(f"S_r{d}", [P, RB, 2, RN]) for d in range(2)]
    rest = [E.sb(f"rest{d}", [P, RB, 2]) for d in range(2)]
    head_cols = E.sb("head_cols", [P, 2])
    e_inc, e_exc, e_neg = (E.sb(n, [P, RB, P]) for n in ("e_inc", "e_exc", "e_neg"))
    grow, decay = E.sb("grow", [P, GH, P]), E.sb("decay", [P, GH, P])
    BT, KT = Y, NM
    KD = [e_inc, e_exc]
    R = [NT_[g][:, :, 0:width[g]] for g in range(G)]
    U = [X[g][:, :, 0:width[g]] for g in range(G)]
    incl = [E.sb(f"incl{d}", [P, P]) for d in range(2)]
    excl = [E.sb(f"excl{d}", [P, P]) for d in range(2)]
    outside = [E.sb(f"outside{d}", [P, P]) for d in range(2)]
    sums = [E.sb(f"sums{d}", [P, 2 * P]) for d in range(2)]
    end_sums = [E.sb(f"end_sums{d}", [P, 2]) for d in range(2)]
    keep = [E.sb(f"keep{d}", [P, TILES]) for d in range(2)]
    levels = [E.sb(f"levels{d}", [P, LEVELS, P]) for d in range(2)]
    ones = E.sb("ones", [P, P])
    ps = E.stack.enter_context(nc.psum_tensor(f"{E.tag}_ps", [P, 8, 512], F32))
    zeros = E.sb("zeros", [P, GR * P // 2])
    UNITS = (LEVELS - 1) * G
    ORDER = (0, 1, 2, 4, 3, 5)
    FREE = 2
    PER_DVE = 49

    names = ("consts", "cleared", "g_rows", "g_sums", "g_shift", "g_decay", "gram", "gram_used", "w_sums", "w_exp",
             "w_used", "turned", "turned_out", "b_pairs", "k_pairs", "b_pairs_used", "k_pairs_used", "x_first", "masked", "x_turned", "x_out",
             "y_product", "y_cleared", "y_out", "z_product", "x_joined", "joined", "zeroed", "state_scaled", "right", "right_g", "right_r", "solved",
             "u_g", "u_r", "outs", "outs_used", "g_state", "turn_done", "kdec", "dve_chain", "pool_chain", "act_chain",
             "pool_tick")
    s = {n: E.sem(n) for n in names}
    early = [E.sem(f"early{d}") for d in range(2)]
    late = [E.sem(f"late{d}") for d in range(2)]

    def head_of(half, slot):
        return 4 * half + 2 * (slot % 2) + slot // 2

    def tile(d, i):
        return i if d == 0 else i * -1 + (TILES - 1)

    def heads(ap, n=P):
        return ap.rearrange("p (h n) -> p h n", n=n)

    def pairs_view(b):
        return ps[:, b:b + 2, :].rearrange("p b (h a n) -> p (b h) a n", h=2, a=2)

    def pair_slots(g, pair):
        return ps[:, g, 0:4 * RN].rearrange("p (a b n) -> p b a n", a=2, n=RN)[:, pair, :, :]

    def rate(name, d, t):
        return bc(rates[name][d][:, bass.ds(t, 1), :].rearrange("p o h -> p (o h)"), P)

    def unit(u):
        m, at = divmod(u, G)
        assert direction[ORDER[at]] == at % 2
        return m + 1, ORDER[at], at % 2

    def all_heads(ap):
        return ap[:, :, :].rearrange("p h n -> p (h n)")

    def half_of(ap, m, side):
        return ap.rearrange("p (a b n) -> p a b n", b=2, n=1 << m)[:, :, side, :]

    def newly_zero(ap, m, d):
        if m == 1:
            return half_of(ap, m, 1 - d)
        return ap.rearrange("p (a b c n) -> p a b c n", b=2, c=2, n=1 << (m - 1))[:, :, 1 - d, d, :]

    def compact(b, h, m, n_heads=GR):
        return ps[:, b, h * P // 2:(h + n_heads) * P // 2].rearrange("p (a n) -> p a n", n=1 << m)

    with nc.Block() as block:
        @block.sync
        def _(sp):
            for dst, name in ((incl, "c_incl"), (excl, "c_excl"), (outside, "c_outside"), (sums, "c_decay_sums"),
                              (end_sums, "c_decay_ends"), (keep, "c_keep")):
                for d in range(2):
                    sp.dma_start(dst[d][:, :], ins[name][d]).then_inc(s["consts"], 16)
            for d in range(2):
                sp.dma_start(levels[d][:, :, :], ins["c_levels"][d].rearrange("m s t -> s m t")).then_inc(s["consts"], 16)
            sp.dma_start(ones[:, :], ins["c_ones"]).then_inc(s["consts"], 16)
            sp.dma_start(head_cols[:, :], ins["c_head_cols"]).then_inc(s["consts"], 16)

            def load_early(d, i):
                t = tile(d, i)
                sp.dma_start(rr[d][:, :, :], shift_fm.rearrange("b p n -> p b n")[:, 0:RB, bass.ds(t * P, P)]).then_inc(early[d], 16)
                sp.dma_start(fd[d][:, :, :, :].rearrange("p a b n -> p (a b n)").unsqueeze(1),
                             fm_dir[d][bass.ds(t, 1)].rearrange("o p n -> p o n")).then_inc(early[d], 16)
                sp.dma_start(td[d][:, :].unsqueeze(1), tm_dir[d][bass.ds(t, 1)].rearrange("o p n -> p o n")).then_inc(early[d], 16)

            def load_late(d, i):
                t = tile(d, i)
                sp.dma_start(fb[d][:, :, :, :].rearrange("p a b n -> p (a b n)").unsqueeze(1),
                             fm_both[bass.ds(t, 1)].rearrange("o p n -> p o n")).then_inc(late[d], 16)
                sp.dma_start(tb[d][:, :, :].rearrange("p a n -> p (a n)").unsqueeze(1),
                             tm_both[bass.ds(t, 1)].rearrange("o p n -> p o n")[:, :, 0:3 * GW]).then_inc(late[d], 16)

            for d in range(2):
                load_late(d, 0)
                load_early(d, 0)
            with sp.Fori(0, TILES - 1) as i:
                for d in range(2):
                    sp.wait_ge(s["w_used"], 2 * i + d + 1)
                    load_early(d, i + 1)
                sp.wait_ge(s["kdec"], 2 * i + 2)
                sp.wait_ge(s["outs"], G * i + G)
                for d in range(2):
                    load_late(d, i + 1)

        @block.tensor
        def _(pe):
            pe.wait_ge(s["consts"], 16 * 16)
            with pe.Fori(0, TILES) as i:
                pe.wait_ge(s["outs_used"], G * i + G)
                for d in range(2):
                    pe.wait_ge(s["g_rows"], 2 * i + d + 1)
                    if d == 1:
                        pe.wait_ge(s["g_shift"], 2 * i + 1)
                    pe.matmul(ps[:, 0, :], ones[:, :], grow[:, :, :], start=True, stop=True).then_inc(s["g_sums"], 1)
                    pe.wait_ge(late[d], 32 * i + 32)
                    for h in range(GH):
                        last = pe.matmul(ps[:, 1 + 2 * d + h // 2, (h % 2) * 256:(h % 2) * 256 + 256], fb[d][:, 0, h, :],
                                         fb[d][:, 0:2, h, :], start=True, stop=True)
                    last.then_inc(s["gram"], 1)
                for d in range(2):
                    pe.wait_ge(early[d], 48 * i + 48)
                    if d == 0:
                        pe.wait_ge(s["turn_done"], i + 1)
                    if d == 1:
                        pe.wait_ge(s["w_exp"], 2 * i + 1)
                    for k in range(RB):
                        pe.matmul(ps[:, 5 + k // 2, (k % 2) * 256:(k % 2) * 256 + 256], td[d][:, k * P:(k + 1) * P],
                                  sums[d][:, :], start=True, stop=True)
                    for k in range(RB):
                        last = pe.matmul(ps[:, 7, 2 * k:2 * k + 2], td[d][:, k * P:(k + 1) * P], end_sums[d][:, :],
                                         start=True, stop=True)
                    last.then_inc(s["w_sums"], 1)
                for d in range(2):
                    pe.wait_ge(s["w_used"], 2 * i + d + 1)
                    if d == 0:
                        pe.wait_ge(s["w_exp"], 2 * i + 2)
                        pe.wait_ge(s["gram_used"], 2 * i + 2)
                    else:
                        pe.wait_ge(s["turned_out"], 4 * i + 2)
                    for u, src in enumerate((BT[d], KT[d])):
                        for k in range(RB):
                            last = pe.transpose(ps[:, 5 + u, k * P:(k + 1) * P], src[:, k, :], ident[:, :])
                        last.then_inc(s["turned"], 1)
                    for half in range(2):
                        for u, (src, made, used) in enumerate(((BT[d], "b_pairs", "b_pairs_used"),
                                                               (KT[d], "k_pairs", "k_pairs_used"))):
                            if d + half > 0:
                                pe.wait_ge(s[used], 4 * i + 2 * d + half)
                            for h in range(GR):
                                head = head_of(half, h)
                                base = RN * (head % 2)
                                last = pe.matmul(ps[:, 1 + 2 * u + h // 2, (h % 2) * 256:(h % 2) * 256 + 256],
                                                 src[base:base + RN, head // 2, :], AR[d][base:base + RN, head // 2, :, :],
                                                 start=True, stop=True)
                            last.then_inc(s[made], 1)
                def turn_x(g):
                    pe.wait_ge(s["x_first"], G * i + g + 1)
                    if g >= 2:
                        pe.wait_ge(s["x_out"], G * i + g - 1)
                    for h in range(GR):
                        last = pe.transpose(ps[:, g % 2, h * P:(h + 1) * P], XT[g][:, h, :], ident[:, :])
                    last.then_inc(s["x_turned"], 1)

                def y(u):
                    m, g, d = unit(u)
                    if m == 1:
                        pe.wait_ge(s["x_out"], G * i + G)
                    else:
                        pe.wait_ge(s["joined"], UNITS * i + u - G + 1 + FREE)
                    pe.wait_ge(s["masked"], UNITS * i + u + 1)
                    for h in range(GR):
                        last = pe.matmul(compact(2 + d, h, m, 1), NM[d][:, h, :], half_of(X[g][:, h, :], m, d), start=True, stop=True)
                    last.then_inc(s["y_product"], 1)

                def z(u):
                    m, g, d = unit(u)
                    pe.wait_ge(s["y_out"], UNITS * i + u + 1)
                    pe.wait_ge(s["joined"], UNITS * i + u + 1)
                    for h in range(GR):
                        last = pe.matmul(compact(4 + d, h, m, 1), Y[d][:, h, :], half_of(XT[g][:, h, :], m, 1 - d), start=True, stop=True)
                    if m < LEVELS - 1:
                        for h in range(GR):
                            last = pe.matmul(compact(4 + d, GR + h, m, 1), XT[g][:, h, :], half_of(Y[d][:, h, :], m, d),
                                             start=True, stop=True)
                    last.then_inc(s["z_product"], 1)

                pe.wait_ge(s["k_pairs_used"], 4 * i + 4)
                pe.wait_ge(s["turned_out"], 4 * i + 4)
                for g in range(G):
                    turn_x(g)
                y(0)
                for u in range(1, UNITS):
                    y(u)
                    z(u - 1)
                z(UNITS - 1)
                pe.wait_ge(s["joined"], UNITS * i + UNITS + FREE)
                pe.wait_ge(s["state_scaled"], i + 1)
                for g in range(G):
                    d, half = direction[g], g % 2
                    if g < 2:
                        for h in range(GR):
                            last = pe.matmul(ps[:, g, h * P:(h + 1) * P], fb[d][:, 0, h, :], S_g[d][:, h, :],
                                             start=True, stop=True)
                    else:
                        for pair in range(2):
                            pe.matmul(pair_slots(g, pair), AR[d][:, 2 * half + pair, 0, :], S_r[d][:, 2 * half + pair, :, :],
                                      start=True, stop=False)
                            for h in (pair, 2 + pair):
                                head = head_of(half, h)
                                last = pe.matmul(ps[:, g, h * RN:(h + 1) * RN], A_v[g][:, h, :],
                                                 tb[d][:, 2, head * RN:(head + 1) * RN], start=False, stop=(h == 2 + pair))
                    last.then_inc(s["right"], 1)
                for g in range(G):
                    if g < 2:
                        pe.wait_ge(s["right_g"], 2 * i + g + 1)
                    else:
                        pe.wait_ge(s["right_r"], 4 * i + g - 1)
                    n = width[g]
                    for h in range(GR):
                        last = pe.matmul(ps[:, g, h * n:(h + 1) * n], XT[g][:, h, :], R[g][:, h, :], start=True, stop=True)
                    last.then_inc(s["solved"], 1)
                for g in range(G):
                    d, half = direction[g], g % 2
                    if g < 2:
                        pe.wait_ge(s["u_g"], 2 * i + g + 1)
                        for h in range(GR):
                            pe.matmul(ps[:, g, h * P:(h + 1) * P], fb[d][:, 1, h, :], S_g[d][:, h, :], start=True, stop=True)
                        for h in range(GR):
                            last = pe.matmul(ps[:, 6 + g, h * P:(h + 1) * P], A_o[g][:, h, :], U[g][:, h, :],
                                             start=True, stop=True)
                        last.then_inc(s["outs"], 1)
                        continue
                    pe.wait_ge(s["u_r"], 4 * i + g - 1)
                    for pair in range(2):
                        pe.matmul(pair_slots(g, pair), AR[d][:, 2 * half + pair, 1, :], S_r[d][:, 2 * half + pair, :, :],
                                  start=True, stop=False)
                        for h in (pair, 2 + pair):
                            head = head_of(half, h)
                            o = ps[:, g, h * RN:(h + 1) * RN]
                            pe.matmul(o, A_o[g][:, h, :], U[g][:, h, :], start=False, stop=False)
                            pe.matmul(o, A_ov[g][:, h, :], tb[d][:, 2, head * RN:(head + 1) * RN], start=False,
                                      stop=(h == 2 + pair))
                    for pair in range(2):
                        k = 2 * half + pair
                        o = ps[:, g, 256 + pair * P:256 + (pair + 1) * P].rearrange("p (a n) -> p a n", a=2)
                        pe.matmul(o, BK[d][:, 0, k * P:(k + 1) * P], U[g].rearrange("p (a b) n -> p b a n", a=2)[:, pair, :, :],
                                  start=True, stop=False)
                        last = pe.matmul(o, BK[d][:, 1, k * P:(k + 1) * P],
                                         tb[d][:, 2, k * P:(k + 1) * P].rearrange("p (a n) -> p a n", a=2),
                                         start=False, stop=True)
                    last.then_inc(s["outs"], 1)
                pe.wait_ge(s["kdec"], 2 * i + 2)
                for d in range(2):
                    pe.wait_ge(s["outs_used"], G * i + G + d + 1)
                    for h in range(GR):
                        last = pe.matmul(ps[:, 6 + d, h * P:(h + 1) * P], KD[d][:, h, :], U[d][:, h, :],
                                         start=True, stop=True)
                    last.then_inc(s["g_state"], 1)

        @block.scalar
        def _(act):
            act.wait_ge(s["zeroed"], 1)
            with act.Fori(0, TILES) as i:
                for d in range(2):
                    act.wait_ge(s["g_shift"], 2 * i + d + 1)
                    act.activation(decay[:, :, :], decay[:, :, :], ACT.Exp).then_inc(s["g_decay"], 1)
                for d in range(2):
                    act.wait_ge(s["w_sums"], 2 * i + d + 1)
                    if d == 1:
                        act.wait_ge(s["w_used"], 2 * i + 1)
                    act.activation(ends[d][:, :, :], ps[:, 7, 0:2 * RB].rearrange("p (b n) -> p b n", n=2),
                                   ACT.Exp).then_inc(s["act_chain"], 1)
                    v = pairs_view(5)
                    act.activation(e_exc[:, :, :], v[:, :, 1, :], ACT.Exp).then_inc(s["act_chain"], 1)
                    act.activation(e_inc[:, :, :], v[:, :, 0, :], ACT.Exp).then_inc(s["act_chain"], 1)
                    act.wait_ge(s["act_chain"], 6 * i + 3 * d + 3)
                    act.activation(e_neg[:, :, :], v[:, :, 0, :], ACT.Exp, scale=-1.0).then_inc(s["w_exp"], 1)
                for d in range(2):
                    for u in range(2):
                        act.wait_ge(s["turned"], 4 * i + 2 * d + u + 1)
                        act.activation(BK[d][:, u, :], ps[:, 5 + u, :], ACT.Copy).then_inc(s["turned_out"], 1)
                for g in range(G):
                    act.wait_ge(s["x_turned"], G * i + g + 1)
                    act.activation(X[g][:, :, :], heads(ps[:, g % 2, :]), ACT.Copy).then_inc(s["x_out"], 1)
                for u in range(UNITS):
                    m, g, d = unit(u)
                    act.wait_ge(s["y_product"], UNITS * i + u + 1 + FREE)
                    if u % G < 2:
                        stale = newly_zero(all_heads(Y[d]), m, d)
                        act.activation(stale, zeros[:, 0:stale.shape[1] * stale.shape[2]].rearrange("p (a n) -> p a n", n=stale.shape[2]),
                                       ACT.Copy).then_inc(s["y_cleared"], 1)
                    act.activation(half_of(all_heads(Y[d]), m, d), compact(2 + d, 0, m), ACT.Copy).then_inc(s["y_out"], 1)
                for g in range(2, G):
                    act.wait_ge(s["right"], G * i + g + 1)
                    act.activation(R[g], heads(ps[:, g, 0:4 * RN], RN), ACT.Copy).then_inc(s["right_r"], 1)
                for g in range(2, G):
                    act.wait_ge(s["solved"], G * i + g + 1)
                    act.activation(U[g], heads(ps[:, g, 0:4 * RN], RN), ACT.Copy).then_inc(s["u_r"], 1)

        @block.gpsimd
        def _(pool):
            for d in range(2):
                pool.memset(S_g[d][:, :, :], 0.0).then_inc(s["cleared"], 1)
                pool.memset(S_r[d][:, :, :, :], 0.0).then_inc(s["cleared"], 1)
            pool.memset(out[:, :, :], 0.0).then_inc(s["cleared"], 1)
            pool.memset(zeros[:, :], 0.0).then_inc(s["zeroed"], 1)
            pool.wait_ge(s["consts"], 16 * 16)
            with pool.Fori(0, TILES) as i:
                for d in range(2):
                    if d == 1:
                        pool.wait_ge(s["g_sums"], 2 * i + 1)
                    pool.sem_inc(s["pool_tick"], 1)
                    pool.tensor_tensor(grow[:, :, :], bcm(incl[d][:, :], GH), rate("g", d, tile(d, i)),
                                       ALU.mult).then_inc(s["g_rows"], 1)

                def x_first(g):
                    pool.tensor_tensor(XT[g][:, :, :], NT_[g][:, :, :], bcm(levels[direction[g]][:, 0, :], GR),
                                       ALU.mult).then_inc(s["pool_chain"], 1)
                    pool.wait_ge(s["pool_chain"], G * i + g + 1)
                    pool.tensor_tensor(XT[g][:, :, :], XT[g][:, :, :], bcm(ident[:, :], GR), ALU.add).then_inc(s["x_first"], 1)

                for g in range(2):
                    pool.wait_ge(s["gram_used"], 2 * i + g + 1)
                    x_first(g)
                pool.wait_ge(s["w_used"], 2 * i + 2)
                for d in range(2):
                    pool.wait_ge(late[d], 32 * i + 32)
                    pool.sem_inc(s["pool_tick"], 1)
                    pool.tensor_tensor(KD[d][:, :, :], heads(tb[d][:, 0, :]), rate("exp_rest", d, tile(d, i)),
                                       ALU.mult).then_inc(s["kdec"], 1)
                for g in range(2, G):
                    pool.wait_ge(s["b_pairs_used"], 4 * i + g - 1)
                    x_first(g)
                pool.wait_ge(s["k_pairs_used"], 4 * i + 4)
                for u in range(UNITS):
                    m, g, d = unit(u)
                    pool.wait_ge(s["y_product"], UNITS * i + u + 1)
                    pool.tensor_tensor(NM[d][:, :, :], NT_[g][:, :, :], bcm(levels[d][:, m, :], GR), ALU.mult).then_inc(s["masked"], 1)

        @block.vector
        def _(dve):
            dve.wait_ge(s["consts"], 16 * 16)
            dve.wait_ge(s["cleared"], 5)
            dve.sem_inc(s["turn_done"], 1)
            dve.sem_inc(s["outs_used"], G)
            dve.sem_inc(s["joined"], FREE)
            dve.sem_inc(s["y_product"], FREE)
            with dve.Fori(0, TILES) as i:
                link = Chain(dve, s["dve_chain"], i, PER_DVE)
                for d in range(2):
                    t = tile(d, i)
                    dve.wait_ge(s["g_sums"], 2 * i + d + 1)
                    link(dve.tensor_tensor(decay[:, :, :], heads(ps[:, 0, :]), rate("G", d, t), ALU.subtract))
                    dve.tensor_tensor(decay[:, :, :], decay[:, :, :], bcm(outside[d][:, :], GH),
                                      ALU.add).then_inc(s["g_shift"], 1)
                    dve.wait_ge(s["g_decay"], 2 * i + d + 1)
                    dve.wait_ge(s["gram"], 2 * i + d + 1)
                    v = pairs_view(1 + 2 * d)
                    for h in range(GH):
                        link(dve.scalar_tensor_tensor(NT_[d][:, h, :], v[:, h, 0, :],
                                                      rates["neg_beta"][d][:, bass.ds(t, 1), h], decay[:, h, :],
                                                      ALU.mult, ALU.mult))
                    dve.tensor_tensor(A_o[d][:, :, :], v[:, :, 1, :], decay[:, :, :], ALU.mult).then_inc(s["gram_used"], 1)
                    dve.wait_ge(s["gram_used"], 2 * i + d + 1)
                for d in range(2):
                    dve.wait_ge(s["w_exp"], 2 * i + d + 1)
                    dve.wait_ge(early[d], 48 * i + 48)
                    dve.wait_ge(late[d], 32 * i + 32)
                    link(dve.scalar_tensor_tensor(AR[d][:, :, 0, :], fb[d][:, 2, :, :], -1.0, e_exc[:, :, :],
                                                  ALU.mult, ALU.mult))
                    link(dve.tensor_tensor(AR[d][:, :, 1, :], rr[d][:, :, :], e_inc[:, :, :], ALU.mult))
                    link(dve.tensor_tensor(BT[d][:, :, :], fd[d][:, 0, :, :], e_neg[:, :, :], ALU.mult))
                    dve.tensor_tensor(KT[d][:, :, :], fd[d][:, 1, :, :], e_neg[:, :, :], ALU.mult).then_inc(s["w_used"], 1)
                for d in range(2):
                    flat = S_r[d][:, :, :, :].rearrange("p k a n -> p k (a n)")
                    link(dve.tensor_tensor(rest[d][:, :, :], bc(ends[d][:, :, 1], 2), bcm(head_cols[:, :], RB), ALU.mult))
                    scaled = dve.tensor_tensor(flat, flat, bc(ends[d][:, :, 0], P), ALU.mult)
                    if d == 0:
                        link(scaled)
                scaled.then_inc(s["state_scaled"], 1)
                dve.wait_ge(s["state_scaled"], i + 1)
                for g in range(2, G):
                    d = direction[g]
                    dve.wait_ge(s["b_pairs"], 4 * i + g - 1)
                    with_b, with_k = pairs_view(1), pairs_view(3)
                    link(dve.tensor_tensor(NT_[g][:, :, :], with_b[:, :, 0, :], bcm(excl[d][:, :], GR), ALU.mult))
                    dve.tensor_tensor(A_o[g][:, :, :], with_b[:, :, 1, :], bcm(incl[d][:, :], GR),
                                      ALU.mult).then_inc(s["b_pairs_used"], 1)
                    dve.wait_ge(s["k_pairs"], 4 * i + g - 1)
                    link(dve.tensor_tensor(A_v[g][:, :, :], with_k[:, :, 0, :], bcm(excl[d][:, :], GR), ALU.mult))
                    dve.tensor_tensor(A_ov[g][:, :, :], with_k[:, :, 1, :], bcm(incl[d][:, :], GR),
                                      ALU.mult).then_inc(s["k_pairs_used"], 1)
                for u in range(UNITS):
                    m, g, d = unit(u)
                    dve.wait_ge(s["z_product"], UNITS * i + u + 1)
                    dve.wait_ge(s["joined"], UNITS * i + u + 1)
                    if m < LEVELS - 1:
                        x = half_of(all_heads(X[g]), m, d)
                        dve.tensor_tensor(x, x, compact(4 + d, GR, m), ALU.add).then_inc(s["x_joined"], 1)
                    x = half_of(all_heads(XT[g]), m, 1 - d)
                    dve.tensor_tensor(x, x, compact(4 + d, 0, m), ALU.add).then_inc(s["joined"], 1)
                for d in range(2):
                    dve.wait_ge(s["right"], G * i + d + 1)
                    link(dve.tensor_tensor(R[d], heads(ps[:, d, :]), rate("exp_G", d, tile(d, i)), ALU.mult))
                    dve.tensor_tensor(R[d], heads(tb[d][:, 1, :]), R[d], ALU.subtract).then_inc(s["right_g"], 1)
                for d in range(2):
                    dve.wait_ge(s["solved"], G * i + d + 1)
                    dve.tensor_tensor(U[d], heads(ps[:, d, :]), rate("beta", d, tile(d, i)), ALU.mult).then_inc(s["u_g"], 1)
                for g in range(G):
                    d, half = direction[g], g % 2
                    t = tile(d, i)
                    dve.wait_ge(s["outs"], G * i + g + 1)
                    if g < 2:
                        o = out[:, bass.ds(t, 1), 0:GW].rearrange("p o (h n) -> p (o h) n", n=P)
                        link(dve.tensor_tensor(R[d], heads(ps[:, d, :]), rate("exp_G", d, t), ALU.mult))
                        link(dve.tensor_tensor(o, o, R[d], ALU.add))
                        dve.tensor_tensor(o, o, heads(ps[:, 6 + d, :]), ALU.add).then_inc(s["outs_used"], 1)
                        continue
                    o = out[:, bass.ds(t, 1), GW + half * 4 * RN:GW + (half + 1) * 4 * RN].rearrange(
                        "p o (b a n) -> p (o a) b n", a=2, n=RN)
                    state = S_r[d][:, 2 * half:2 * half + 2, :, :].rearrange("p k a n -> p (k a) n")
                    link(dve.tensor_tensor(state, state, heads(ps[:, g, 256:512], RN), ALU.add))
                    link(dve.tensor_tensor(state, state, bc(rest[d][:, 2 * half:2 * half + 2, :].rearrange("p k a -> p (k a)"), RN),
                                           ALU.mult))
                    dve.tensor_tensor(o, o, ps[:, g, 0:4 * RN].rearrange("p (a b n) -> p a b n", a=2, n=RN), ALU.add).then_inc(s["outs_used"], 1)
                dve.wait_ge(s["outs_used"], G * i + 2 * G)
                for d in range(2):
                    more = keep[d][:, bass.ds(i, 1)]
                    dve.wait_ge(s["g_state"], 2 * i + d + 1)
                    link(dve.tensor_scalar(S_r[d][:, :, :, :], S_r[d][:, :, :, :], more, None, ALU.mult))
                    link(dve.tensor_tensor(S_g[d][:, :, :], S_g[d][:, :, :], rate("exp_last", d, tile(d, i)), ALU.mult))
                    link(dve.tensor_tensor(S_g[d][:, :, :], S_g[d][:, :, :], heads(ps[:, 6 + d, :]), ALU.add))
                    link(dve.tensor_scalar(S_g[d][:, :, :], S_g[d][:, :, :], more, None, ALU.mult))
                dve.sem_inc(s["turn_done"], 1)
                link.done()


def gate_outputs(nc, E, ins, out, z_tm, tm_both):
    o_norm = E.sb("o_norm", [P, GD])
    ln_g, ln_b = E.sb("ln_g", [P, RW]), E.sb("ln_b", [P, RW])
    eps_g, eps_r = E.sb("eps_g", [P, 1]), E.sb("eps_r", [P, 1])
    z = [E.sb(f"z{j}", [P, GW]) for j in range(2)]
    gb = [E.sb(f"gb{j}", [P, 2, RW]) for j in range(2)]
    sq = [E.sb(f"sq{j}", [P, D]) for j in range(2)]
    stat = [E.sb(f"stat{j}", [P, GH + RH]) for j in range(2)]
    mean = [E.sb(f"mean{j}", [P, RH]) for j in range(2)]
    params, eps_set, centred, squared, summed, rooted, inverse, dve_chain, act_chain, pool_chain, tick, used_g, used_r = (
        E.sem(n) for n in ("params", "eps_set", "centred", "squared", "summed", "rooted", "inverse", "dve_chain",
                           "act_chain", "pool_chain", "tick", "used_g", "used_r"))
    FREE = 2
    loaded = [E.sem(f"loaded{j}") for j in range(2)]
    with nc.Block() as block:
        @block.sync
        def _(sp):
            sp.dma_start(o_norm[:, :], ins["gdn_o_norm"][0].partition_broadcast(P)).then_inc(params, 16)
            sp.dma_start(ln_g[:, :], ins["rwkv_ln_g"][0].partition_broadcast(P)).then_inc(params, 16)
            sp.dma_start(ln_b[:, :], ins["rwkv_ln_b"][0].partition_broadcast(P)).then_inc(params, 16)

            def load(t, j):
                sp.dma_start(z[j][:, :].unsqueeze(1), z_tm[bass.ds(t, 1)].rearrange("o p n -> p o n")).then_inc(loaded[j], 16)
                sp.dma_start(gb[j][:, :, :].rearrange("p a n -> p (a n)").unsqueeze(1),
                             tm_both[bass.ds(t, 1)].rearrange("o p n -> p o n")[:, :, 3 * GW:5 * GW]).then_inc(loaded[j], 16)

            for j in range(2):
                load(j, j)
            with sp.Fori(0, TILES // 2 - 1) as i:
                for j in range(2):
                    sp.wait_ge(used_r, 2 * i + j + 1)
                    sp.sem_inc(tick, 1)
                    sp.wait_ge(used_g, 2 * i + j + 1 + FREE)
                    sp.sem_inc(tick, 1)
                    load(2 * i + 2 + j, j)

        @block.scalar
        def _(act):
            act.wait_ge(eps_set, 2)
            with act.Fori(0, TILES // 2) as i:
                for j in range(2):
                    act.wait_ge(centred, 2 * i + j + 1)
                    act.activation(sq[j][:, :].unsqueeze(1), out[:, bass.ds(2 * i + j, 1), :], ACT.Square).then_inc(squared, 1)
                for j in range(2):
                    act.wait_ge(summed, 2 * i + j + 1)
                    act.activation(stat[j][:, 0:GH], stat[j][:, 0:GH], ACT.Sqrt, bias=eps_g[:, :],
                                   scale=1.0 / GD).then_inc(act_chain, 1)
                    act.wait_ge(act_chain, 2 * i + j + 1)
                    act.activation(stat[j][:, GH:], stat[j][:, GH:], ACT.Sqrt, bias=eps_r[:, :],
                                   scale=1.0 / RN).then_inc(rooted, 1)

        @block.vector
        def _(dve):
            dve.memset(eps_g[:, :], EPS).then_inc(eps_set, 1)
            dve.memset(eps_r[:, :], LN_EPS).then_inc(eps_set, 1)
            dve.wait_ge(params, 48)
            with dve.Fori(0, TILES // 2) as i:
                link = Chain(dve, dve_chain, i, 14)
                for j in range(2):
                    orr = out[:, bass.ds(2 * i + j, 1), GW:D].rearrange("p o (h n) -> p (o h) n", n=RN)
                    link(dve.tensor_reduce(mean[j][:, :], orr, AX.X, ALU.add))
                    link(dve.tensor_scalar(mean[j][:, :], mean[j][:, :], 1.0 / RN, None, ALU.mult))
                    dve.tensor_tensor(orr, orr, bc(mean[j][:, :], RN), ALU.subtract).then_inc(centred, 1)
                for j in range(2):
                    dve.wait_ge(squared, 2 * i + j + 1)
                    dve.wait_ge(used_g, 2 * i + j + 1)
                    link(dve.tensor_reduce(stat[j][:, 0:GH], sq[j][:, 0:GW].rearrange("p (h n) -> p h n", n=GD), AX.X, ALU.add))
                    dve.tensor_reduce(stat[j][:, GH:], sq[j][:, GW:].rearrange("p (h n) -> p h n", n=RN), AX.X,
                                      ALU.add).then_inc(summed, 1)
                for j in range(2):
                    orr = out[:, bass.ds(2 * i + j, 1), GW:D].rearrange("p o (h n) -> p (o h) n", n=RN)
                    of = out[:, bass.ds(2 * i + j, 1), GW:D]
                    dve.wait_ge(rooted, 2 * i + j + 1)
                    dve.reciprocal(stat[j][:, :], stat[j][:, :]).then_inc(inverse, 1)
                    dve.wait_ge(inverse, 2 * i + j + 1)
                    dve.wait_ge(loaded[j], 32 * i + 32)
                    link(dve.tensor_tensor(orr, orr, bc(stat[j][:, GH:], RN), ALU.mult))
                    link(dve.tensor_tensor(of, of, ln_g[:, :].unsqueeze(1), ALU.mult))
                    link(dve.tensor_tensor(of, of, ln_b[:, :].unsqueeze(1), ALU.add))
                    link(dve.tensor_tensor(of, of, gb[j][:, 1:2, :], ALU.add))
                    dve.tensor_tensor(of, of, gb[j][:, 0:1, :], ALU.mult).then_inc(used_r, 1)
                dve.wait_ge(used_r, 2 * i + 2)
                link.done()

        @block.gpsimd
        def _(pool):
            pool.sem_inc(used_g, FREE)
            pool.wait_ge(params, 48)
            with pool.Fori(0, TILES // 2) as i:
                link = Chain(pool, pool_chain, i, 4)
                for j in range(2):
                    og = out[:, bass.ds(2 * i + j, 1), 0:GW].rearrange("p o (h n) -> p (o h) n", n=GD)
                    pool.wait_ge(inverse, 2 * i + j + 1)
                    pool.wait_ge(loaded[j], 32 * i + 32)
                    pool.sem_inc(tick, 1)
                    link(pool.tensor_tensor(og, og, bc(stat[j][:, 0:GH], GD), ALU.mult))
                    pool.sem_inc(tick, 1)
                    link(pool.tensor_tensor(og, og, bcm(o_norm[:, :], GH), ALU.mult))
                    pool.sem_inc(tick, 1)
                    pool.tensor_tensor(og, og, z[j][:, :].rearrange("p (h n) -> p h n", n=GD), ALU.mult).then_inc(used_g, 1)
                pool.wait_ge(used_g, 2 * i + 2 + FREE)
                link.done()


def project_out(nc, E, ident, mix, w_out):
    CHUNKS = 4
    PER = KB // CHUNKS
    w_raw = E.sb("w_raw", [P, KB, D])
    w = E.pair("w", [P, KB, D])
    mT = [E.pair(f"mT{j}", [P, KB, P]) for j in range(2)]
    ps = [E.stack.enter_context(nc.psum_tensor(f"{E.tag}_ps{j}", [P, 2, 512], F32)) for j in range(4)]
    w_loaded = [E.sem(f"w_loaded{c}") for c in range(CHUNKS)]
    w_high, w_low, turned, high_done, low_done, multiplied, done = (
        E.sem(n) for n in ("w_high", "w_low", "turned", "high_done", "low_done", "multiplied", "done"))

    def halves(ap):
        return ap[:, :, :].rearrange("p (a b) n -> p a (b n)", a=2)

    with nc.Block() as block:
        @block.sync
        def _(sp):
            for c in range(CHUNKS):
                sp.dma_start(w_raw[:, c * PER:(c + 1) * PER, :],
                             w_out.rearrange("(k p) n -> p k n", p=P)[:, c * PER:(c + 1) * PER, :]).then_inc(w_loaded[c], 16)

        @block.tensor
        def _(pe):
            def turn(t):
                if t >= 2:
                    pe.wait_ge(low_done, t - 1)
                for k in range(KB):
                    last = pe.transpose(ps[t % 2][:, k // 4, (k % 4) * P:(k % 4 + 1) * P], mix[:, t, k * P:(k + 1) * P], ident[:, :])
                last.then_inc(turned, 1)

            turn(0)
            for t in range(TILES):
                if t + 1 < TILES:
                    turn(t + 1)
                pe.wait_ge(low_done, t + 1)
                if t >= 2:
                    pe.wait_ge(done, t - 1)
                for half in range(2):
                    for k in range(KB):
                        if t + half == 0:
                            pe.wait_ge(w_low, k + 1)
                        last = product(pe, ps[2 + t % 2][:, half, :], both(mT[t % 2], slice(None), k),
                                       both(w, slice(None), k, slice(half * 512, (half + 1) * 512)), k == 0, k == KB - 1)
                last.then_inc(multiplied, 1)

        @block.scalar
        def _(act):
            def high(t):
                act.wait_ge(turned, t + 1)
                if t >= 2:
                    act.wait_ge(multiplied, t - 1)
                act.activation(halves(mT[t % 2][0]), ps[t % 2][:, :, :], ACT.Copy).then_inc(high_done, 1)

            high(0)
            for k in range(KB):
                if k % PER == 0:
                    act.wait_ge(w_loaded[k // PER], 16)
                act.activation(w[0][:, k, :], w_raw[:, k, :], ACT.Copy).then_inc(w_high, 1)
            for t in range(TILES):
                if t + 1 < TILES:
                    high(t + 1)
                act.wait_ge(multiplied, t + 1)
                act.activation(mix[:, t, :].rearrange("p (a n) -> p a n", a=2), ps[2 + t % 2][:, :, :], ACT.Copy).then_inc(done, 1)
            act.wait_ge(done, TILES)

        @block.vector
        def _(dve):
            def low(t):
                dve.wait_ge(high_done, t + 1)
                dve.tensor_tensor(halves(mT[t % 2][1]), ps[t % 2][:, :, :], halves(mT[t % 2][0]).bitcast(F32),
                                  ALU.subtract).then_inc(low_done, 1)

            low(0)
            for k in range(KB):
                dve.wait_ge(w_high, k + 1)
                dve.tensor_tensor(w[1][:, k, :], w_raw[:, k, :], w[0][:, k, :].bitcast(F32), ALU.subtract).then_inc(w_low, 1)
            for t in range(1, TILES):
                low(t)


def latents(nc, E, ins, hT, spare, qlT, kvlT, krT):
    n_cols = Q_LORA + KV_LORA + ROPE
    half = ROPE // 2
    w_raw = spare[:, 0:KB // 2, :].rearrange("p t (a n) -> p (t a) n", a=2)
    w = E.pair("w", [P, KB, n_cols + ROPE])
    ones = E.sb("ones", [P, P])
    eps = E.sb("eps", [P, 1])
    cos, sin = E.sb("cos", [ROPE, NT]), E.sb("sin", [ROPE, NT])
    g = E.sb("g", [P, 3])
    raw = E.sb("raw", [P, 3, 512])
    sq = E.sb("sq", [P, 3, 512])
    root = E.sb("root", [P, 2, 512])
    part = [E.sb(f"part{u}", [ROPE, 512]) for u in range(2)]
    bank = E.banks(8)
    w_loaded, w_high, w_low = (E.sem(n) for n in ("w_loaded", "w_high", "w_low"))
    loaded, eps_set, multiplied, raw_out, squared, sums, rooted, normal, rope_done, dve_chain = (
        E.sem(n) for n in ("loaded", "eps_set", "multiplied", "raw_out", "squared", "sums", "rooted", "normal", "rope_done",
                           "dve_chain"))
    w_in = ins["w_in_odd"][0].rearrange("(k p) n -> p k n", p=P)
    rope0 = Q_LORA + KV_LORA
    with nc.Block() as block:
        @block.sync
        def _(sp):
            sp.dma_start(w_raw[:, :, 0:n_cols], w_in).then_inc(w_loaded, 16)
            sp.dma_start(w_raw[:, :, n_cols:n_cols + half], w_in[:, :, rope0 + half:rope0 + ROPE]).then_inc(w_loaded, 16)
            sp.dma_start(w_raw[:, :, n_cols + half:n_cols + ROPE], w_in[:, :, rope0:rope0 + half]).then_inc(w_loaded, 16)
            sp.dma_start(ones[:, :], ins["c_ones"]).then_inc(loaded, 16)
            sp.dma_start(cos[:, :], ins["c_cos"]).then_inc(loaded, 16)
            sp.dma_start(sin[:, :], ins["c_sin"]).then_inc(loaded, 16)
            sp.dma_start(g[:, 0:2], ins["mla_q_norm"][0].rearrange("(k p) -> p k", p=P),
                         allow_slow_non_contiguous=True).then_inc(loaded, 16)
            sp.dma_start(g[:, 2:3], ins["mla_kv_norm"].rearrange("n p -> p n"), allow_slow_non_contiguous=True).then_inc(loaded, 16)

        @block.tensor
        def _(pe):
            pe.wait_ge(loaded, 16 * 5)
            for q, (t0, n) in enumerate(PIECES):
                if q > 0:
                    pe.wait_ge(raw_out, 3 * q)
                    pe.wait_ge(rope_done, q)
                for b in range(5):
                    c0, m = (b * P, P) if b < 3 else (rope0 + (b - 3) * ROPE, ROPE)
                    for k in range(KB):
                        if q + b == 0:
                            pe.wait_ge(w_low, k + 1)
                        last = product(pe, bank[b][0:m, 0:n], both(w, slice(None), k, slice(c0, c0 + m)),
                                       both(hT, slice(None), k, slice(t0, t0 + n)), k == 0, k == KB - 1)
                    last.then_inc(multiplied, 1)
                pe.wait_ge(squared, 3 * q + 3)
                if q > 0:
                    pe.wait_ge(rooted, 2 * q)
                pe.matmul(bank[5][:, 0:n], ones[:, :], sq[:, 0, 0:n], start=True, stop=False)
                pe.matmul(bank[5][:, 0:n], ones[:, :], sq[:, 1, 0:n], start=False, stop=True)
                pe.matmul(bank[6][:, 0:n], ones[:, :], sq[:, 2, 0:n], start=True, stop=True).then_inc(sums, 1)

        @block.scalar
        def _(act):
            act.wait_ge(eps_set, 1)
            act.wait_ge(w_loaded, 48)
            for k in range(KB):
                act.activation(w[0][:, k, :], w_raw[:, k, :], ACT.Copy).then_inc(w_high, 1)
            for q, (t0, n) in enumerate(PIECES):
                if q > 0:
                    act.wait_ge(normal, 3 * q)
                for b in range(3):
                    act.wait_ge(multiplied, 5 * q + b + 1)
                    act.activation(raw[:, b, 0:n], bank[b][:, 0:n], ACT.Copy).then_inc(raw_out, 1)
                act.wait_ge(raw_out, 3 * q + 3)
                for b in range(3):
                    act.activation(sq[:, b, 0:n], raw[:, b, 0:n], ACT.Square).then_inc(squared, 1)
                act.wait_ge(sums, q + 1)
                for u, width in enumerate((Q_LORA, KV_LORA)):
                    act.activation(root[:, u, 0:n], bank[5 + u][:, 0:n], ACT.Sqrt, bias=eps[:, :],
                                   scale=1.0 / width).then_inc(rooted, 1)

        @block.vector
        def _(dve):
            dve.memset(eps[:, :], EPS).then_inc(eps_set, 1)
            link = Chain(dve, dve_chain)
            dve.wait_ge(loaded, 16 * 5)
            for k in range(KB):
                dve.wait_ge(w_high, k + 1)
                dve.tensor_tensor(w[1][:, k, :], w_raw[:, k, :], w[0][:, k, :].bitcast(F32), ALU.subtract).then_inc(w_low, 1)
            for q, (t0, n) in enumerate(PIECES):
                for u, table in enumerate((cos, sin)):
                    dve.wait_ge(multiplied, 5 * q + 4 + u)
                    link(dve.tensor_tensor(part[u][:, 0:n], bank[3 + u][0:ROPE, 0:n], table[:, t0:t0 + n], ALU.mult))
                dve.tensor_tensor(krT[:, t0:t0 + n], part[0][:, 0:n], part[1][:, 0:n], ALU.add).then_inc(rope_done, 1)
                dve.wait_ge(rope_done, q + 1)
                dve.wait_ge(rooted, 2 * q + 2)
                link(dve.reciprocal(root[:, :, 0:n], root[:, :, 0:n]))
                for b in range(3):
                    dst = qlT[:, b, t0:t0 + n] if b < 2 else kvlT[:, t0:t0 + n]
                    dve.scalar_tensor_tensor(dst, raw[:, b, 0:n], g[:, b:b + 1], root[:, b // 2, 0:n],
                                             ALU.mult, ALU.mult).then_inc(normal, 1)
            dve.wait_ge(normal, 3 * len(PIECES))


def values(nc, E, ins, kvlT, V):
    w = E.sb("w", [P, MH * MV])
    bank = E.banks(8)
    loaded, product, act_out, dve_out = (E.sem(n) for n in ("loaded", "product", "act_out", "dve_out"))
    wv = ins["mla_w_kv_b"][0].rearrange("p (h n) -> p h n", n=NOPE + MV)
    with nc.Block() as block:
        @block.sync
        def _(sp):
            sp.dma_start(w[:, :].rearrange("p (h n) -> p h n", n=MV), wv[:, :, NOPE:NOPE + MV]).then_inc(loaded, 16)

        @block.tensor
        def _(pe):
            pe.wait_ge(loaded, 16)
            for t in range(TILES):
                if t >= 4:
                    pe.wait_ge(act_out, t - 3)
                    pe.wait_ge(dve_out, t - 3)
                for half in range(2):
                    pe.matmul(bank[2 * (t % 4) + half][:, :], kvlT[:, t * P:(t + 1) * P], w[:, half * 512:(half + 1) * 512],
                              start=True, stop=True).then_inc(product, 1)

        @block.scalar
        def _(act):
            for t in range(TILES):
                act.wait_ge(product, 2 * t + 1)
                act.activation(V[:, t, 0:512], bank[2 * (t % 4)][:, :], ACT.Copy).then_inc(act_out, 1)
            act.wait_ge(act_out, TILES)

        @block.vector
        def _(dve):
            for t in range(TILES):
                dve.wait_ge(product, 2 * t + 2)
                dve.tensor_copy(V[:, t, 512:1024], bank[2 * (t % 4) + 1][:, :]).then_inc(dve_out, 1)
            dve.wait_ge(dve_out, TILES)


def attend(nc, E, ins, ident, qlT, kvlT, krT, V, out):
    half = ROPE // 2
    SCALE = float(NOPE + ROPE) ** -0.5
    wq = E.sb("wq", [P, 2, NOPE])
    wr = E.sb("wr", [P, 2, 2, ROPE])
    wk = E.sb("wk", [P, NOPE])
    qn, kn, qr, kr = (E.pair(n, [P, NT]) for n in ("qn", "kn", "qr", "kr"))
    kr_twice, tables = E.sb("kr_twice", [P, NT]), E.sb("tables", [P, NT])
    terms = [E.sb(f"terms{u}", [P, 512]) for u in range(2)]
    w_sm = [E.sb(f"w_sm{j}", [P, T_PROMPT]) for j in range(2)]
    wT = [E.sb(f"wT{j}", [P, T_PROMPT // P, P]) for j in range(2)]
    mx, neg = (E.sb(n, [P, 2]) for n in ("mx", "neg"))
    total, inv = (E.sb(n, [P, TILES]) for n in ("total", "inv"))
    ps = E.stack.enter_context(nc.psum_tensor(f"{E.tag}_ps", [P, 8, 512], F32))
    SCORES, TURN, OUT = (0, 2), 4, 6
    names = ("w_loaded", "q_product", "r_product", "k_product", "q_out", "k_out", "r_out", "scores", "shifted", "exped",
             "turned", "turned_a", "turned_b", "weighted", "written", "dve_chain",
             "q_low", "k_low", "kr_loaded", "kr_high", "kr_low")
    s = {n: E.sem(n) for n in names}
    w_q = ins["mla_w_q_b"][0].rearrange("(k p) n -> p k n", p=P)
    w_kv = ins["mla_w_kv_b"][0]
    NQ = len(PIECES)

    def keys(t):
        return (0, T_PROMPT) if t < TILES_P else (T_PROMPT, T_SAMPLE)

    with nc.Block() as block:
        @block.sync
        def _(sp):
            def load(h):
                c = h * (NOPE + ROPE)
                sp.dma_start(wq[:, :, :], w_q[:, :, bass.ds(c, NOPE)]).then_inc(s["w_loaded"], 16)
                sp.dma_start(wr[:, :, 0, :], w_q[:, :, bass.ds(c + NOPE, ROPE)]).then_inc(s["w_loaded"], 16)
                sp.dma_start(wr[:, :, 1, 0:half], w_q[:, :, bass.ds(c + NOPE + half, half)]).then_inc(s["w_loaded"], 16)
                sp.dma_start(wr[:, :, 1, half:ROPE], w_q[:, :, bass.ds(c + NOPE, half)]).then_inc(s["w_loaded"], 16)
                sp.dma_start(wk[:, :], w_kv[:, bass.ds(h * (NOPE + MV), NOPE)]).then_inc(s["w_loaded"], 16)

            load(0)
            for u, table in enumerate((ins["c_cos"], ins["c_sin"])):
                sp.dma_start(kr_twice[u * ROPE:(u + 1) * ROPE, :], krT[:, :]).then_inc(s["kr_loaded"], 16)
                sp.dma_start(tables[u * ROPE:(u + 1) * ROPE, :], table).then_inc(s["kr_loaded"], 16)
            with sp.Fori(0, MH - 1) as h:
                sp.wait_ge(s["k_product"], NQ * h + NQ)
                load(h + 1)

        @block.tensor
        def _(pe):
            pe.wait_ge(s["kr_low"], 1)
            with pe.Fori(0, MH) as h:
                pe.wait_ge(s["w_loaded"], 80 * h + 80)
                pe.wait_ge(s["exped"], TILES * h + 2)
                for q, (t0, n) in enumerate(PIECES):
                    if q == 2:
                        for name in ("q_low", "k_low", "r_out"):
                            pe.wait_ge(s[name], NQ * h + 1)
                    for k in range(2):
                        last = pe.matmul(ps[:, q % 2, 0:n], wq[:, k, :], qlT[:, k, t0:t0 + n], start=(k == 0), stop=(k == 1))
                    last.then_inc(s["q_product"], 1)
                    for k in range(2):
                        last = pe.matmul(ps[:, 2 + q % 2, 0:n], wr[:, k, :, :].rearrange("p u n -> p (u n)"),
                                         qlT[:, k, t0:t0 + n], start=(k == 0), stop=(k == 1))
                    last.then_inc(s["r_product"], 1)
                    pe.matmul(ps[:, 4 + q % 2, 0:n], wk[:, :], kvlT[:, t0:t0 + n], start=True, stop=True).then_inc(s["k_product"], 1)
                for name in ("q_low", "k_low", "r_out"):
                    pe.wait_ge(s[name], NQ * h + NQ)

                def scores(t):
                    k0, nk = keys(t)
                    pe.wait_ge(s["exped"], TILES * h + t + 1)
                    for c in range(0, nk, 512):
                        n = min(512, nk - c)
                        o = ps[:, SCORES[t % 2] + c // 512, 0:n]
                        queries, source = slice(t * P, (t + 1) * P), slice(k0 + c, k0 + c + n)
                        product(pe, o, both(qn, slice(None), queries), both(kn, slice(None), source), True, False)
                        last = product(pe, o, both(qr, slice(None), queries), both(kr, slice(None), source), False, True)
                    last.then_inc(s["scores"], 1)

                def turn(t):
                    nk = keys(t)[1]
                    pe.wait_ge(s["exped"], TILES * h + t + 1 + 2)
                    pe.wait_ge(s["turned_a"], TILES * h + t + 1)
                    pe.wait_ge(s["turned_b"], TILES * h + t + 1)
                    for b in range(nk // P):
                        last = pe.transpose(ps[:, TURN + b // 4, (b % 4) * P:(b % 4 + 1) * P],
                                            w_sm[t % 2][:, b * P:(b + 1) * P], ident[:, :])
                    last.then_inc(s["turned"], 1)

                def weigh(t):
                    k0, nk = keys(t)
                    pe.wait_ge(s["turned_a"], TILES * h + t + 2)
                    pe.wait_ge(s["turned_b"], TILES * h + t + 2)
                    pe.wait_ge(s["written"], TILES * h + t + 1)
                    for b in range(nk // P):
                        last = pe.matmul(ps[:, OUT + t % 2, 0:MV], wT[t % 2][:, b, :],
                                         V[:, k0 // P + b, bass.ds(h * MV, MV)], start=(b == 0), stop=(b == nk // P - 1))
                    last.then_inc(s["weighted"], 1)

                for t in range(TILES + 2):
                    if t < TILES:
                        scores(t)
                    if 1 <= t <= TILES:
                        turn(t - 1)
                    if t >= 2:
                        weigh(t - 2)

        @block.scalar
        def _(act):
            act.sem_inc(s["exped"], 2)
            act.sem_inc(s["turned_a"], 1)
            with act.Fori(0, MH) as h:
                for q, (t0, n) in enumerate(PIECES):
                    act.wait_ge(s["q_product"], NQ * h + q + 1)
                    if q == 0:
                        act.wait_ge(s["scores"], TILES * h + 1)
                    act.activation(qn[0][:, t0:t0 + n], ps[:, q % 2, 0:n], ACT.Copy).then_inc(s["q_out"], 1)
                    act.wait_ge(s["k_product"], NQ * h + q + 1)
                    act.activation(kn[0][:, t0:t0 + n], ps[:, 4 + q % 2, 0:n], ACT.Copy).then_inc(s["k_out"], 1)

                def exps(t):
                    nk = keys(t)[1]
                    act.wait_ge(s["shifted"], TILES * h + t + 1)
                    act.activation(w_sm[t % 2][:, 0:nk], ps[:, SCORES[t % 2]:SCORES[t % 2] + 2, :].rearrange("p a n -> p (a n)")[:, 0:nk],
                                   ACT.Exp, bias=neg[:, t % 2:t % 2 + 1], scale=SCALE,
                                   accum_out=total[:, t:t + 1]).then_inc(s["exped"], 1)

                def copy(t):
                    nb = keys(t)[1] // P // 2
                    act.wait_ge(s["turned"], TILES * h + t + 1)
                    act.activation(wT[t % 2][:, 0:nb, :].rearrange("p b n -> p (b n)"), ps[:, TURN, 0:nb * P],
                                   ACT.Copy).then_inc(s["turned_a"], 1)

                for t in range(TILES + 1):
                    if t < TILES:
                        exps(t)
                    if t >= 1:
                        copy(t - 1)

        @block.vector
        def _(dve):
            dve.sem_inc(s["turned_b"], 1)
            dve.sem_inc(s["scores"], 1)
            dve.sem_inc(s["written"], 2)
            dve.wait_ge(s["kr_loaded"], 64)
            dve.tensor_copy(kr[0][:, :], kr_twice[:, :]).then_inc(s["kr_high"], 1)
            dve.wait_ge(s["kr_high"], 1)
            dve.tensor_tensor(kr[1][:, :], kr_twice[:, :], kr[0][:, :].bitcast(F32), ALU.subtract).then_inc(s["kr_low"], 1)
            with dve.Fori(0, MH) as h:
                link = Chain(dve, s["dve_chain"], h, 2 * NQ + 2 * TILES)
                for q, (t0, n) in enumerate(PIECES):
                    dve.wait_ge(s["r_product"], NQ * h + q + 1)
                    link(dve.tensor_tensor(terms[q % 2][:, 0:n], ps[:, 2 + q % 2, 0:n], tables[:, t0:t0 + n], ALU.mult))
                    link(dve.tensor_copy(qr[0][:, t0:t0 + n], terms[q % 2][:, 0:n]))
                    dve.tensor_tensor(qr[1][:, t0:t0 + n], terms[q % 2][:, 0:n], qr[0][:, t0:t0 + n].bitcast(F32),
                                      ALU.subtract).then_inc(s["r_out"], 1)
                    dve.wait_ge(s["q_out"], NQ * h + q + 1)
                    dve.tensor_tensor(qn[1][:, t0:t0 + n], ps[:, q % 2, 0:n], qn[0][:, t0:t0 + n].bitcast(F32),
                                      ALU.subtract).then_inc(s["q_low"], 1)
                    dve.wait_ge(s["k_out"], NQ * h + q + 1)
                    dve.tensor_tensor(kn[1][:, t0:t0 + n], ps[:, 4 + q % 2, 0:n], kn[0][:, t0:t0 + n].bitcast(F32),
                                      ALU.subtract).then_inc(s["k_low"], 1)
                    dve.wait_ge(s["r_out"], NQ * h + q + 1)

                def shift(t):
                    nk = keys(t)[1]
                    dve.wait_ge(s["scores"], TILES * h + t + 2)
                    j = slice(t % 2, t % 2 + 1)
                    link(dve.reduce_max(mx[:, j], ps[:, SCORES[t % 2]:SCORES[t % 2] + 2, :].rearrange("p a n -> p (a n)")[:, 0:nk], AX.X))
                    dve.tensor_scalar(neg[:, j], mx[:, j], -SCALE, None, ALU.mult).then_inc(s["shifted"], 1)

                def copy(t):
                    nb = keys(t)[1] // P // 2
                    dve.wait_ge(s["turned"], TILES * h + t + 1)
                    bank, c0 = (TURN + 1, 0) if nb == 4 else (TURN, nb * P)
                    if nb < 4:
                        dve.wait_ge(s["turned_a"], TILES * h + t + 2)
                    dve.tensor_copy(wT[t % 2][:, nb:2 * nb, :].rearrange("p b n -> p (b n)"), ps[:, bank, c0:c0 + nb * P]
                                    ).then_inc(s["turned_b"], 1)

                def write(t):
                    j = slice(t, t + 1)
                    link(dve.reciprocal(inv[:, j], total[:, j]))
                    dve.wait_ge(s["weighted"], TILES * h + t + 1)
                    dve.tensor_scalar(out[:, t, bass.ds(h * MV, MV)], ps[:, OUT + t % 2, 0:MV], inv[:, j], None,
                                      ALU.mult).then_inc(s["written"], 1)

                for t in range(TILES + 2):
                    if t < TILES:
                        shift(t)
                    if 1 <= t <= TILES:
                        copy(t - 1)
                    if t >= 2:
                        write(t - 2)
                link.done()


def latent_tensors(nc, stack):
    return [stack.enter_context(nc.sbuf_tensor(name, shape, F32))
            for name, shape in (("qlT", [P, 2, NT]), ("kvlT", [P, NT]), ("krT", [ROPE, NT]))]


def clear_semaphores(nc, sems):
    with nc.Block() as block:
        @block.sync
        def _(sp):
            for sem in sems:
                sp.sem_clear(sem)


def program(nc, ins, outs, stop=99):
    scratch = {}

    def dram(name, shape):
        scratch[name] = nc.dram_tensor(f"s_{name}", shape, F32, kind="Internal").ap()
        return scratch[name]

    with ExitStack() as whole:
        def scope(tag):
            stack = ExitStack()
            E = Env(nc, stack, tag)
            E.sems = whole
            return stack, E

        _, top = scope("top")
        top.stack = whole
        acc = top.sb("acc", [P, TILES, D])
        gates = top.sb("gates", [P, TILES, 4 * GH])
        ident = top.sb("ident", [P, P])
        ident_loaded = top.sem("ident_loaded")
        with nc.Block() as block:
            @block.sync
            def _(sp):
                sp.dma_start(ident[:, :], ins["c_ident"]).then_inc(ident_loaded, 16)
                sp.wait_ge(ident_loaded, 16)

        conv_fm = dram("conv", [CONV_BLOCKS, P, NT])
        shift_fm = dram("shift", [RWKV_BLOCKS, P, NT])
        z_tm = dram("z", [TILES, P, GW])

        def phase(tag, f, *args, **kw):
            stack, E = scope(tag)
            with stack:
                E.sems = stack
                f(nc, E, *args, **kw)
                clear_semaphores(nc, E.made)

        x_in = token_tiles(ins["x_prompt"], ins["x_sample"])
        x_tm = dram("x", [TILES, P, D]).rearrange("t p d -> p t d")
        x_mid = (x_tm[:, 0:TILES_P, :], x_tm[:, TILES_P:TILES, :])
        x_out = token_tiles(*outs)

        def pair(stack, name):
            return [stack.enter_context(nc.sbuf_tensor(f"{name}_{part}", [P, KB, NT], F32R)) for part in ("high", "low")]

        with ExitStack() as wide:
            hT = pair(wide, "hT_first")
            phase("norm0", residual_norm, x_in, None, hT, ident, acc, None, ins["norm_mix_pre"][0])
            w_in = ins["w_in_even"][0]
            phase("conv", in_proj_fm, hT, w_in, 0, CONV_BLOCKS // 3, conv_fm, ins["gdn_conv"][0], True)
            phase("shift", in_proj_fm, hT, w_in, GDN_COLS, RWKV_BLOCKS // 3, shift_fm, ins["rwkv_mu"][0], False)
            phase("gates", in_proj_tm, hT, w_in, gates, z_tm)
        if stop > 1:
            mix_scopes(nc, phase, dram, ins, acc, gates, ident, conv_fm, shift_fm, z_tm, stop)
        if stop <= 4:
            return scratch
        with ExitStack() as wide:
            hT = pair(wide, "hT_ffn0")
            phase("norm1", residual_norm, x_in, x_mid, hT, ident, acc, ins["norm_mix_post"][0], ins["norm_ffn_pre"][0])
            phase("ffn0", feed_forward, hT, acc, ins["w_ff1"][0], ins["w_ff2"][0])
        if stop == 5:
            return scratch
        with ExitStack() as own:
            latent = latent_tensors(nc, own)
            with ExitStack() as wide:
                hT = pair(wide, "hT_attention")
                phase("norm2", residual_norm, x_mid, x_mid, hT, ident, acc, ins["norm_ffn_post"][0], ins["norm_mix_pre"][1])
                phase("latent", latents, ins, hT, acc, *latent)
            V = own.enter_context(nc.sbuf_tensor("V", [P, TILES, MH * MV], F32))
            phase("values", values, ins, latent[1], V)
            phase("attend", attend, ins, ident, *latent, V, acc)
        phase("out1", project_out, ident, acc, ins["w_out_odd"][0])
        if stop <= 6:
            return scratch
        with ExitStack() as wide:
            hT = pair(wide, "hT_ffn1")
            phase("norm3", residual_norm, x_mid, x_mid, hT, ident, acc, ins["norm_mix_post"][1], ins["norm_ffn_pre"][1])
            phase("ffn1", feed_forward, hT, acc, ins["w_ff1"][1], ins["w_ff2"][1])
        phase("norm4", residual_norm, x_mid, x_out, None, ident, acc, ins["norm_ffn_post"][1], None)
    return scratch


def constants():
    s = np.arange(P)[:, None]
    t = np.arange(P)[None, :]
    mid = P // 2
    c = {"c_ident": np.eye(P), "c_ones": np.ones((P, P))}
    block = np.arange(3 * GH)[None, :, None]
    of = np.where(block < 2 * GH, block, 2 * GH + 2 * (block - 2 * GH) + s[:, :, None] // RN)
    c["c_norm_cols"] = (of == np.arange(NORMS)[None, None, :]) * 1.0
    c["c_norm_rows"] = c["c_norm_cols"].transpose(2, 1, 0)
    c["c_head_cols"] = (s // RN == np.arange(2)[None, :]) * 1.0
    incl = np.stack([s <= t, s >= t]) * 1.0
    excl = np.stack([s < t, s > t]) * 1.0
    c["c_incl"], c["c_excl"] = incl, excl
    c["c_outside"] = (incl - 1.0) * 1e9
    rate = -math.exp(-0.5)
    upto_mid = incl[:, :, mid:mid + 1]
    c["c_decay_sums"] = rate * (np.concatenate([incl, excl], 2) - upto_mid)
    c["c_decay_ends"] = rate * np.concatenate([upto_mid, 1.0 - upto_mid], 2)
    levels = []
    for m in range(LEVELS):
        n = 1 << m
        lower = ((s // n) % 2 == 0) & (t // n == s // n + 1)
        levels.append(lower)
    c["c_levels"] = np.stack([np.stack(levels), np.stack(levels).transpose(0, 2, 1)]) * 1.0
    keep = np.ones((2, P, TILES))
    keep[0, :, TILES_P - 1] = 0.0
    keep[1, :, TILES - TILES_P - 1] = 0.0
    c["c_keep"] = keep
    inv = 1.0 / (np.float32(10000.0) ** (np.arange(0, ROPE, 2, dtype=np.float32) / np.float32(ROPE)))
    at = np.concatenate([np.arange(T_PROMPT), np.arange(T_SAMPLE)]).astype(np.float32)
    ang = (inv.astype(np.float32)[:, None] * at[None, :]).astype(np.float32)
    c["c_cos"] = np.concatenate([np.cos(ang), np.cos(ang)], 0)
    c["c_sin"] = np.concatenate([-np.sin(ang), np.sin(ang)], 0)
    return {k: np.ascontiguousarray(v, dtype=np.float32) for k, v in c.items()}


_OUTS = ((1, T_PROMPT, D), (1, T_SAMPLE, D))


def kernel(**inputs):
    import concourse.bacc as bacc
    from concourse.bass_utils import run_bass_kernel_spmd

    nc = bacc.Bacc("TRN2", target_bir_lowering=False, num_devices=1)
    arrays, ins = {}, {}
    for name, a in {**inputs, **constants()}.items():
        a = np.ascontiguousarray(a)
        arrays[f"in_{name}"] = a
        ins[name] = nc.dram_tensor(f"in_{name}", a.shape, F32, kind="ExternalInput").ap()
    outs = tuple(nc.dram_tensor(f"out_{i}", shape, F32, kind="ExternalOutput").ap() for i, shape in enumerate(_OUTS))
    program(nc, ins, outs)
    r = run_bass_kernel_spmd(nc, [arrays], core_ids=[0])
    return tuple(r.results[0][f"out_{i}"] for i in range(len(_OUTS)))
```
